# Optimizing a Trainium2 kernel written in Bass

```python
import jax, jax.numpy as jnp
from jax import lax
import numpy as np

D_MODEL = 1024
BATCH = 1
SEQ = 1024
DEPTH = 1
DEC_BATCH = 8
DEC_SEQ = 1
PAST_LEN = 8192
PAGE_SIZE = 128

POOL_WIDTH = D_MODEL // 4
POOL_WINDOWS = (2, 4, 8, 16)
N_POOL_GROUPS = len(POOL_WINDOWS)
POOL_GROUP = POOL_WIDTH // N_POOL_GROUPS
POOL_BUF = max(POOL_WINDOWS) - 1
SCONV_WIDTH = (D_MODEL - POOL_WIDTH) // 2
CONF_WIDTH = D_MODEL - POOL_WIDTH - SCONV_WIDTH
HEAD_DIM = 64
SCONV_K = 3
CONF_K = 31
D_FF = 4 * D_MODEL
IN_SPLITS = tuple(np.cumsum([POOL_WIDTH, SCONV_WIDTH, SCONV_WIDTH, SCONV_WIDTH, CONF_WIDTH]).tolist())
IN_COLS = POOL_WIDTH + 3 * SCONV_WIDTH + 2 * CONF_WIDTH
N_MOD = 6
EPS = 1e-6

kernel_name = "hybrid_pool_shortconv_conformer_decoder_step"

def rmsnorm(x, g):
    xf = x.astype(jnp.float32)
    y = xf * lax.rsqrt(jnp.mean(xf * xf, axis=-1, keepdims=True) + EPS)
    return (y * g.astype(jnp.float32)).astype(x.dtype)

def layernorm(x, g, b):
    xf = x.astype(jnp.float32)
    mu = jnp.mean(xf, axis=-1, keepdims=True)
    var = jnp.mean(jnp.square(xf - mu), axis=-1, keepdims=True)
    y = (xf - mu) * lax.rsqrt(var + EPS)
    return (y * g.astype(jnp.float32) + b.astype(jnp.float32)).astype(x.dtype)

def causal_dwconv(x_ext, w):
    return lax.conv_general_dilated(
        x_ext, w[:, None, :].astype(x_ext.dtype), window_strides=(1,), padding='VALID',
        dimension_numbers=('NWC', 'WIO', 'NWC'), feature_group_count=x_ext.shape[-1])

def pool_mix(u_ext, pos, w_grp, scale):
    b, _, _ = u_ext.shape
    t = pos.shape[0]
    uf = u_ext.astype(jnp.float32)
    cs = jnp.cumsum(jnp.pad(uf, ((0, 0), (1, 0), (0, 0))), axis=1)
    u_new = uf[:, POOL_BUF:]
    outs = []
    for g, w in enumerate(POOL_WINDOWS):
        sl = slice(g * POOL_GROUP, (g + 1) * POOL_GROUP)
        hi = cs[:, POOL_BUF + 1:POOL_BUF + 1 + t, sl]
        lo = cs[:, POOL_BUF + 1 - w:POOL_BUF + 1 - w + t, sl]
        cnt = jnp.minimum(pos + 1, w).astype(jnp.float32)[None, :, None]
        outs.append((hi - lo) / cnt - u_new[..., sl])
    d = jnp.stack(outs, axis=2)
    y = jnp.einsum('btgc,gcd->btgd', d, w_grp.astype(jnp.float32)).reshape(b, t, POOL_WIDTH)
    return (y * scale.astype(jnp.float32)).astype(u_ext.dtype)

def mixer(h, buf_pool, buf_sconv, buf_conf, pos, w_in, pool_w, pool_scale, sconv_w,
          conf_w, conf_b, conf_ln_g, conf_ln_b, w_out):
    z = h @ w_in
    u, gb, gc, v, ga, gg = jnp.split(z, IN_SPLITS, axis=-1)
    u_ext = jnp.concatenate([buf_pool.astype(u.dtype), u], axis=1)
    ya = pool_mix(u_ext, pos, pool_w, pool_scale)
    cv_ext = jnp.concatenate([buf_sconv.astype(v.dtype), gc * v], axis=1)
    yb = gb * causal_dwconv(cv_ext, sconv_w)
    gl_ext = jnp.concatenate([buf_conf.astype(ga.dtype), ga * jax.nn.sigmoid(gg)], axis=1)
    dc = causal_dwconv(gl_ext, conf_w) + conf_b
    yc = jax.nn.silu(layernorm(dc, conf_ln_g, conf_ln_b))
    y = jnp.concatenate([ya, yb, yc], axis=-1) @ w_out
    return (y, u_ext[:, -POOL_BUF:], cv_ext[:, -(SCONV_K - 1):], gl_ext[:, -(CONF_K - 1):])

def trunk(x, c, st_pool, st_sconv, st_conf, pos, w_ada, b_ada, norm1_g, norm2_g, w_in, pool_w,
          pool_scale, sconv_w, conf_w, conf_b, conf_ln_g, conf_ln_b, w_out, w_ff1, w_ff2, final_g):
    new_pool, new_sconv, new_conf = [], [], []
    c_act = jax.nn.silu(c)
    for l in range(DEPTH):
        mod = (c_act @ w_ada[l] + b_ada[l])[:, None, :]
        sh1, sc1, g1, sh2, sc2, g2 = jnp.split(mod, N_MOD, axis=-1)
        h = rmsnorm(x, norm1_g[l]) * (1 + sc1) + sh1
        y, bp, bs, bc = mixer(h, st_pool[l], st_sconv[l], st_conf[l], pos, w_in[l], pool_w[l],
                              pool_scale[l], sconv_w[l], conf_w[l], conf_b[l], conf_ln_g[l],
                              conf_ln_b[l], w_out[l])
        x = x + g1 * y
        h = rmsnorm(x, norm2_g[l]) * (1 + sc2) + sh2
        x = x + g2 * (jnp.square(jax.nn.relu(h @ w_ff1[l])) @ w_ff2[l])
        new_pool.append(bp); new_sconv.append(bs); new_conf.append(bc)
    return (rmsnorm(x, final_g), jnp.stack(new_pool), jnp.stack(new_sconv), jnp.stack(new_conf))

def setup_inputs(seed: int = 0) -> dict:
    key = jax.random.key(seed)
    ks = jax.random.split(key, 24)
    f32 = jnp.float32
    nrm = lambda k, s, sc: (jax.random.normal(k, s, f32) * sc)
    D = D_MODEL
    return {
        "x_prompt": nrm(ks[0], (BATCH, SEQ, D), 1.0),
        "x_sample": nrm(ks[1], (DEC_BATCH, DEC_SEQ, D), 1.0),
        "c_prompt": nrm(ks[2], (BATCH, D), 1.0),
        "c_sample": nrm(ks[3], (DEC_BATCH, D), 1.0),
        "state_pool": nrm(ks[4], (DEPTH, DEC_BATCH, POOL_BUF, POOL_WIDTH), 1.0),
        "state_sconv": nrm(ks[5], (DEPTH, DEC_BATCH, SCONV_K - 1, SCONV_WIDTH), 1.0),
        "state_conf": nrm(ks[6], (DEPTH, DEC_BATCH, CONF_K - 1, CONF_WIDTH), 0.5),
        "w_ada": nrm(ks[7], (DEPTH, D, N_MOD * D), 0.5 * D ** -0.5),
        "b_ada": nrm(ks[8], (DEPTH, N_MOD * D), 0.01),
        "norm1_g": 1.0 + nrm(ks[9], (DEPTH, D), 0.02),
        "norm2_g": 1.0 + nrm(ks[10], (DEPTH, D), 0.02),
        "w_in": nrm(ks[11], (DEPTH, D, IN_COLS), D ** -0.5),
        "pool_w": nrm(ks[12], (DEPTH, N_POOL_GROUPS, POOL_GROUP, POOL_GROUP), POOL_GROUP ** -0.5),
        "pool_scale": 1.0 + nrm(ks[13], (DEPTH, POOL_WIDTH), 0.1),
        "sconv_w": nrm(ks[14], (DEPTH, SCONV_K, SCONV_WIDTH), SCONV_K ** -0.5),
        "conf_w": nrm(ks[15], (DEPTH, CONF_K, CONF_WIDTH), CONF_K ** -0.5),
        "conf_b": nrm(ks[16], (DEPTH, CONF_WIDTH), 0.01),
        "conf_ln_g": 1.0 + nrm(ks[17], (DEPTH, CONF_WIDTH), 0.02),
        "conf_ln_b": nrm(ks[18], (DEPTH, CONF_WIDTH), 0.01),
        "w_out": nrm(ks[19], (DEPTH, D, D), D ** -0.5),
        "w_ff1": nrm(ks[20], (DEPTH, D, D_FF), D ** -0.5),
        "w_ff2": nrm(ks[21], (DEPTH, D_FF, D), D_FF ** -0.5),
        "final_g": 1.0 + nrm(ks[22], (D,), 0.02),
    }

def reference(x_prompt, x_sample, c_prompt, c_sample, state_pool, state_sconv, state_conf,
              w_ada, b_ada, norm1_g, norm2_g, w_in, pool_w, pool_scale, sconv_w, conf_w, conf_b,
              conf_ln_g, conf_ln_b, w_out, w_ff1, w_ff2, final_g):
    dt = x_prompt.dtype
    bp = x_prompt.shape[0]
    z_pool = jnp.zeros((DEPTH, bp, POOL_BUF, POOL_WIDTH), dt)
    z_sconv = jnp.zeros((DEPTH, bp, SCONV_K - 1, SCONV_WIDTH), dt)
    z_conf = jnp.zeros((DEPTH, bp, CONF_K - 1, CONF_WIDTH), dt)
    pos_p = jnp.arange(x_prompt.shape[1], dtype=jnp.int32)
    pos_s = PAST_LEN + jnp.arange(x_sample.shape[1], dtype=jnp.int32)
    y_prompt, np_pool, np_sconv, np_conf = trunk(
        x_prompt, c_prompt, z_pool, z_sconv, z_conf, pos_p, w_ada, b_ada, norm1_g, norm2_g, w_in,
        pool_w, pool_scale, sconv_w, conf_w, conf_b, conf_ln_g, conf_ln_b, w_out, w_ff1, w_ff2, final_g)
    y_sample, ns_pool, ns_sconv, ns_conf = trunk(
        x_sample, c_sample, state_pool, state_sconv, state_conf, pos_s, w_ada, b_ada, norm1_g, norm2_g,
        w_in, pool_w, pool_scale, sconv_w, conf_w, conf_b, conf_ln_g, conf_ln_b, w_out, w_ff1, w_ff2, final_g)
    return (y_prompt, y_sample, np_pool, np_sconv, np_conf, ns_pool, ns_sconv, ns_conf)


_drawn_inputs = setup_inputs


def setup_inputs(seed=0):
    import zlib

    import numpy as np

    out = dict(_drawn_inputs(seed))
    spreads = {}
    factors = {'b_ada': 3.001,
     'norm2_g': 6.242,
     'pool_scale': 3.806,
     'conf_b': 8.0,
     'conf_ln_g': 8.0,
     'conf_ln_b': 8.0,
     'final_g': 2.817}
    for name, (base, spread) in spreads.items():
        noise = np.random.default_rng([zlib.crc32(name.encode()), seed]).standard_normal(out[name].shape)
        drawn = base * np.exp(spread * noise) if base else spread * noise
        out[name] = __import__('jax').numpy.asarray(drawn.astype(out[name].dtype))
    for name, factor in factors.items():
        out[name] = (out[name] * factor).astype(out[name].dtype)
    return out
```

```python
from contextlib import ExitStack

import concourse.bass as bass
from concourse import mybir

F32 = mybir.dt.float32
F32R = mybir.dt.float32r
ALU = mybir.AluOpType
ACT = mybir.ActivationFunctionType
AX_X = mybir.AxisListType.X

P = 128
D = 1024
T = 1024
S = 8
N = T + S
NT = 3
TW = N // NT
KD = D // P
R = 1 + S
EPS = 1e-6
POOL_C, CONV_C = 2, 3
WINDOWS = (2, 4, 8, 16)
PBUF = 15
SK = 3
CK = 31
FF_C = 32
FG = 4
NG = FF_C // FG
PAD = 16
MROUNDS = 3
MC = 6 * KD // MROUNDS
ADA_SLOTS = 5
LASTC = 38

U0, GB0, GC0, V0, GA0, GG0 = 0, 2, 5, 8, 11, 14


def plan():
    units, chunks = [], []

    def chunk(name, by):
        chunks.append((name, by))

    chunk("states", "V")
    for i in range(KD):
        chunk(("x", i), "V")
    chunk("norm1", "-")
    for c in range(CONV_C):
        units.append((("gg", c), len(chunks)))
        chunk(("gg", c), "-")
        units.append((("ga", c), len(chunks)))
        chunk(("ga", c), "-")
    for c in range(POOL_C):
        units.append((("u", c), len(chunks)))
        chunk(("u", c), "-")
        if c == 1:
            chunk(("ya", 0), "-")
    for c in range(CONV_C):
        units.append((("v", c), len(chunks)))
        chunk(("v", c), "-")
        if c == 0:
            chunk(("ya", 1), "-")
        units.append((("gc", c), len(chunks)))
        chunk(("gc", c), "V")
        units.append((("gb", c), len(chunks)))
        chunk(("gb", c), "-")
    for d in range(KD):
        units.append((("p1", d), len(chunks)))
        chunk(("p1", d), "V")
        if d == 1:
            chunk("lnmean", "-")
        if d == 4:
            chunk("lnvar", "-")
    for d in range(KD):
        if d % 2 == 1:
            units.append((("p2", d // 2), len(chunks)))
        chunk(("p2", d), "V")
    chunk("norm2", "-")
    return units, chunks


UNITS, CHUNKS = plan()
UNIT_AT = {name: i for i, (name, _) in enumerate(UNITS)}
CHUNK_AT = {name: i for i, (name, _) in enumerate(CHUNKS)}
U_FF = len(UNITS)
C_FF = len(CHUNKS)
FREED_V = [sum(by == "V" for _, by in CHUNKS[:i + 1]) for i in range(C_FF)]
V_FF = FREED_V[-1]
C_FIN = C_FF + FF_C + NG * KD
U_END = U_FF + 2 * FF_C
BLOCKS = {"gg": 8, "ga": 8, "u": 8, "v": 8, "gc": 8, "gb": 8, "p1": 5, "p2": 6}
ADA_AFTER = {UNIT_AT[("gg", 0)]: 3, UNIT_AT[("ga", 0)]: 3, UNIT_AT[("gg", 1)]: 2,
             UNIT_AT[("ga", 1)]: 3, UNIT_AT[("gg", 2)]: 3, UNIT_AT[("ga", 2)]: 2}


def decoder_trunk(nc, x_prompt, x_sample, c_prompt, c_sample, state_pool, state_sconv, state_conf,
                  w_ada, b_ada, norm1_g, norm2_g, w_in, pool_w, pool_scale, sconv_w, conf_w,
                  conf_b, conf_ln_g, conf_ln_b, w_out, w_ff1, w_ff2, final_g,
                  y_prompt, y_sample, np_pool, np_sconv, np_conf, ns_pool, ns_sconv, ns_conf):
    ctx = ExitStack()

    def sb(name, shape, dt=F32, scope=ctx):
        return scope.enter_context(nc.sbuf_tensor(name, shape, dt))

    def sem(name):
        return ctx.enter_context(nc.semaphore(name))

    with ctx:
        xT = sb("xT", [P, KD, N])
        whi = sb("whi", [P, 2, 8, P], F32R)
        wlo = sb("wlo", [P, 2, 8, P], F32R)
        wraw = sb("wraw", [P, 2, 8 * P])
        work = [sb(f"work{i}", [P, PAD + N]) for i in range(3)]
        wk = [w[:, PAD:] for w in work]
        ident = sb("ident", [P, P])
        ones = sb("ones", [P, P])
        modT = sb("modT", [P, 6 * KD, R])
        vecT = sb("vecT", [P, 84])
        tapT = sb("tapT", [P, CK * CONV_C])
        cT = sb("cT", [P, KD, 32])
        A1 = sb("A1", [P, KD, R])
        A2 = sb("A2", [P, KD, R])
        pw = sb("pw", [P, POOL_C, P])
        past_pool = sb("past_pool", [P, POOL_C, S])
        past_sconv = sb("past_sconv", [P, CONV_C, S])
        past_conf = sb("past_conf", [P, CONV_C, S])
        head_rc = sb("head_rc", [P, POOL_C, PAD])
        gate_s = sb("gate_s", [P, KD, S])
        hs = sb("hs", [P, KD, S])
        small = sb("small", [P, KD, S])
        last_cols = sb("last_cols", [P, 2, P])
        states_out = sb("states_out", [P, 2, P])
        sumsq = sb("sumsq", [P, R])
        rstd = sb("rstd", [P, R])

        b_adaT = vecT[:, 0:48]
        n1T, n2T = vecT[:, 48:56], vecT[:, 56:64]
        pscaleT = vecT[:, 64:66]
        sconvT = vecT[:, 66:75]
        cbT, lgT, lbT = vecT[:, 75:78], vecT[:, 78:81], vecT[:, 81:84]

        with ExitStack() as scope:
            ada1 = sb("ada1", [P, KD, 2048], scope=scope)
        hhi = sb("hhi", [P, KD, N], F32R)
        hlo = sb("hlo", [P, KD, N], F32R)
        with ExitStack() as scope:
            xrow = sb("xrow", [P, KD, D], scope=scope)
            xsrow = sb("xsrow", [S, D], scope=scope)
            crow = sb("crow", [32, D], scope=scope)
            csig = sb("csig", [32, D], scope=scope)
            vrow = sb("vrow", [84, P], scope=scope)
            taprow = sb("taprow", [CK * CONV_C, P], scope=scope)
            st_pool = sb("st_pool", [S * PBUF, 256], scope=scope)
            st_conf = sb("st_conf", [S // 2 * (CK - 1), 2, 384], scope=scope)
            st_sconv = sb("st_sconv", [S * (SK - 1), 384], scope=scope)
            past_prod = sb("past_prod", [P, S * (CK - 1)], scope=scope)
        with ExitStack() as scope:
            with ExitStack() as heads:
                glu = sb("glu", [P, CONV_C, N], scope=heads)
                dc = sb("dc", [P, CONV_C, N], scope=heads)
                ada2 = sb("ada2", [P, ADA_SLOTS, 2048], scope=heads)
            yc_hi = sb("yc_hi", [P, CONV_C, N], F32R, scope=scope)
            yc_lo = sb("yc_lo", [P, CONV_C, N], F32R, scope=scope)
            yab_hi = sb("yab_hi", [P, 5, N], F32R, scope=scope)
            yab_lo = sb("yab_lo", [P, 5, N], F32R, scope=scope)
        hid_hi = sb("hid_hi", [P, 2 * FG, N], F32R)
        hid_lo = sb("hid_lo", [P, 2 * FG, N], F32R)

        acc = ctx.enter_context(nc.psum_tensor("acc", [P, 2, 3, 512], F32))
        modps = ctx.enter_context(nc.psum_tensor("modps", [P, 512], F32))
        tps = ctx.enter_context(nc.psum_tensor("tps", [P, 512], F32))

        const_ready = sem("const_ready")
        crow_cleared = sem("crow_cleared")
        c_loaded = sem("c_loaded")
        vec_loaded = sem("vec_loaded")
        st_loaded = sem("st_loaded")
        pw_loaded = sem("pw_loaded")
        x_loaded = [sem(f"x_loaded{i}") for i in range(KD)]
        ada1_loaded = [sem(f"ada1_loaded{k}") for k in range(KD)]
        ada2_loaded = [sem(f"ada2_loaded{k}") for k in range(ADA_SLOTS)]
        w_loaded = [sem(f"w_loaded{s}") for s in range(2)]
        whi_ready = sem("whi_ready")
        wlo_ready = sem("wlo_ready")
        psum_full = sem("psum_full")
        freed_v = sem("freed_v")
        tps_full = sem("tps_full")
        tps_read = sem("tps_read")
        csig_ready = sem("csig_ready")
        c_ready = sem("c_ready")
        sq_ready = sem("sq_ready")
        sq_used = sem("sq_used")
        xs_ready = sem("xs_ready")
        ada_used = sem("ada_used")
        mod_full = sem("mod_full")
        mod_rows = sem("mod_rows")
        mod_ready = sem("mod_ready")
        ms_ready = sem("ms_ready")
        root_ready = sem("root_ready")
        rstd_ready = sem("rstd_ready")
        hpre_ready = sem("hpre_ready")
        hhi_ready = sem("hhi_ready")
        hlo_ready = sem("hlo_ready")
        h_sample_ready = sem("h_sample_ready")
        sig_ready = sem("sig_ready")
        glu_ready = sem("glu_ready")
        conv_step = sem("conv_step")
        u_ready = sem("u_ready")
        pool_ready = sem("pool_ready")
        v_ready = sem("v_ready")
        yb_ready = sem("yb_ready")
        yhi_ready = sem("yhi_ready")
        ylo_ready = sem("ylo_ready")
        centred = sem("centred")
        ln_scaled = sem("ln_scaled")
        lsig_ready = sem("lsig_ready")
        silu_ready = sem("silu_ready")
        last_u = sem("last_u")
        last_v = sem("last_v")
        x_updated = sem("x_updated")
        relu_ready = sem("relu_ready")
        hid_hi_ready = sem("hid_hi_ready")
        hid_lo_ready = sem("hid_lo_ready")
        sumsq_ready = sem("sumsq_ready")
        out_ready = sem("out_ready")
        gain_loaded = sem("gain_loaded")
        y_stored = [sem(f"y_stored{i}") for i in range(2)]
        old_stored = sem("old_stored")
        new_stored = sem("new_stored")
        states_ready = sem("states_ready")
        order = sem("order")
        porder = sem("porder")

        def chunk_of(n):
            return acc[:, n % 2, :, :]

        def flat(ap):
            return ap[:, :, 0:TW]

        def tiled(ap):
            return ap.rearrange("p (t w) -> p t w", t=NT)

        def pair(ap):
            return ap.rearrange("p (t w) -> p t w", t=2)

        def w_source(u):
            name, _ = UNITS[u]
            kind, c = name
            col0 = {"gg": GG0, "ga": GA0, "u": U0, "v": V0, "gc": GC0, "gb": GB0}
            if kind in col0:
                j = col0[kind] + c
                return w_in[0, :, j * P:(j + 1) * P].rearrange("(k p) n -> p k n", p=P)
            if kind == "p1":
                return w_out[0, 0:5 * P, c * P:(c + 1) * P].rearrange("(k p) n -> p k n", p=P)
            return w_out[0, 5 * P:8 * P, c * 256:(c + 1) * 256].rearrange("(k p) n -> p k n", p=P)

        def blocks_of(u):
            return BLOCKS[UNITS[u][0][0]]

        w1v = w_ff1[0].rearrange("(k p) n -> p k n", p=P)
        w2v = w_ff2[0].rearrange("(f p) n -> p f n", p=P)

        block = ctx.enter_context(nc.Block())

        @block.sync
        def _(sp):
            def load_w(u):
                if u >= 2:
                    sp.wait_ge(wlo_ready, u - 1)
                src = w_source(u)
                n = blocks_of(u) * P
                dst = wraw[:, u % 2, 0:n].rearrange("p (k n) -> p k n", k=src.shape[1])
                sp.dma_start(dst, src).then_inc(w_loaded[u % 2], 16)

            def load_ada(s):
                b, k = 1 + s // KD, s % KD
                if s >= ADA_SLOTS:
                    used = KD + s - ADA_SLOTS
                    if used % KD == KD - 1:
                        sp.wait_ge(mod_full, used // KD + 1)
                    else:
                        sp.wait_ge(ada_used, used + 1 - used // KD)
                sp.dma_start(ada2[:, s % ADA_SLOTS, :],
                             w_ada[0, k * P:(k + 1) * P, b * 2048:(b + 1) * 2048]
                             ).then_inc(ada2_loaded[s % ADA_SLOTS], 16)

            for i in range(KD):
                sp.dma_start(xrow[:, i, :], x_prompt[0, i * P:(i + 1) * P, :]).then_inc(x_loaded[i], 16)
            for k in range(KD):
                sp.dma_start(ada1[:, k, :], w_ada[0, k * P:(k + 1) * P, 0:2048]
                             ).then_inc(ada1_loaded[k], 16)
            load_w(0)
            load_w(1)
            sp.wait_ge(psum_full, CHUNK_AT["norm1"] + 1)
            sp.wait_ge(freed_v, FREED_V[CHUNK_AT["states"]])
            for s in range(ADA_SLOTS):
                load_ada(s)
            s = ADA_SLOTS
            for u in range(2, U_FF):
                more = sum(n for v, n in ADA_AFTER.items() if v <= u - 2)
                while s < 16 and s < ADA_SLOTS + more:
                    load_ada(s)
                    s += 1
                load_w(u)

            def load_ff(u, slot, src, k):
                sp.wait_ge(wlo_ready, u - 1)
                sp.dma_start(wraw[:, slot, :].rearrange("p (k n) -> p k n", k=k), src
                             ).then_inc(w_loaded[slot], 16)

            def load_up(u0, f0):
                for j in range(FG):
                    load_ff(u0 + j, (U_FF + j) % 2, w1v[:, :, bass.ds((f0 + j) * P, P)], KD)

            def load_down(u0, f0):
                for j in range(FG):
                    load_ff(u0 + j, (U_FF + j) % 2, w2v[:, bass.ds(f0, FG), j * 256:(j + 1) * 256], FG)

            load_up(U_FF, 0)
            with sp.Fori(0, NG - 1) as g:
                load_up(U_FF + 4 + g * 8, g * FG + FG)
                load_down(U_FF + 8 + g * 8, g * FG)
            load_down(U_FF + 60, (NG - 1) * FG)

            sp.wait_ge(wlo_ready, U_END - 1)
            sp.dma_start(wraw[:, (U_END - 2) % 2, :], final_g.rearrange("(a n) -> a n", a=1)
                         .broadcast_to([P, D])).then_inc(gain_loaded, 16)
            for i in range(KD + 1):
                sp.wait_ge(out_ready, i + 1)
                if i < KD:
                    sp.dma_start(y_prompt[0, i * P:(i + 1) * P, :], wk[i % 2][:, 0:D]
                                 ).then_inc(y_stored[i % 2], 16)
                else:
                    sp.dma_start(y_sample.rearrange("s a d -> (s a) d"), wk[i % 2][P - S:P, 0:D]
                                 ).then_inc(y_stored[i % 2], 16)
            sp.wait_ge(y_stored[0], 16 * 5)
            sp.wait_ge(y_stored[1], 16 * 4)

        @block.gpsimd
        def _(pool):
            nc.gpsimd.memset(crow[:], 0.0).then_inc(crow_cleared, 1)
            made = 0

            def const(ins):
                nonlocal made
                made += 1
                ins.then_inc(const_ready, 1)
                return made

            const(nc.gpsimd.memset(ones[:], 1.0))
            pool.wait_ge(const_ready, const(nc.gpsimd.memset(ident[:], 0.0)))
            const(nc.gpsimd.affine_select(out=ident[:], in_=ident[:], compare_op=ALU.not_equal, fill=1.0,
                                          base=0, pattern=[[-1, P]], channel_multiplier=1))
            const(nc.gpsimd.memset(pw[:], 0.0))
            const(nc.gpsimd.memset(last_cols[:], 0.0))
            for w in work:
                const(nc.gpsimd.memset(w[:, 0:PAD], 0.0))
            for g, w in enumerate(WINDOWS):
                half = slice(64 * (g % 2), 64 * (g % 2) + 64)
                pool.wait_ge(const_ready, const(nc.gpsimd.memset(head_rc[half, g // 2, :], 1.0 / w)))
                for t in range(w - 1):
                    const(nc.gpsimd.memset(head_rc[half, g // 2, t:t + 1], 1.0 / (t + 1)))

            def low(u, slot, n):
                pool.wait_ge(whi_ready, u + 1)
                a = wraw[:, slot, 0:n * P]
                b = whi[:, slot, 0:n, :].bitcast(F32).rearrange("p k n -> p (k n)")
                o = wlo[:, slot, 0:n, :].rearrange("p k n -> p (k n)")
                nc.gpsimd.tensor_tensor(o, a, b, ALU.subtract).then_inc(wlo_ready, 1)

            links = 0

            def link(ins):
                nonlocal links
                links += 1
                ins.then_inc(porder, 1)
                pool.wait_ge(porder, links)

            def sample_h(n, A, shift):
                pool.wait_ge(rstd_ready, n + 1)
                xs = xT[:, :, T:N]
                r = wk[0][:, T:N].unsqueeze(1).broadcast_to([P, KD, S])
                link(nc.gpsimd.tensor_tensor(hs[:], xs, r, ALU.mult))
                link(nc.gpsimd.tensor_tensor(hs[:], hs[:], A[:, :, 1:R], ALU.mult))
                link(nc.gpsimd.tensor_tensor(hs[:], hs[:], modT[:, shift:shift + KD, 1:R], ALU.add))
                link(nc.gpsimd.tensor_copy(hhi[:, :, T:N], hs[:]))
                nc.gpsimd.tensor_tensor(hlo[:, :, T:N], hs[:], hhi[:, :, T:N].bitcast(F32),
                                        ALU.subtract).then_inc(h_sample_ready, 1)

            pool.wait_ge(const_ready, made)
            low(0, 0, 8)
            low(1, 1, 8)
            sample_h(0, A1, 0)
            for u in range(2, U_FF):
                low(u, u % 2, blocks_of(u))
            low(U_FF, U_FF % 2, 8)
            low(U_FF + 1, (U_FF + 1) % 2, 8)
            sample_h(1, A2, 3 * KD)
            with pool.Fori(U_FF + 2, U_END, 2) as u:
                low(u, U_FF % 2, 8)
                low(u + 1, (U_FF + 1) % 2, 8)

        @block.scalar
        def _(act):
            act.wait_ge(crow_cleared, 1)
            act.dma_start(crow[0:1, :], c_prompt).then_inc(c_loaded, 16)
            act.dma_start(crow[1:R, :], c_sample).then_inc(c_loaded, 16)
            rows = [(b_ada, 48), (norm1_g, 8), (norm2_g, 8), (pool_scale, 2), (sconv_w, 9),
                    (conf_b, 3), (conf_ln_g, 3), (conf_ln_b, 3)]
            at = 0
            for v, n in rows:
                v2 = (v.rearrange("l a n -> (l a n)") if len(v.shape) == 3 else v.rearrange("l n -> (l n)"))
                act.dma_start(vrow[at:at + n, :], v2.rearrange("(c p) -> c p", p=P)).then_inc(vec_loaded, 16)
                at += n
            act.dma_start(taprow[:], conf_w.rearrange("l a n -> (l a n)").rearrange("(c p) -> c p", p=P)
                          ).then_inc(vec_loaded, 16)
            act.dma_start(st_pool[:], state_pool.rearrange("l b t n -> (l b t) n")).then_inc(st_loaded, 16)
            act.dma_start(st_sconv[:], state_sconv.rearrange("l b t n -> (l b t) n")).then_inc(st_loaded, 16)
            conf_rows = state_conf.rearrange("l b t n -> (l b t) n")
            for i in range(2):
                act.dma_start(st_conf[:, i, :], conf_rows[i * 120:(i + 1) * 120, :]).then_inc(st_loaded, 16)
            act.dma_start(xsrow[:], x_sample.rearrange("s a d -> (s a) d")).then_inc(st_loaded, 16)
            act.wait_ge(const_ready, 4)
            for g in range(4):
                h = 64 * (g % 2)
                act.dma_start(pw[h:h + 64, g // 2, h:h + 64], pool_w[0, g]).then_inc(pw_loaded, 16)
            act.dma_start(ns_pool[0, :, 0:PBUF - 1, :], state_pool[0, :, 1:PBUF, :]).then_inc(old_stored, 16)
            act.dma_start(ns_sconv[0, :, 0:SK - 2, :], state_sconv[0, :, 1:SK - 1, :]).then_inc(old_stored, 16)
            act.dma_start(ns_conf[0, :, 0:CK - 2, :], state_conf[0, :, 1:CK - 1, :]).then_inc(old_stored, 16)

            act.wait_ge(c_loaded, 32)
            nc.scalar.activation(csig[:], crow[:], ACT.Sigmoid).then_inc(csig_ready, 1)

            for i in range(KD + 1):
                if i < KD:
                    act.wait_ge(freed_v, FREED_V[CHUNK_AT[("x", i)]])
                    src, dst = xT[:, :, i * P:(i + 1) * P], wk[i % 3][:, 0:D].rearrange("p (k n) -> p k n", k=KD)
                else:
                    act.wait_ge(xs_ready, 1)
                    src, dst = xT[:, :, T:N], wk[i % 3][:, 0:KD * S].rearrange("p (k n) -> p k n", k=KD)
                if i >= 3:
                    act.wait_ge(sq_used, i - 2)
                nc.scalar.activation(dst, src, ACT.Square).then_inc(sq_ready, 1)

            def high(u, slot, n, nth, prev_chunk):
                act.wait_ge(w_loaded[slot], nth * 16)
                if prev_chunk is not None:
                    act.wait_ge(psum_full, prev_chunk + 1)
                nc.scalar.activation(whi[:, slot, 0:n, :].rearrange("p k n -> p (k n)"),
                                     wraw[:, slot, 0:n * P], ACT.Copy).then_inc(whi_ready, 1)

            def high_of(u):
                if u < U_FF:
                    n = blocks_of(u)
                else:
                    n = 8
                high(u, u % 2, n, u // 2 + 1, UNITS[u - 2][1] if u >= 2 else None)

            high_of(0)
            high_of(1)

            def root(n):
                act.wait_ge(ms_ready, n + 1)
                nc.scalar.activation(wk[0][:], wk[0][:], ACT.Sqrt).then_inc(root_ready, 1)

            def h_high(n, shift):
                for k in range(KD):
                    act.wait_ge(hpre_ready, n * KD + k + 1)
                    nc.scalar.activation(hhi[:, k, 0:T], wk[1 + k % 2][:, 0:T], ACT.Identity,
                                         bias=modT[:, shift + k, 0:1]).then_inc(hhi_ready, 1)

            root(0)
            h_high(0, 0)


            def ya_high(c):
                n = CHUNK_AT[("ya", c)]
                act.wait_ge(psum_full, n + 1)
                nc.scalar.activation(tiled(yab_hi[:, c, :]), flat(chunk_of(n)), ACT.Copy,
                                     scale=pscaleT[:, c:c + 1]).then_inc(yhi_ready, 1)

            for u in range(U_FF):
                (kind, c), n = UNITS[u]
                ps = flat(chunk_of(n))
                high_of(u + 2)
                if kind == "gg":
                    if c:
                        act.wait_ge(glu_ready, c)
                    nc.scalar.activation(tiled(wk[2]), ps, ACT.Sigmoid).then_inc(sig_ready, 1)
                if kind == "u":
                    nc.scalar.activation(last_cols[:, 0, 23 * c:23 * c + 23],
                                         chunk_of(n)[:, 2, TW - 23:TW], ACT.Copy).then_inc(last_u, 1)
                    if c == 1:
                        act.wait_ge(pool_ready, 1)
                    nc.scalar.activation(tiled(wk[c]), ps, ACT.Copy).then_inc(u_ready, 1)
                    if c == 1:
                        ya_high(0)
                if kind == "v":
                    if c == 0:
                        act.wait_ge(pool_ready, 2)
                    else:
                        act.wait_ge(ylo_ready, POOL_C + c)
                    nc.scalar.activation(tiled(wk[0]), ps, ACT.Copy).then_inc(v_ready, 1)
                    if c == 0:
                        ya_high(1)
                if kind == "gb":
                    act.wait_ge(yb_ready, c + 1)
                    nc.scalar.activation(yab_hi[:, POOL_C + c, :], wk[0][:], ACT.Copy).then_inc(yhi_ready, 1)
                if kind == "p1" and c == 2:
                    for j in range(CONV_C):
                        act.wait_ge(centred, j + 1)
                        nc.scalar.activation(wk[j][:], dc[:, j, :], ACT.Square).then_inc(sq_ready, 1)
                if kind == "p1" and c == 5:
                    root(1)
                if kind == "p1" and c == 5:
                    act.wait_ge(states_ready, 1)
                    for j in range(POOL_C):
                        r, cols = 23 * j, slice(j * P, (j + 1) * P)
                        act.dma_start(np_pool[0, 0, :, cols], states_out[r:r + PBUF, 0, :]).then_inc(new_stored, 16)
                        act.dma_start(ns_pool[0, :, PBUF - 1, cols], states_out[r + PBUF:r + 23, 0, :]
                                      ).then_inc(new_stored, 16)
                    for j in range(CONV_C):
                        r, cols = 46 + 10 * j, slice(j * P, (j + 1) * P)
                        act.dma_start(np_sconv[0, 0, :, cols], states_out[r:r + 2, 0, :]).then_inc(new_stored, 16)
                        act.dma_start(ns_sconv[0, :, SK - 2, cols], states_out[r + 2:r + 10, 0, :]
                                      ).then_inc(new_stored, 16)
                        r = LASTC * j
                        act.dma_start(np_conf[0, 0, :, cols], states_out[r:r + CK - 1, 1, :]).then_inc(new_stored, 16)
                        act.dma_start(ns_conf[0, :, CK - 2, cols], states_out[r + CK - 1:r + LASTC, 1, :]
                                      ).then_inc(new_stored, 16)
                if kind == "p1" and c == 6:
                    for j in range(CONV_C):
                        act.wait_ge(ln_scaled, j + 1)
                        if j == 2:
                            act.wait_ge(silu_ready, 1)
                        nc.scalar.activation(wk[1 + j % 2][:], dc[:, j, :], ACT.Sigmoid,
                                             bias=lbT[:, j:j + 1]).then_inc(lsig_ready, 1)
                    for j in range(CONV_C):
                        act.wait_ge(silu_ready, j + 1)
                        nc.scalar.activation(yc_hi[:, j, :], dc[:, j, :], ACT.Copy).then_inc(yhi_ready, 1)

            act.wait_ge(x_updated, 4)
            for k in range(KD):
                if k >= 3:
                    act.wait_ge(sq_used, KD + k - 2)
                nc.scalar.activation(wk[k % 3][:], xT[:, k, :], ACT.Square).then_inc(sq_ready, 1)
            root(2)
            h_high(1, 3 * KD)


            def hidden(at, slot, j):
                act.wait_ge(psum_full, C_FF + at + 1)
                act.wait_ge(freed_v, V_FF + at)
                nc.scalar.activation(tiled(wk[0]), flat(acc[:, (C_FF + j) % 2, :, :]), ACT.Relu
                                     ).then_inc(relu_ready, 1)
                act.wait_ge(freed_v, V_FF + at + 1)
                nc.scalar.activation(hid_hi[:, slot + j, :], wk[1 + j % 2][:], ACT.Copy
                                     ).then_inc(hid_hi_ready, 1)

            def high_ff(j0, pairs, last):
                u = U_FF + j0 + 2
                high(u, u % 2, 8, u // 2 + 1 + pairs, C_FF + last)

            for j in range(FG):
                high_ff(j, 0, j)
                hidden(j, 0, j)

            def step(g, slot):
                for j in range(FG):
                    high_ff(4 + j, g * 4, g * 12 + 4 + j)
                    hidden(g * 12 + 4 + j, slot, j)
                for j in range(FG):
                    high_ff(8 + j, g * 4, g * 12 + 9 + 2 * j)

            with act.Fori(0, NG - 2, 2) as g:
                step(g, FG)
                step(g + 1, 0)
            step(NG - 2, FG)
            for j in range(2):
                high_ff(60 + j, 0, C_FIN - C_FF - 2 * FG + 2 * j + 1)

            def row_sum(i):
                act.wait_ge(psum_full, C_FIN + i + 1)
                if i:
                    act.wait_ge(sumsq_ready, i)
                nc.scalar.activation(pair(wk[2][:, 0:D]), acc[:, (C_FIN + i) % 2, 0:2, :], ACT.Square,
                                     accum_out=sumsq[:, i:i + 1]).then_inc(sumsq_ready, 1)

            row_sum(0)
            for i in range(KD + 1):
                if i < KD:
                    row_sum(i + 1)
                act.wait_ge(ms_ready, 3 + i + 1)
                nc.scalar.activation(rstd[:, i:i + 1], rstd[:, i:i + 1], ACT.Sqrt).then_inc(root_ready, 1)
            act.wait_ge(old_stored, 16 * 3 if SK > 2 else 0)
            act.wait_ge(new_stored, 16 * (2 * POOL_C + 4 * CONV_C))

        @block.vector
        def _(dve):
            links = 0

            def link(ins):
                nonlocal links
                links += 1
                ins.then_inc(order, 1)
                dve.wait_ge(order, links)

            dve.wait_ge(csig_ready, 1)
            nc.vector.tensor_tensor(csig[:], crow[:], csig[:], ALU.mult).then_inc(c_ready, 1)
            dve.wait_ge(tps_full, 1)
            nc.vector.tensor_copy(cT[:], tps[:, 192:448].rearrange("p (k r) -> p k r", k=KD)).then_inc(tps_read, 1)
            nc.vector.tensor_copy(vecT[:], tps[:, 0:84]).then_inc(tps_read, 1)
            nc.vector.tensor_copy(tapT[:], tps[:, 84:84 + CK * CONV_C]).then_inc(tps_read, 1)
            dve.wait_ge(tps_read, 3)

            dve.wait_ge(psum_full, 1)
            dve.wait_ge(const_ready, 8)
            nc.vector.tensor_copy(xT[:, :, T:N], acc[:, 0, 2, 256:256 + KD * S].rearrange("p (k s) -> p k s", k=KD)
                                  ).then_inc(xs_ready, 1)

            def past(dst, ps, taps, k):
                prod = past_prod[:, 0:S * k].rearrange("p (b t) -> p b t", b=S)
                link(nc.vector.tensor_tensor(prod, ps.rearrange("p (b t) -> p b t", b=S),
                                             taps.unsqueeze(1).broadcast_to([P, S, k]), ALU.mult))
                link(nc.vector.tensor_reduce(dst, prod, AX_X, ALU.add))

            for c in range(CONV_C):
                conf_taps = tapT[:].rearrange("p (j c) -> p c j", c=CONV_C)[:, c, 0:CK - 1]
                past(past_conf[:, c, :], acc[:, 0, c, 0:S * (CK - 1)], conf_taps, CK - 1)
                taps = sconvT.rearrange("p (j c) -> p c j", c=CONV_C)[:, c, 0:SK - 1]
                past(past_sconv[:, c, :], acc[:, 0, c, 240:240 + S * (SK - 1)], taps, SK - 1)
            for g, w in enumerate(WINDOWS):
                half, c = slice(64 * (g % 2), 64 * (g % 2) + 64), g // 2
                rows = acc[half, 0, c, 256:256 + S * PBUF].rearrange("p (b t) -> p b t", b=S)
                ins = nc.vector.tensor_reduce(past_pool[half, c, :], rows[:, :, PBUF - (w - 1):PBUF], AX_X, ALU.add)
                if g < 3:
                    link(ins)
                else:
                    ins.then_inc(freed_v, 1)

            for i in range(KD):
                n = CHUNK_AT[("x", i)]
                dve.wait_ge(psum_full, n + 1)
                nc.vector.tensor_copy(xT[:, :, i * P:(i + 1) * P],
                                      chunk_of(n)[:, 0:2, :].rearrange("p a (b n) -> p (a b) n", n=P)
                                      ).then_inc(freed_v, 1)

            def mod_to_rows(b):
                dve.wait_ge(mod_full, b + 1)
                nc.vector.tensor_copy(wk[1][:, 0:512], modps[:]).then_inc(mod_rows, 1)

            def mod_finish(b):
                dve.wait_ge(tps_full, 2 + b)
                src = tps[:].rearrange("p (q j r) -> p j q r", q=4, j=4)[:, :, :, 0:R]
                dst = modT[:, b * MC:(b + 1) * MC, :].rearrange("p (j q) r -> p j q r", q=4)
                bias = b_adaT[:, b * MC:(b + 1) * MC].rearrange("p (j q) -> p j q", q=4)
                for j in range(4):
                    ins = nc.vector.tensor_tensor(dst[:, j], src[:, j],
                                                  bias[:, j].unsqueeze(2).broadcast_to([P, 4, R]), ALU.add)
                    if j < 3:
                        ins.then_inc(order, 1)
                ins.then_inc(mod_ready, 1)
                nonlocal links
                links += 3
                dve.wait_ge(order, links)
                dve.wait_ge(mod_ready, b + 1)

            def gains(A, scale, gT):
                nc.vector.scalar_tensor_tensor(A[:], modT[:, scale:scale + KD, :], 1.0,
                                               gT.unsqueeze(2).broadcast_to([P, KD, R]),
                                               ALU.add, ALU.mult).then_inc(order, 1)
                nonlocal links
                links += 1
                dve.wait_ge(order, links)

            def invert(n):
                dve.wait_ge(root_ready, n + 1)

            def h_low(nth, A, shift):
                def pre(k):
                    if k >= 2:
                        dve.wait_ge(hlo_ready, nth * KD + k - 1)
                    nc.vector.scalar_tensor_tensor(wk[1 + k % 2][:, 0:T], xT[:, k, 0:T], A[:, k, 0:1],
                                                   wk[0][:, 0:T], ALU.mult, ALU.mult).then_inc(hpre_ready, 1)

                pre(0)
                for k in range(KD):
                    if k + 1 < KD:
                        pre(k + 1)
                    dve.wait_ge(hpre_ready, nth * KD + k + 1)
                    dve.wait_ge(hhi_ready, nth * KD + k + 1)
                    nc.vector.scalar_tensor_tensor(hlo[:, k, 0:T], wk[1 + k % 2][:, 0:T],
                                                   modT[:, shift + k, 0:1], hhi[:, k, 0:T].bitcast(F32),
                                                   ALU.add, ALU.subtract).then_inc(hlo_ready, 1)

            dve.wait_ge(psum_full, CHUNK_AT["norm1"] + 1)
            nc.vector.tensor_scalar(pair(wk[0][:, 0:T]), acc[:, :, 2, :], 1.0 / D, EPS, ALU.mult, ALU.add
                                    ).then_inc(order, 1)
            links += 1
            nc.vector.tensor_scalar(wk[0][:, T:N], tps[:, 448:448 + S], 1.0 / D, EPS, ALU.mult, ALU.add
                                    ).then_inc(ms_ready, 1)
            mod_to_rows(0)
            mod_finish(0)
            gains(A1, KD, n1T)
            dve.wait_ge(root_ready, 1)
            nc.vector.reciprocal(wk[0][:], wk[0][:]).then_inc(rstd_ready, 1)
            dve.wait_ge(rstd_ready, 1)
            h_low(0, A1, 0)

            steps = [(c, s) for c in range(CONV_C) for s in range(CK + 1)]
            done = 0

            def convolve(count):
                nonlocal done
                for c, s in steps[done:done + count]:
                    if s == 0:
                        dve.wait_ge(glu_ready, c + 1)
                        ins = nc.vector.tensor_scalar(dc[:, c, :], glu[:, c, :], tapT[:, 3 * (CK - 1) + c:3 * (CK - 1) + c + 1],
                                                      cbT[:, c:c + 1], ALU.mult, ALU.add)
                    else:
                        dve.wait_ge(conv_step, done)
                        if s < CK:
                            tap = 3 * (CK - 1 - s) + c
                            ins = nc.vector.scalar_tensor_tensor(dc[:, c, s:T], glu[:, c, 0:T - s], tapT[:, tap:tap + 1],
                                                                 dc[:, c, s:T], ALU.mult, ALU.add)
                        else:
                            ins = nc.vector.tensor_tensor(dc[:, c, T:N], dc[:, c, T:N], past_conf[:, c, :], ALU.add)
                    ins.then_inc(conv_step, 1)
                    done += 1

            def pooled(c):
                dve.wait_ge(u_ready, c + 1)
                u, s2 = work[c], work[2]
                if c == 0:
                    s4 = work[1]
                else:
                    dve.wait_ge(psum_full, CHUNK_AT[("ya", 0)] + 1)
                    s4 = work[0]

                def twice(dst, src, w, lo):
                    link(nc.vector.tensor_tensor(dst[lo:P, PAD:PAD + T], src[lo:P, PAD:PAD + T],
                                                 src[lo:P, PAD - w:PAD - w + T], ALU.add))

                twice(s2, u, 1, 0)
                if c == 0:
                    twice(s4, s2, 2, 64)
                    low, high_ = s2, s4
                else:
                    twice(s4, s2, 2, 0)
                    twice(s2, s4, 4, 0)
                    twice(s4, s2, 8, 64)
                    low, high_ = s2, s4
                for hf, s in ((0, low), (1, high_)):
                    p, w = slice(64 * hf, 64 * hf + 64), WINDOWS[2 * c + hf]
                    link(nc.vector.tensor_tensor(s[p, PAD + T:], u[p, PAD + T:], past_pool[p, c, :], ALU.add))
                    link(nc.vector.tensor_tensor(s[p, PAD:2 * PAD], s[p, PAD:2 * PAD], head_rc[p, c, :], ALU.mult))
                    link(nc.vector.tensor_tensor(u[p, PAD:2 * PAD], s[p, PAD:2 * PAD], u[p, PAD:2 * PAD], ALU.subtract))
                    ins = nc.vector.scalar_tensor_tensor(u[p, 2 * PAD:], s[p, 2 * PAD:], 1.0 / w, u[p, 2 * PAD:],
                                                         ALU.mult, ALU.subtract)
                    if hf == 0:
                        link(ins)
                    else:
                        ins.then_inc(pool_ready, 1)

            def ya_low(c):
                n = CHUNK_AT[("ya", c)]
                dve.wait_ge(yhi_ready, c + 1)
                nc.vector.scalar_tensor_tensor(tiled(yab_lo[:, c, :]), flat(chunk_of(n)), pscaleT[:, c:c + 1],
                                               tiled(yab_hi[:, c, :].bitcast(F32)), ALU.mult, ALU.subtract
                                               ).then_inc(ylo_ready, 1)

            def residual(n, d, gate):
                ps = acc[:, n % 2, :, :]
                g1 = modT[:, gate + d, 0:1]
                w2 = T - 2 * TW
                nc.vector.scalar_tensor_tensor(pair(xT[:, d, 0:2 * TW]), ps[:, 0:2, 0:TW], g1,
                                               pair(xT[:, d, 0:2 * TW]), ALU.mult, ALU.add)
                nc.vector.scalar_tensor_tensor(xT[:, d, 2 * TW:T], ps[:, 2, 0:w2], g1,
                                               xT[:, d, 2 * TW:T], ALU.mult, ALU.add)
                nc.vector.tensor_copy(gate_s[:, d, :], ps[:, 2, w2:TW]).then_inc(freed_v, 1)

            def residual_sample(gate, wait_copy, updated):
                dve.wait_ge(freed_v, wait_copy)
                nc.vector.tensor_tensor(small[:], gate_s[:], modT[:, gate:gate + KD, 1:R], ALU.mult
                                        ).then_inc(x_updated, 1)
                dve.wait_ge(x_updated, updated - 1)
                nc.vector.tensor_tensor(xT[:, :, T:N], xT[:, :, T:N], small[:], ALU.add).then_inc(x_updated, 1)

            for u in range(U_FF):
                (kind, c), n = UNITS[u]
                ps = flat(chunk_of(n))
                if kind == "gg" and c == 1:
                    pass
                if kind == "ga":
                    dve.wait_ge(psum_full, n + 1)
                    dve.wait_ge(sig_ready, c + 1)
                    nc.vector.tensor_tensor(last_cols[:, 1, LASTC * c:LASTC * c + LASTC],
                                            chunk_of(n)[:, 2, TW - LASTC:TW], wk[2][:, N - LASTC:N], ALU.mult
                                            ).then_inc(last_v, 1)
                    nc.vector.tensor_tensor(tiled(glu[:, c, :]), ps, tiled(wk[2]), ALU.mult).then_inc(glu_ready, 1)
                    if c == 1:
                        mod_to_rows(1)
                    if c == 2:
                        mod_to_rows(2)
                    convolve(14 if c < 2 else 7)
                if kind == "gg" and c == 2:
                    mod_finish(1)
                if kind == "u":
                    if c == 0:
                        mod_finish(2)
                        gains(A2, 4 * KD, n2T)
                    pooled(c)
                    convolve(4)
                    if c == 1:
                        ya_low(0)
                if kind == "v":
                    if c == 0:
                        ya_low(1)
                    convolve(7)
                if kind == "gc":
                    dve.wait_ge(psum_full, n + 1)
                    dve.wait_ge(v_ready, c + 1)
                    if c == 0:
                        dve.wait_ge(psum_full, CHUNK_AT[("ya", 1)] + 1)
                    nc.vector.tensor_tensor(last_cols[:, 0, 46 + 10 * c:56 + 10 * c],
                                            chunk_of(n)[:, 2, TW - 10:TW], wk[0][:, N - 10:N], ALU.mult
                                            ).then_inc(last_v, 1)
                    nc.vector.tensor_tensor(tiled(wk[1]), ps, tiled(wk[0]), ALU.mult).then_inc(freed_v, 1)
                    dve.wait_ge(freed_v, FREED_V[n])
                    cv, out = wk[1], wk[2]
                    tap = [sconvT[:, 3 * j + c:3 * j + c + 1] for j in range(SK)]
                    link(nc.vector.tensor_scalar(out[:], cv[:], tap[2], None, ALU.mult))
                    for s in (1, 2):
                        link(nc.vector.scalar_tensor_tensor(out[:, s:T], cv[:, 0:T - s], tap[2 - s], out[:, s:T],
                                                            ALU.mult, ALU.add))
                    link(nc.vector.tensor_tensor(out[:, T:N], out[:, T:N], past_sconv[:, c, :], ALU.add))
                    convolve(5)
                if kind == "gb":
                    dve.wait_ge(psum_full, n + 1)
                    nc.vector.tensor_tensor(tiled(wk[0]), ps, tiled(wk[2]), ALU.mult).then_inc(yb_ready, 1)
                    dve.wait_ge(yb_ready, c + 1)
                    dve.wait_ge(yhi_ready, POOL_C + c + 1)
                    nc.vector.tensor_tensor(yab_lo[:, POOL_C + c, :], wk[0][:], yab_hi[:, POOL_C + c, :].bitcast(F32),
                                            ALU.subtract).then_inc(ylo_ready, 1)
                    convolve(6 if c < 2 else 200)
                if kind == "p1":
                    dve.wait_ge(psum_full, n + 1)
                    residual(n, c, 2 * KD)
                    if c == 0:
                        dve.wait_ge(tps_full, 5)
                        nc.vector.tensor_copy(states_out[:], tps[:, 0:2 * P].rearrange("p (a n) -> p a n", a=2)
                                              ).then_inc(states_ready, 1)
                    if c == 2:
                        m = CHUNK_AT["lnmean"]
                        dve.wait_ge(psum_full, m + 1)
                        for j in range(CONV_C):
                            nc.vector.scalar_tensor_tensor(tiled(dc[:, j, :]), flat(chunk_of(m)), -1.0 / 384,
                                                           tiled(dc[:, j, :]), ALU.mult, ALU.add).then_inc(centred, 1)
                    if c == 5:
                        m = CHUNK_AT["lnvar"]
                        dve.wait_ge(psum_full, m + 1)
                        nc.vector.tensor_scalar(tiled(wk[0]), flat(chunk_of(m)), 1.0 / 384, EPS, ALU.mult, ALU.add
                                                ).then_inc(ms_ready, 1)
                    if c == 6:
                        dve.wait_ge(root_ready, 2)
                        link(nc.vector.reciprocal(wk[0][:], wk[0][:]))
                        dve.wait_ge(centred, CONV_C)
                        for j in range(CONV_C):
                            nc.vector.scalar_tensor_tensor(dc[:, j, :], dc[:, j, :], lgT[:, j:j + 1], wk[0][:],
                                                           ALU.mult, ALU.mult).then_inc(ln_scaled, 1)
                        for j in range(CONV_C):
                            dve.wait_ge(ln_scaled, j + 1)
                            dve.wait_ge(lsig_ready, j + 1)
                            nc.vector.scalar_tensor_tensor(dc[:, j, :], dc[:, j, :], lbT[:, j:j + 1], wk[1 + j % 2][:],
                                                           ALU.add, ALU.mult).then_inc(silu_ready, 1)
                        for j in range(CONV_C):
                            dve.wait_ge(silu_ready, j + 1)
                            dve.wait_ge(yhi_ready, 5 + j + 1)
                            nc.vector.tensor_tensor(yc_lo[:, j, :], dc[:, j, :], yc_hi[:, j, :].bitcast(F32),
                                                    ALU.subtract).then_inc(ylo_ready, 1)
                    if c == 7:
                        residual_sample(2 * KD, FREED_V[n], 2)
                if kind == "p2":
                    for d in (2 * c, 2 * c + 1):
                        m = CHUNK_AT[("p2", d)]
                        dve.wait_ge(psum_full, m + 1)
                        if d == 0:
                            dve.wait_ge(x_updated, 2)
                        residual(m, d, 2 * KD)
                    if c == 3:
                        residual_sample(2 * KD, V_FF, 4)

            dve.wait_ge(psum_full, CHUNK_AT["norm2"] + 1)
            nc.vector.tensor_scalar(tiled(wk[0]), flat(chunk_of(CHUNK_AT["norm2"])), 1.0 / D, EPS, ALU.mult, ALU.add
                                    ).then_inc(ms_ready, 1)
            dve.wait_ge(root_ready, 3)
            nc.vector.reciprocal(wk[0][:], wk[0][:]).then_inc(rstd_ready, 1)
            dve.wait_ge(rstd_ready, 2)
            h_low(1, A2, 3 * KD)

            def hidden(at, f, slot, j):
                dve.wait_ge(psum_full, C_FF + at + 1)
                dve.wait_ge(relu_ready, f + 1)
                q = wk[1 + j % 2]
                nc.vector.scalar_tensor_tensor(tiled(q), flat(acc[:, (C_FF + j) % 2, :, :]), 0.0, tiled(wk[0]),
                                               ALU.max, ALU.mult).then_inc(freed_v, 1)
                dve.wait_ge(freed_v, V_FF + at + 1)
                dve.wait_ge(hid_hi_ready, f + 1)
                nc.vector.tensor_tensor(hid_lo[:, slot + j, :], q[:], hid_hi[:, slot + j, :].bitcast(F32),
                                        ALU.subtract).then_inc(hid_lo_ready, 1)

            def down(at, updated):
                for d in range(KD):
                    dve.wait_ge(psum_full, C_FF + at + d + 1)
                    if d == 0:
                        dve.wait_ge(x_updated, updated)
                    residual(C_FF + d, d, 5 * KD)
                residual_sample(5 * KD, V_FF + at + KD, updated + 2)

            for j in range(FG):
                hidden(j, j, 0, j)

            def step(g, slot):
                for j in range(FG):
                    hidden(g * 12 + 4 + j, g * FG + FG + j, slot, j)
                down(g * 12 + 8, g * 2 + 4)

            with dve.Fori(0, NG - 2, 2) as g:
                step(g, FG)
                step(g + 1, 0)
            step(NG - 2, FG)
            down(C_FIN - C_FF - KD, 2 * (NG - 1) + 4)

            dve.wait_ge(gain_loaded, 16)
            gain = wraw[:, (U_END - 2) % 2, :]

            def mean_square(i):
                dve.wait_ge(sumsq_ready, i + 1)
                nc.vector.tensor_scalar(rstd[:, i:i + 1], sumsq[:, i:i + 1], 1.0 / D, EPS, ALU.mult, ALU.add
                                        ).then_inc(ms_ready, 1)

            mean_square(0)
            for i in range(KD + 1):
                if i < KD:
                    mean_square(i + 1)
                dve.wait_ge(root_ready, 3 + i + 1)
                link(nc.vector.reciprocal(rstd[:, i:i + 1], rstd[:, i:i + 1]))
                if i >= 2:
                    dve.wait_ge(y_stored[i % 2], 16 * (i // 2))
                nc.vector.scalar_tensor_tensor(pair(wk[i % 2][:, 0:D]), acc[:, (C_FIN + i) % 2, 0:2, :],
                                               rstd[:, i:i + 1], pair(gain), ALU.mult, ALU.mult
                                               ).then_inc(out_ready, 1)

        @block.tensor
        def _(pe):
            def freed(n):
                if n < 0:
                    return
                name, by = CHUNKS[n]
                if by == "V":
                    pe.wait_ge(freed_v, FREED_V[n])
                elif name == "norm1":
                    pe.wait_ge(ms_ready, 1)
                elif name == "lnmean":
                    pe.wait_ge(centred, CONV_C)
                elif name == "lnvar":
                    pe.wait_ge(ms_ready, 2)
                elif name == "norm2":
                    pe.wait_ge(ms_ready, 3)
                elif name[0] == "ya":
                    pe.wait_ge(ylo_ready, name[1] + 1)
                elif name[0] == "ga":
                    pe.wait_ge(glu_ready, name[1] + 1)
                elif name[0] == "gb":
                    pe.wait_ge(yb_ready, name[1] + 1)
                elif name[0] == "gg":
                    pe.wait_ge(sig_ready, name[1] + 1)
                elif name[0] == "u":
                    pe.wait_ge(u_ready, name[1] + 1)
                else:
                    pe.wait_ge(v_ready, name[1] + 1)

            def product(out, slot, blocks, hi, lo, ready=None):
                for i, (b, k) in enumerate(blocks):
                    if ready:
                        ready(k)
                    for w, x in ((whi, hi), (whi, lo), (wlo, hi)):
                        for t in range(NT):
                            last = nc.tensor.matmul(out[:, t, 0:TW], w[:, slot, b, :], x[:, k, t * TW:(t + 1) * TW],
                                                    start=(i == 0 and w is whi and x is hi),
                                                    stop=(i == len(blocks) - 1 and w is wlo))
                return last

            def sum_squares(out, rhs, first, last):
                return nc.tensor.matmul(out, ones[:], rhs, start=first, stop=last)

            pe.wait_ge(const_ready, 3)
            pe.wait_ge(vec_loaded, 16 * 9)
            nc.tensor.transpose(tps[:, 0:84], vrow[:], ident[0:84, 0:84])
            nc.tensor.transpose(tps[:, 84:84 + CK * CONV_C], taprow[:], ident[0:CK * CONV_C, 0:CK * CONV_C])
            pe.wait_ge(c_ready, 1)
            for k in range(KD):
                last = nc.tensor.transpose(tps[:, 192 + 32 * k:224 + 32 * k], csig[:, k * P:(k + 1) * P],
                                           ident[0:32, 0:32])
            last.then_inc(tps_full, 1)
            pe.wait_ge(st_loaded, 16 * 5)
            for c in range(CONV_C):
                cols = slice(c * P, (c + 1) * P)
                for i in range(2):
                    nc.tensor.transpose(acc[:, 0, c, i * 120:(i + 1) * 120], st_conf[:, i, cols], ident[0:120, 0:120])
                nc.tensor.transpose(acc[:, 0, c, 240:256], st_sconv[:, cols], ident[0:16, 0:16])
                if c < POOL_C:
                    nc.tensor.transpose(acc[:, 0, c, 256:376], st_pool[:, cols], ident[0:120, 0:120])
            for k in range(KD):
                last = nc.tensor.transpose(acc[:, 0, 2, 256 + 8 * k:264 + 8 * k], xsrow[:, k * P:(k + 1) * P],
                                           ident[0:S, 0:S])
            last.then_inc(psum_full, 1)

            def sum_tile(i):
                pe.wait_ge(sq_ready, i + 1)
                if i < KD:
                    sq, out = wk[i % 3][:, 0:D], acc[:, i // 4, 2, (i % 4) * P:(i % 4 + 1) * P]
                    w = P
                else:
                    sq, out = wk[i % 3][:, 0:KD * S], tps[:, 448:448 + S]
                    w = S
                    pe.wait_ge(tps_read, 3)
                for k in range(KD):
                    last = sum_squares(out, sq[:, k * w:(k + 1) * w], k == 0, k == KD - 1)
                last.then_inc(sq_used, 1) if i < KD else last.then_inc(psum_full, 1)

            for i in range(KD):
                n = CHUNK_AT[("x", i)]
                pe.wait_ge(x_loaded[i], 16)
                freed(n - 2)
                for k in range(KD):
                    last = nc.tensor.transpose(chunk_of(n)[:, k // 4, (k % 4) * P:(k % 4 + 1) * P],
                                               xrow[:, i, k * P:(k + 1) * P], ident[:])
                last.then_inc(psum_full, 1)
                if i == 0:
                    freed(0)
                if i:
                    sum_tile(i - 1)
            sum_tile(KD - 1)
            sum_tile(KD)

            def modulate(s):
                b, k = s // KD, s % KD
                if b == 0:
                    pe.wait_ge(ada1_loaded[k], 16)
                    src = ada1[:, k, :]
                    if k == 0:
                        pe.wait_ge(tps_read, 3)
                else:
                    q = s - KD
                    pe.wait_ge(ada2_loaded[q % ADA_SLOTS], 16 * (q // ADA_SLOTS + 1))
                    src = ada2[:, q % ADA_SLOTS, :]
                    if k == 0:
                        pe.wait_ge(mod_rows, b)
                for j in range(4):
                    last = nc.tensor.matmul(modps[32 * j:32 * j + 32, :], cT[:, k, :], src[:, j * 512:(j + 1) * 512],
                                            start=(k == 0), stop=(k == KD - 1), tile_position=(0, 32 * j),
                                            skip_group_check=True)
                last.then_inc(mod_full if k == KD - 1 else ada_used, 1)

            def mod_transpose(b):
                pe.wait_ge(mod_rows, b + 1)
                pe.wait_ge(ms_ready, 1) if b == 0 else pe.wait_ge(mod_ready, b)
                for q in range(4):
                    last = nc.tensor.transpose(tps[:, q * P:(q + 1) * P], wk[1][:, q * P:(q + 1) * P], ident[:])
                last.then_inc(tps_full, 1)

            for k in range(KD):
                modulate(k)
            mod_transpose(0)

            s = KD
            for u in range(U_FF):
                (kind, c), n = UNITS[u]
                pe.wait_ge(wlo_ready, u + 1)
                ready = None
                if u == 0:
                    pe.wait_ge(h_sample_ready, 1)
                    ready = lambda k: pe.wait_ge(hlo_ready, k + 1)
                if kind == "p1":
                    if c == 0:
                        pe.wait_ge(ylo_ready, 5)
                    blocks, hi, lo = [(b, b) for b in range(5)], yab_hi, yab_lo
                elif kind != "p2":
                    blocks, hi, lo = [(b, b) for b in range(KD)], hhi, hlo
                if kind != "p2":
                    freed(n - 2)
                    product(chunk_of(n), u % 2, blocks, hi, lo, ready).then_inc(psum_full, 1)
                else:
                    if c == 0:
                        pe.wait_ge(ylo_ready, 8)
                    for d in (2 * c, 2 * c + 1):
                        m = CHUNK_AT[("p2", d)]
                        freed(m - 2)
                        product(chunk_of(m), u % 2, [(2 * b + d % 2, b) for b in range(CONV_C)], yc_hi, yc_lo
                                ).then_inc(psum_full, 1)
                for _ in range(ADA_AFTER.get(u, 0)):
                    modulate(s)
                    s += 1
                if kind == "ga" and c == 1:
                    mod_transpose(1)
                if kind == "u" and c == 0:
                    mod_transpose(2)
                pooled = {("u", 1): 0, ("v", 0): 1}.get((kind, c))
                if pooled is not None:
                    m = CHUNK_AT[("ya", pooled)]
                    freed(m - 2)
                    pe.wait_ge(pool_ready, pooled + 1)
                    pe.wait_ge(pw_loaded, 16 * 4)
                    for t in range(NT):
                        last = nc.tensor.matmul(chunk_of(m)[:, t, 0:TW], pw[:, pooled, :],
                                                wk[pooled][:, t * TW:(t + 1) * TW], start=True, stop=True)
                    last.then_inc(psum_full, 1)
                if kind == "gb" and c == 2:
                    pe.wait_ge(mod_ready, 3)
                    pe.wait_ge(last_u, 2)
                    pe.wait_ge(last_v, 2 * CONV_C)
                    for a in range(2):
                        last = nc.tensor.transpose(tps[:, a * P:(a + 1) * P], last_cols[:, a, :], ident[:])
                    last.then_inc(tps_full, 1)
                if kind == "p1" and c in (1, 4):
                    m = CHUNK_AT["lnmean" if c == 1 else "lnvar"]
                    freed(m - 2)
                    for j in range(CONV_C):
                        if c == 1:
                            pe.wait_ge(conv_step, (j + 1) * (CK + 1))
                        else:
                            pe.wait_ge(sq_ready, KD + 1 + j + 1)
                        for t in range(NT):
                            cols = slice(t * TW, (t + 1) * TW)
                            src = dc[:, j, cols] if c == 1 else wk[j][:, cols]
                            last = sum_squares(chunk_of(m)[:, t, 0:TW], src, j == 0, j == CONV_C - 1)
                    last.then_inc(psum_full, 1)

            m = CHUNK_AT["norm2"]
            freed(m - 2)
            for k in range(KD):
                pe.wait_ge(sq_ready, KD + 1 + CONV_C + k + 1)
                for t in range(NT):
                    last = sum_squares(chunk_of(m)[:, t, 0:TW], wk[k % 3][:, t * TW:(t + 1) * TW], k == 0, k == KD - 1)
                last.then_inc(sq_used if k < KD - 1 else psum_full, 1)

            def up(at, j0, pairs, ready=None):
                for j in range(FG):
                    pe.wait_ge(wlo_ready, U_FF + j0 + j + 1 + pairs * 2)
                    freed_before(at + j)
                    product(acc[:, (C_FF + j) % 2, :, :], (U_FF + j) % 2, [(b, b) for b in range(KD)], hhi, hlo,
                            ready if j == 0 else None).then_inc(psum_full, 1)

            def freed_before(at):
                if isinstance(at, int) and at < 2:
                    freed(C_FF + at - 2)
                else:
                    pe.wait_ge(freed_v, V_FF - 1 + at)

            def down(at, j0, pairs, f, slot):
                pe.wait_ge(hid_lo_ready, f)
                for j in range(FG):
                    pe.wait_ge(wlo_ready, U_FF + j0 + j + 1 + pairs * 2)
                    for dd in range(2):
                        d = 2 * j + dd
                        freed_before(at + d)
                        product(acc[:, (C_FF + d) % 2, :, :], (U_FF + j) % 2,
                                [(2 * b + dd, slot + b) for b in range(FG)], hid_hi, hid_lo).then_inc(psum_full, 1)

            pe.wait_ge(h_sample_ready, 2)
            up(0, 0, 0, lambda k: pe.wait_ge(hlo_ready, KD + k + 1))

            def step(g, slot):
                up(g * 12 + 4, 4, g * 4)
                down(g * 12 + 8, 8, g * 4, g * FG + FG, FG - slot)

            with pe.Fori(0, NG - 2, 2) as g:
                step(g, FG)
                step(g + 1, 0)
            step(NG - 2, FG)
            down(C_FIN - C_FF - KD, 2 * FF_C - 4, 0, FF_C, FG)

            pe.wait_ge(x_updated, 2 * NG + 4)
            for i in range(KD + 1):
                if i >= 2:
                    pe.wait_ge(out_ready, i - 1)
                c0 = i * P if i < KD else N - P
                for k in range(KD):
                    last = nc.tensor.transpose(acc[:, (C_FIN + i) % 2, k // 4, (k % 4) * P:(k % 4 + 1) * P],
                                               xT[:, k, c0:c0 + P], ident[:])
                last.then_inc(psum_full, 1)


_INS = ["x_prompt", "x_sample", "c_prompt", "c_sample", "state_pool", "state_sconv", "state_conf", "w_ada", "b_ada",
        "norm1_g", "norm2_g", "w_in", "pool_w", "pool_scale", "sconv_w", "conf_w", "conf_b", "conf_ln_g",
        "conf_ln_b", "w_out", "w_ff1", "w_ff2", "final_g"]
_OUTS = [(1, T, D), (S, 1, D), (1, 1, PBUF, 256), (1, 1, SK - 1, 384), (1, 1, CK - 1, 384),
         (1, S, PBUF, 256), (1, S, SK - 1, 384), (1, S, CK - 1, 384)]


def kernel(**inputs):
    import numpy as _np
    import concourse.bacc as _bacc
    from concourse import mybir as _mybir
    from concourse.bass_utils import run_bass_kernel_spmd as _run

    nc = _bacc.Bacc("TRN2", target_bir_lowering=False, num_devices=1)
    arrays, args = {}, []
    for name in _INS:
        a = _np.ascontiguousarray(inputs[name])
        arrays[f"in_{name}"] = a
        args.append(nc.dram_tensor(f"in_{name}", a.shape, _mybir.dt.from_np(a.dtype), kind="ExternalInput").ap())
    for i, shape in enumerate(_OUTS):
        args.append(nc.dram_tensor(f"out_{i}", shape, F32, kind="ExternalOutput").ap())
    decoder_trunk(nc, *args)
    r = _run(nc, [arrays], core_ids=[0])
    return tuple(r.results[0][f"out_{i}"] for i in range(len(_OUTS)))
```

```python
from contextlib import ExitStack

import concourse.bass as bass
from concourse import mybir

F32 = mybir.dt.float32
F32R = mybir.dt.float32r
ALU = mybir.AluOpType
ACT = mybir.ActivationFunctionType
AX_X = mybir.AxisListType.X

P = 128
D = 1024
T = 1024
S = 8
N = T + S
NT = 3
TW = N // NT
KD = D // P
R = 1 + S
EPS = 1e-6
POOL_C, CONV_C = 2, 3
WINDOWS = (2, 4, 8, 16)
PBUF = 15
SK = 3
CK = 31
FF_C = 32
FG = 4
NG = FF_C // FG
PAD = 16
MROUNDS = 3
MC = 6 * KD // MROUNDS
ADA_SLOTS = 5
LASTC = 38

U0, GB0, GC0, V0, GA0, GG0 = 0, 2, 5, 8, 11, 14


def plan():
    units, chunks = [], []

    def chunk(name, by):
        chunks.append((name, by))

    for i in range(KD):
        chunk(("x", i), "V")
    chunk("states", "V")
    chunk("norm1", "-")
    for c in range(CONV_C):
        units.append((("gg", c), len(chunks)))
        chunk(("gg", c), "-")
        units.append((("ga", c), len(chunks)))
        chunk(("ga", c), "-")
    for c in range(POOL_C):
        units.append((("u", c), len(chunks)))
        chunk(("u", c), "-")
        if c == 1:
            chunk(("ya", 0), "-")
    for c in range(CONV_C):
        units.append((("v", c), len(chunks)))
        chunk(("v", c), "-")
        if c == 0:
            chunk(("ya", 1), "-")
        units.append((("gc", c), len(chunks)))
        chunk(("gc", c), "V")
        units.append((("gb", c), len(chunks)))
        chunk(("gb", c), "-")
    for d in range(KD):
        units.append((("p1", d), len(chunks)))
        chunk(("p1", d), "V")
        if d == 1:
            chunk("lnmean", "-")
        if d == 4:
            chunk("lnvar", "-")
    for d in range(KD):
        if d % 2 == 1:
            units.append((("p2", d // 2), len(chunks)))
        chunk(("p2", d), "V")
    chunk("norm2", "-")
    return units, chunks


UNITS, CHUNKS = plan()
UNIT_AT = {name: i for i, (name, _) in enumerate(UNITS)}
CHUNK_AT = {name: i for i, (name, _) in enumerate(CHUNKS)}
U_FF = len(UNITS)
C_FF = len(CHUNKS)
FREED_V = [sum(by == "V" for _, by in CHUNKS[:i + 1]) for i in range(C_FF)]
V_FF = FREED_V[-1]
C_FIN = C_FF + FF_C + NG * KD
U_END = U_FF + 2 * FF_C
LN_ROOT = 4
BLOCKS = {"gg": 8, "ga": 8, "u": 8, "v": 8, "gc": 8, "gb": 8, "p1": 5, "p2": 6}
ADA = MROUNDS * KD
ADA_AFTER = {1: 4, 2: 4, 3: 3, 4: 3, 5: 2}


def decoder_trunk(nc, x_prompt, x_sample, c_prompt, c_sample, state_pool, state_sconv, state_conf,
                  w_ada, b_ada, norm1_g, norm2_g, w_in, pool_w, pool_scale, sconv_w, conf_w,
                  conf_b, conf_ln_g, conf_ln_b, w_out, w_ff1, w_ff2, final_g,
                  y_prompt, y_sample, np_pool, np_sconv, np_conf, ns_pool, ns_sconv, ns_conf):
    ctx = ExitStack()
    COLS_AHEAD = 3
    LAG = 2
    SQ = {2: 0, 3: CONV_C, 4: CONV_C + KD}
    ADDED = {2: 0, 3: 1, 4: KD - 1}

    def sb(name, shape, dt=F32, scope=ctx):
        return scope.enter_context(nc.sbuf_tensor(name, shape, dt))

    def sem(name):
        return ctx.enter_context(nc.semaphore(name))

    with ctx:
        xT = sb("xT", [P, KD, N])
        whi = sb("whi", [P, 2, 8, P], F32R)
        wlo = sb("wlo", [P, 2, 8, P], F32R)
        wraw = sb("wraw", [P, 2, 8 * P])
        work = [sb(f"work{i}", [P, PAD + N]) for i in range(3)]
        wk = [w[:, PAD:] for w in work]
        ident = sb("ident", [P, P])
        ones = sb("ones", [P, P])
        halves = sb("halves", [P, 2, 32])
        modT = sb("modT", [P, 6 * KD, R])
        vecT = sb("vecT", [P, 84])
        tapT = sb("tapT", [P, CK * CONV_C])
        cT = sb("cT", [P, KD, 32])
        A1 = sb("A1", [P, KD, R])
        A2 = sb("A2", [P, KD, R])
        pw = sb("pw", [P, POOL_C, P])
        past_pool = sb("past_pool", [P, POOL_C, S])
        past_sconv = sb("past_sconv", [P, CONV_C, S])
        past_conf = sb("past_conf", [P, CONV_C, S])
        head_rc = sb("head_rc", [P, POOL_C, PAD])
        gate_s = sb("gate_s", [P, KD, S])
        hs = sb("hs", [P, KD, S])
        sample_sq = sb("sample_sq", [P, S])
        small = sb("small", [P, KD, S])
        last_cols = sb("last_cols", [P, 2, P])
        states_out = sb("states_out", [P, 2, P])
        sumsq = sb("sumsq", [P, R])
        rstd = sb("rstd", [P, R])

        b_adaT = vecT[:, 0:48]
        n1T, n2T = vecT[:, 48:56], vecT[:, 56:64]
        pscaleT = vecT[:, 64:66]
        sconvT = vecT[:, 66:75]
        cbT, lgT, lbT = vecT[:, 75:78], vecT[:, 78:81], vecT[:, 81:84]

        with ExitStack() as scope:
            xrow = sb("xrow", [P, KD, D], scope=scope)
            xsrow = sb("xsrow", [S, D], scope=scope)
            crow = sb("crow", [32, D], scope=scope)
            csig = sb("csig", [32, D], scope=scope)
            vrow = sb("vrow", [84, P], scope=scope)
            taprow = sb("taprow", [CK * CONV_C, P], scope=scope)
            st_pool = sb("st_pool", [S * PBUF, 256], scope=scope)
            st_conf = sb("st_conf", [S // 2 * (CK - 1), 2, 384], scope=scope)
            st_sconv = sb("st_sconv", [S * (SK - 1), 384], scope=scope)
        hhi = sb("hhi", [P, KD, N], F32R)
        hlo = sb("hlo", [P, KD, N], F32R)
        with ExitStack() as scope:
            with ExitStack() as heads:
                glu = sb("glu", [P, CONV_C, N], scope=heads)
                dc = sb("dc", [P, CONV_C, N], scope=heads)
                ada = sb("ada", [P, ADA_SLOTS, 2048], scope=heads)
            yc_hi = sb("yc_hi", [P, CONV_C, N], F32R, scope=scope)
            yc_lo = sb("yc_lo", [P, CONV_C, N], F32R, scope=scope)
            yab_hi = sb("yab_hi", [P, 5, N], F32R, scope=scope)
            yab_lo = sb("yab_lo", [P, 5, N], F32R, scope=scope)
        hid_hi = sb("hid_hi", [P, 2 * FG, N], F32R)
        hid_lo = sb("hid_lo", [P, 2 * FG, N], F32R)

        acc = ctx.enter_context(nc.psum_tensor("acc", [P, 2, 3, 512], F32))
        modps = ctx.enter_context(nc.psum_tensor("modps", [P, 512], F32))
        tps = ctx.enter_context(nc.psum_tensor("tps", [P, 512], F32))

        const_ready = sem("const_ready")
        crow_cleared = sem("crow_cleared")
        c_loaded = sem("c_loaded")
        vec_loaded = sem("vec_loaded")
        st_loaded = sem("st_loaded")
        xs_loaded = sem("xs_loaded")
        st_copied = sem("st_copied")
        pw_loaded = sem("pw_loaded")
        x_loaded = [sem(f"x_loaded{i}") for i in range(KD)]
        ada_loaded = [sem(f"ada_loaded{k}") for k in range(ADA_SLOTS)]
        w_loaded = [sem(f"w_loaded{s}") for s in range(2)]
        whi_ready = sem("whi_ready")
        wlo_ready = sem("wlo_ready")
        psum_full = sem("psum_full")
        freed_v = sem("freed_v")
        tps_full = sem("tps_full")
        tps_read = sem("tps_read")
        csig_ready = sem("csig_ready")
        halves_ready = sem("halves_ready")
        c_ready = sem("c_ready")
        sq_ready = sem("sq_ready")
        sq_added = sem("sq_added")
        xsq_ready = sem("xsq_ready")
        sq_used = sem("sq_used")
        ada_used = sem("ada_used")
        mod_rows = sem("mod_rows")
        mod_ready = sem("mod_ready")
        ms_ready = sem("ms_ready")
        root_ready = sem("root_ready")
        diag_ready = sem("diag_ready")
        rstd_ready = sem("rstd_ready")
        gains_ready = sem("gains_ready")
        hpre_ready = sem("hpre_ready")
        hhi_ready = sem("hhi_ready")
        hlo_ready = sem("hlo_ready")
        h_sample_ready = sem("h_sample_ready")
        sig_ready = sem("sig_ready")
        glu_ready = sem("glu_ready")
        conv_step = sem("conv_step")
        u_ready = sem("u_ready")
        pool_ready = sem("pool_ready")
        v_ready = sem("v_ready")
        yb_ready = sem("yb_ready")
        yhi_ready = sem("yhi_ready")
        ylo_ready = sem("ylo_ready")
        centred = sem("centred")
        ln_scaled = sem("ln_scaled")
        lsig_ready = sem("lsig_ready")
        silu_ready = sem("silu_ready")
        last_u = sem("last_u")
        last_v = sem("last_v")
        x_updated = sem("x_updated")
        relu_ready = sem("relu_ready")
        hid_hi_ready = sem("hid_hi_ready")
        hid_lo_ready = sem("hid_lo_ready")
        sumsq_ready = sem("sumsq_ready")
        out_ready = sem("out_ready")
        gain_loaded = sem("gain_loaded")
        y_stored = [sem(f"y_stored{i}") for i in range(3)]
        old_stored = sem("old_stored")
        new_stored = sem("new_stored")
        states_ready = sem("states_ready")
        order = sem("order")
        porder = sem("porder")

        def chunk_of(n):
            return acc[:, n % 2, :, :]

        def flat(ap):
            return ap[:, :, 0:TW]

        def tiled(ap):
            return ap.rearrange("p (t w) -> p t w", t=NT)

        def pair(ap):
            return ap.rearrange("p (t w) -> p t w", t=2)

        def rows_bank(i):
            return acc[:].rearrange("p a t w -> p (a t) w")[:, 2 * (i % 3):2 * (i % 3) + 2, :]

        def w_source(u):
            name, _ = UNITS[u]
            kind, c = name
            col0 = {"gg": GG0, "ga": GA0, "u": U0, "v": V0, "gc": GC0, "gb": GB0}
            if kind in col0:
                j = col0[kind] + c
                return w_in[0, :, j * P:(j + 1) * P].rearrange("(k p) n -> p k n", p=P)
            if kind == "p1":
                return w_out[0, 0:5 * P, c * P:(c + 1) * P].rearrange("(k p) n -> p k n", p=P)
            return w_out[0, 5 * P:8 * P, c * 256:(c + 1) * 256].rearrange("(k p) n -> p k n", p=P)

        def blocks_of(u):
            return BLOCKS[UNITS[u][0][0]]

        def sq_tile(d):
            return 0 if d == 0 else 1 + d % 2

        w1v = w_ff1[0].rearrange("(k p) n -> p k n", p=P)
        w2v = w_ff2[0].rearrange("(f p) n -> p f n", p=P)

        block = ctx.enter_context(nc.Block())

        @block.sync
        def _(sp):
            def load_w(u):
                if u >= 2:
                    sp.wait_ge(wlo_ready, u - 1)
                src = w_source(u)
                n = blocks_of(u) * P
                dst = wraw[:, u % 2, 0:n].rearrange("p (k n) -> p k n", k=src.shape[1])
                sp.dma_start(dst, src).then_inc(w_loaded[u % 2], 16)

            def load_ada(q):
                if q >= ADA_SLOTS:
                    sp.wait_ge(ada_used, q - ADA_SLOTS + 1)
                dst = ada[:, q % ADA_SLOTS, :]
                if q < KD:
                    for m in range(2):
                        sp.dma_start(dst.rearrange("p (k m n) -> p k m n", k=KD, m=2)[:, :, m, :],
                                     w_ada[0, :, m * D + q * P:m * D + (q + 1) * P].rearrange("(k p) n -> p k n", p=P)
                                     ).then_inc(ada_loaded[q % ADA_SLOTS], 16)
                else:
                    b, k = q // KD, q % KD
                    sp.dma_start(dst, w_ada[0, k * P:(k + 1) * P, b * 2048:(b + 1) * 2048]
                                 ).then_inc(ada_loaded[q % ADA_SLOTS], 16)

            for i in range(KD):
                sp.dma_start(xrow[:, i, :], x_prompt[0, i * P:(i + 1) * P, :]).then_inc(x_loaded[i], 16)
            rows = [(b_ada, 48), (norm1_g, 8), (norm2_g, 8), (pool_scale, 2), (sconv_w, 9),
                    (conf_b, 3), (conf_ln_g, 3), (conf_ln_b, 3)]
            at = 0
            for v, n in rows:
                v2 = (v.rearrange("l a n -> (l a n)") if len(v.shape) == 3 else v.rearrange("l n -> (l n)"))
                sp.dma_start(vrow[at:at + n, :], v2.rearrange("(c p) -> c p", p=P)).then_inc(vec_loaded, 16)
                at += n
            sp.dma_start(taprow[:], conf_w.rearrange("l a n -> (l a n)").rearrange("(c p) -> c p", p=P)
                          ).then_inc(vec_loaded, 16)
            load_ada(0)
            load_ada(1)
            load_w(0)
            load_w(1)
            for q in range(2, KD + ADA_SLOTS):
                load_ada(q)
            q = KD + ADA_SLOTS
            for u in range(2, U_FF):
                more = sum(n for v, n in ADA_AFTER.items() if v <= u - 2)
                load_w(u)
                while q < ADA and q < KD + ADA_SLOTS + more:
                    load_ada(q)
                    q += 1

            def load_ff(u, slot, src, k):
                sp.wait_ge(wlo_ready, u - 1)
                sp.dma_start(wraw[:, slot, :].rearrange("p (k n) -> p k n", k=k), src
                             ).then_inc(w_loaded[slot], 16)

            def load_up(u0, f0):
                for j in range(FG):
                    load_ff(u0 + j, (U_FF + j) % 2, w1v[:, :, bass.ds((f0 + j) * P, P)], KD)

            def load_down(u0, f0):
                for j in range(FG):
                    load_ff(u0 + j, (U_FF + j) % 2, w2v[:, bass.ds(f0, FG), j * 256:(j + 1) * 256], FG)

            load_up(U_FF, 0)
            with sp.Fori(0, NG - 1) as g:
                load_up(U_FF + 4 + g * 8, g * FG + FG)
                load_down(U_FF + 8 + g * 8, g * FG)
            load_down(U_FF + 60, (NG - 1) * FG)

            sp.wait_ge(wlo_ready, U_END - 1)
            sp.dma_start(wraw[:, (U_END - 2) % 2, :], final_g.rearrange("(a n) -> a n", a=1)
                         .broadcast_to([P, D])).then_inc(gain_loaded, 16)
            for i in range(KD + 1):
                sp.wait_ge(out_ready, i + 1)
                if i < KD:
                    sp.dma_start(y_prompt[0, i * P:(i + 1) * P, :], wk[i % 3][:, 0:D]
                                 ).then_inc(y_stored[i % 3], 16)
                else:
                    sp.dma_start(y_sample.rearrange("s a d -> (s a) d"), wk[i % 3][0:S, 0:D]
                                 ).then_inc(y_stored[i % 3], 16)
            for i in range(3):
                sp.wait_ge(y_stored[i], 16 * 3)

        @block.gpsimd
        def _(pool):
            nc.gpsimd.memset(crow[:], 0.0).then_inc(crow_cleared, 1)
            made = 0

            def const(ins):
                nonlocal made
                made += 1
                ins.then_inc(const_ready, 1)
                return made

            const(nc.gpsimd.memset(ones[:], 1.0))
            pool.wait_ge(const_ready, const(nc.gpsimd.memset(ident[:], 0.0)))
            const(nc.gpsimd.affine_select(out=ident[:], in_=ident[:], compare_op=ALU.not_equal, fill=1.0,
                                          base=0, pattern=[[-1, P]], channel_multiplier=1))
            const(nc.gpsimd.memset(pw[:], 0.0))
            const(nc.gpsimd.memset(last_cols[:], 0.0))
            const(nc.gpsimd.memset(sumsq[:], 1.0))
            for w in work:
                const(nc.gpsimd.memset(w[:, 0:PAD], 0.0))
            for g, w in enumerate(WINDOWS):
                half = slice(64 * (g % 2), 64 * (g % 2) + 64)
                pool.wait_ge(const_ready, const(nc.gpsimd.memset(head_rc[half, g // 2, :], 1.0 / w)))
                for t in range(w - 1):
                    const(nc.gpsimd.memset(head_rc[half, g // 2, t:t + 1], 1.0 / (t + 1)))

            pool.dma_start(st_pool[:], state_pool.rearrange("l b t n -> (l b t) n")).then_inc(st_loaded, 16)
            pool.dma_start(st_sconv[:], state_sconv.rearrange("l b t n -> (l b t) n")).then_inc(st_loaded, 16)
            conf_rows = state_conf.rearrange("l b t n -> (l b t) n")
            for i in range(2):
                pool.dma_start(st_conf[:, i, :], conf_rows[i * 120:(i + 1) * 120, :]).then_inc(st_loaded, 16)
            pool.wait_ge(const_ready, 4)
            for g in range(4):
                h = 64 * (g % 2)
                pool.dma_start(pw[h:h + 64, g // 2, h:h + 64], pool_w[0, g]).then_inc(pw_loaded, 16)

            def low(u, slot, n):
                pool.wait_ge(whi_ready, u + 1)
                a = wraw[:, slot, 0:n * P]
                b = whi[:, slot, 0:n, :].bitcast(F32).rearrange("p k n -> p (k n)")
                o = wlo[:, slot, 0:n, :].rearrange("p k n -> p (k n)")
                nc.gpsimd.tensor_tensor(o, a, b, ALU.subtract).then_inc(wlo_ready, 1)

            links = 0

            def link(ins):
                nonlocal links
                links += 1
                ins.then_inc(porder, 1)
                pool.wait_ge(porder, links)

            def sample_h(A, shift, k0, k1):
                n = k1 - k0
                xs = xT[:, k0:k1, T:N]
                h = hs[:, k0:k1, :]
                r = wk[0][:, T:N].unsqueeze(1).broadcast_to([P, n, S])
                link(nc.gpsimd.tensor_tensor(h, xs, r, ALU.mult))
                link(nc.gpsimd.tensor_tensor(h, h, A[:, k0:k1, 1:R], ALU.mult))
                link(nc.gpsimd.tensor_tensor(h, h, modT[:, shift + k0:shift + k1, 1:R], ALU.add))
                link(nc.gpsimd.tensor_copy(hhi[:, k0:k1, T:N], h))
                nc.gpsimd.tensor_tensor(hlo[:, k0:k1, T:N], h, hhi[:, k0:k1, T:N].bitcast(F32),
                                        ALU.subtract).then_inc(h_sample_ready, 1)

            pool.wait_ge(const_ready, made)
            low(0, 0, 8)
            low(1, 1, 8)
            pool.wait_ge(rstd_ready, 1)
            for k in range(KD):
                pool.wait_ge(gains_ready, k + 1)
                sample_h(A1, 0, k, k + 1)
            for u in range(2, U_FF + 2):
                low(u, u % 2, blocks_of(u) if u < U_FF else 8)
            pool.wait_ge(rstd_ready, 2)
            pool.wait_ge(gains_ready, KD + 1)
            sample_h(A2, 3 * KD, 0, KD)
            with pool.Fori(U_FF + 2, U_END, 2) as u:
                low(u, U_FF % 2, 8)
                low(u + 1, (U_FF + 1) % 2, 8)

        @block.scalar
        def _(act):
            act.wait_ge(crow_cleared, 1)
            act.dma_start(crow[0:1, :], c_prompt).then_inc(c_loaded, 16)
            act.dma_start(crow[1:R, :], c_sample).then_inc(c_loaded, 16)
            act.dma_start(xsrow[:], x_sample.rearrange("s a d -> (s a) d")).then_inc(xs_loaded, 16)

            def row_sum(i, rows, src):
                if i:
                    act.wait_ge(sumsq_ready, i)
                nc.scalar.activation(wk[1][rows, 0:D], src, ACT.Square, accum_out=sumsq[rows, i:i + 1]
                                     ).then_inc(sumsq_ready, 1)

            act.wait_ge(const_ready, 6)
            for i in range(KD):
                if i == 3:
                    act.wait_ge(c_loaded, 32)
                    nc.scalar.activation(csig[:], crow[:], ACT.Sigmoid).then_inc(csig_ready, 1)
                act.wait_ge(x_loaded[i], 16)
                row_sum(i, slice(0, P), xrow[:, i, :])
            act.wait_ge(xs_loaded, 16)
            row_sum(KD, slice(0, S), xsrow[:])

            def high(u, slot, n, nth, prev_chunk):
                act.wait_ge(w_loaded[slot], nth * 16)
                if prev_chunk is not None:
                    act.wait_ge(psum_full, prev_chunk + 1)
                nc.scalar.activation(whi[:, slot, 0:n, :].rearrange("p k n -> p (k n)"),
                                     wraw[:, slot, 0:n * P], ACT.Copy).then_inc(whi_ready, 1)

            def high_of(u):
                if u < U_FF:
                    n = blocks_of(u)
                else:
                    n = 8
                high(u, u % 2, n, u // 2 + 1, UNITS[u - 2][1] if u >= 2 else None)

            def root(n):
                act.wait_ge(ms_ready, n)
                nc.scalar.activation(rstd[:], rstd[:], ACT.Sqrt).then_inc(root_ready, 1)

            def spread_copy(n, m):
                act.wait_ge(psum_full, m + 1)
                nc.scalar.activation(tiled(wk[0]), flat(chunk_of(m)), ACT.Copy).then_inc(rstd_ready, 1)

            def squares(n, d, updated):
                act.wait_ge(freed_v, updated)
                if d >= 3:
                    act.wait_ge(sq_added, ADDED[n] + d - 2)
                nc.scalar.activation(wk[sq_tile(d)][:, 0:T], xT[:, d, 0:T], ACT.Square).then_inc(sq_ready, 1)

            def h_high(n, shift):
                for k in range(KD):
                    act.wait_ge(hpre_ready, n * KD + k + 1)
                    nc.scalar.activation(hhi[:, k, 0:T], wk[1 + k % 2][:, 0:T], ACT.Identity,
                                         bias=modT[:, shift + k, 0:1]).then_inc(hhi_ready, 1)

            root(1)
            m = CHUNK_AT["states"]
            act.wait_ge(psum_full, m + 1)
            nc.scalar.activation(dc[:, :, 0:256], chunk_of(m)[:, :, 0:256], ACT.Copy).then_inc(st_copied, 1)
            nc.scalar.activation(dc[:, 0:POOL_C, 256:376], chunk_of(m)[:, 0:POOL_C, 256:376], ACT.Copy
                                 ).then_inc(st_copied, 1)
            spread_copy(1, CHUNK_AT["norm1"])
            high_of(0)
            high_of(1)
            h_high(0, 0)


            def ya_high(c):
                n = CHUNK_AT[("ya", c)]
                act.wait_ge(psum_full, n + 1)
                nc.scalar.activation(tiled(yab_hi[:, c, :]), flat(chunk_of(n)), ACT.Copy,
                                     scale=pscaleT[:, c:c + 1]).then_inc(yhi_ready, 1)

            for u in range(U_FF):
                (kind, c), n = UNITS[u]
                ps = flat(chunk_of(n))
                if kind == "p2":
                    squares(3, 2 * c, FREED_V[CHUNK_AT[("p2", 2 * c)]])
                if kind == "p1" and c == 2:
                    for j in range(CONV_C):
                        act.wait_ge(centred, j + 1)
                        nc.scalar.activation(wk[j][:], dc[:, j, :], ACT.Square).then_inc(sq_ready, 1)
                if kind == "p1" and c == LN_ROOT:
                    root(2)
                if kind == "p1" and c == 5:
                    for j in range(CONV_C):
                        act.wait_ge(ln_scaled, j + 1)
                        if j == 2:
                            act.wait_ge(silu_ready, 1)
                        nc.scalar.activation(wk[1 + j % 2][:], dc[:, j, :], ACT.Sigmoid,
                                             bias=lbT[:, j:j + 1]).then_inc(lsig_ready, 1)
                high_of(u + 2)
                if kind == "gg":
                    if c:
                        act.wait_ge(glu_ready, c)
                    nc.scalar.activation(tiled(wk[2]), ps, ACT.Sigmoid).then_inc(sig_ready, 1)
                if kind == "gg" and c == 2:
                    act.dma_start(ns_pool[0, :, 0:PBUF - 1, :], state_pool[0, :, 1:PBUF, :]).then_inc(old_stored, 16)
                    act.dma_start(ns_sconv[0, :, 0:SK - 2, :], state_sconv[0, :, 1:SK - 1, :]).then_inc(old_stored, 16)
                    act.dma_start(ns_conf[0, :, 0:CK - 2, :], state_conf[0, :, 1:CK - 1, :]).then_inc(old_stored, 16)
                if kind == "u":
                    nc.scalar.activation(last_cols[:, 0, 23 * c:23 * c + 23],
                                         chunk_of(n)[:, 2, TW - 23:TW], ACT.Copy).then_inc(last_u, 1)
                    if c == 1:
                        act.wait_ge(pool_ready, 1)
                    nc.scalar.activation(tiled(wk[c]), ps, ACT.Copy).then_inc(u_ready, 1)
                    if c == 1:
                        ya_high(0)
                if kind == "v":
                    if c == 0:
                        act.wait_ge(pool_ready, 2)
                    else:
                        act.wait_ge(ylo_ready, POOL_C + c)
                    nc.scalar.activation(tiled(wk[0]), ps, ACT.Copy).then_inc(v_ready, 1)
                    if c == 0:
                        ya_high(1)
                if kind == "gb":
                    act.wait_ge(yb_ready, c + 1)
                    nc.scalar.activation(yab_hi[:, POOL_C + c, :], wk[0][:], ACT.Copy).then_inc(yhi_ready, 1)
                if kind == "p1" and c == 5:
                    act.wait_ge(states_ready, 1)
                    for j in range(POOL_C):
                        r, cols = 23 * j, slice(j * P, (j + 1) * P)
                        act.dma_start(np_pool[0, 0, :, cols], states_out[r:r + PBUF, 0, :]).then_inc(new_stored, 16)
                        act.dma_start(ns_pool[0, :, PBUF - 1, cols], states_out[r + PBUF:r + 23, 0, :]
                                      ).then_inc(new_stored, 16)
                    for j in range(CONV_C):
                        r, cols = 46 + 10 * j, slice(j * P, (j + 1) * P)
                        act.dma_start(np_sconv[0, 0, :, cols], states_out[r:r + 2, 0, :]).then_inc(new_stored, 16)
                        act.dma_start(ns_sconv[0, :, SK - 2, cols], states_out[r + 2:r + 10, 0, :]
                                      ).then_inc(new_stored, 16)
                        r = LASTC * j
                        act.dma_start(np_conf[0, 0, :, cols], states_out[r:r + CK - 1, 1, :]).then_inc(new_stored, 16)
                        act.dma_start(ns_conf[0, :, CK - 2, cols], states_out[r + CK - 1:r + LASTC, 1, :]
                                      ).then_inc(new_stored, 16)
                if kind == "p1" and c == 5:
                    for j in range(CONV_C):
                        act.wait_ge(silu_ready, j + 1)
                        nc.scalar.activation(yc_hi[:, j, :], dc[:, j, :], ACT.Copy).then_inc(yhi_ready, 1)
                if kind == "p2":
                    squares(3, 2 * c + 1, FREED_V[CHUNK_AT[("p2", 2 * c + 1)]])

            root(3)
            spread_copy(2, CHUNK_AT["norm2"])
            h_high(1, 3 * KD)

            def hidden(at, slot, j):
                act.wait_ge(psum_full, C_FF + at + 1)
                act.wait_ge(freed_v, V_FF + at)
                nc.scalar.activation(tiled(wk[0]), flat(acc[:, (C_FF + j) % 2, :, :]), ACT.Relu
                                     ).then_inc(relu_ready, 1)
                act.wait_ge(freed_v, V_FF + at + 1)
                nc.scalar.activation(hid_hi[:, slot + j, :], wk[1 + j % 2][:], ACT.Copy
                                     ).then_inc(hid_hi_ready, 1)

            def high_ff(j0, pairs, last):
                u = U_FF + j0 + 2
                high(u, u % 2, 8, u // 2 + 1 + pairs, C_FF + last)

            for j in range(FG):
                high_ff(j, 0, j)
                hidden(j, 0, j)

            def step(g, slot):
                for j in range(FG):
                    high_ff(4 + j, g * 4, g * 12 + 4 + j)
                    hidden(g * 12 + 4 + j, slot, j)
                for j in range(FG):
                    high_ff(8 + j, g * 4, g * 12 + 9 + 2 * j)

            with act.Fori(0, NG - 2, 2) as g:
                step(g, FG)
                step(g + 1, 0)
            step(NG - 2, FG)
            at = C_FIN - C_FF - KD
            act.wait_ge(hid_lo_ready, FF_C)
            for d in range(KD):
                if d in (1, 3):
                    high_ff(60 + d // 2, 0, at + d)
                squares(4, d, V_FF + at + d + 1)
            root(4)
            act.wait_ge(old_stored, 16 * 3)
            act.wait_ge(new_stored, 16 * (2 * POOL_C + 4 * CONV_C))

        @block.vector
        def _(dve):
            links = 0

            def link(ins):
                nonlocal links
                links += 1
                ins.then_inc(order, 1)
                dve.wait_ge(order, links)

            dve.wait_ge(const_ready, 3)
            pairs = ident[:].rearrange("p (m h r) -> p m h r", m=2, h=2)
            nc.vector.tensor_tensor(halves[:], pairs[:, :, 0, :], pairs[:, :, 1, :], ALU.add).then_inc(halves_ready, 1)
            for i in range(KD):
                n = CHUNK_AT[("x", i)]
                if i == 4:
                    dve.wait_ge(csig_ready, 1)
                    nc.vector.tensor_tensor(csig[:], crow[:], csig[:], ALU.mult).then_inc(c_ready, 1)
                dve.wait_ge(psum_full, n + 1)
                nc.vector.tensor_copy(xT[:, :, i * P:(i + 1) * P],
                                      chunk_of(n)[:, 0:2, :].rearrange("p a (b n) -> p (a b) n", n=P)
                                      ).then_inc(freed_v, 1)

            def mean_squares(n, src, width):
                for rows, cols in ((slice(0, P), slice(0, KD)), (slice(0, S), slice(KD, R))):
                    ins = nc.vector.tensor_scalar(rstd[rows, cols], src[rows, cols], 1.0 / width, EPS,
                                                  ALU.mult, ALU.add)
                    if cols.start == 0:
                        link(ins)
                    else:
                        ins.then_inc(ms_ready, 1)

            def diagonals(n):
                dve.wait_ge(root_ready, n)
                link(nc.vector.reciprocal(rstd[:], rstd[:]))
                link(nc.vector.tensor_scalar(wk[1][:, T:N], ident[:, 0:S], rstd[:, KD:R], None, ALU.mult))
                nc.vector.tensor_tensor(wk[1][:, 0:T].rearrange("p (i n) -> p i n", n=P),
                                        ident[:].unsqueeze(1).broadcast_to([P, KD, P]),
                                        rstd[:, 0:KD].unsqueeze(2).broadcast_to([P, KD, P]), ALU.mult
                                        ).then_inc(diag_ready, 1)

            dve.wait_ge(sumsq_ready, R)
            nc.vector.tensor_scalar(rstd[:], sumsq[:], 1.0 / D, EPS, ALU.mult, ALU.add).then_inc(ms_ready, 1)
            dve.wait_ge(tps_full, 1)
            nc.vector.tensor_copy(cT[:], tps[:, 192:448].rearrange("p (k r) -> p k r", k=KD)).then_inc(tps_read, 1)
            nc.vector.tensor_copy(vecT[:], tps[:, 0:84]).then_inc(tps_read, 1)
            nc.vector.tensor_copy(tapT[:], tps[:, 84:84 + CK * CONV_C]).then_inc(tps_read, 1)
            dve.wait_ge(tps_read, 3)
            diagonals(1)

            m = CHUNK_AT["states"]
            dve.wait_ge(psum_full, m + 1)
            dve.wait_ge(st_copied, 2)
            nc.vector.tensor_copy(xT[:, :, T:N], chunk_of(m)[:, 2, 376:376 + KD * S]
                                  .rearrange("p (k s) -> p k s", k=KD)).then_inc(freed_v, 1)

            def mod_to_rows(b):
                dve.wait_ge(ada_used, (b + 1) * KD)
                nc.vector.tensor_copy(wk[1][:, 0:512], modps[:]).then_inc(mod_rows, 1)

            def mod_finish(b):
                dve.wait_ge(tps_full, KD + 1 + b)
                src = tps[:].rearrange("p (q j r) -> p j q r", q=4, j=4)[:, :, :, 0:R]
                dst = modT[:, b * MC:(b + 1) * MC, :].rearrange("p (j q) r -> p j q r", q=4)
                bias = b_adaT[:, b * MC:(b + 1) * MC].rearrange("p (j q) -> p j q", q=4)
                for j in range(4):
                    ins = nc.vector.tensor_tensor(dst[:, j], src[:, j],
                                                  bias[:, j].unsqueeze(2).broadcast_to([P, 4, R]), ALU.add)
                    if j < 3:
                        ins.then_inc(order, 1)
                ins.then_inc(mod_ready, 1)
                nonlocal links
                links += 3
                dve.wait_ge(order, links)
                dve.wait_ge(mod_ready, b)

            def h_pre(nth, k, A):
                if k >= 2:
                    dve.wait_ge(hlo_ready, nth * KD + k - 1)
                nc.vector.scalar_tensor_tensor(wk[1 + k % 2][:, 0:T], xT[:, k, 0:T], A[:, k, 0:1],
                                               wk[0][:, 0:T], ALU.mult, ALU.mult).then_inc(hpre_ready, 1)

            def h_low(nth, k, shift):
                dve.wait_ge(hpre_ready, nth * KD + k + 1)
                dve.wait_ge(hhi_ready, nth * KD + k + 1)
                nc.vector.scalar_tensor_tensor(hlo[:, k, 0:T], wk[1 + k % 2][:, 0:T],
                                               modT[:, shift + k, 0:1], hhi[:, k, 0:T].bitcast(F32),
                                               ALU.add, ALU.subtract).then_inc(hlo_ready, 1)

            def cols_to_rows(k):
                dve.wait_ge(ada_used, k + 1)
                if k >= 2:
                    dve.wait_ge(tps_full, k)
                nc.vector.tensor_copy(states_out[:, k % 2, :], modps[:, 0:P]
                                      ).then_inc(mod_rows, 1)

            def cols_finish(k):
                dve.wait_ge(tps_full, 2 + k)
                for m in range(2):
                    at = 32 * m
                    j = m * KD + k
                    link(nc.vector.tensor_scalar(modT[:, j, :], tps[:, at:at + R], b_adaT[:, j:j + 1], None, ALU.add))
                nc.vector.tensor_scalar(A1[:, k, :], modT[:, KD + k, :], 1.0, n1T[:, k:k + 1], ALU.add, ALU.mult
                                        ).then_inc(gains_ready, 1)
                dve.wait_ge(gains_ready, k + 1)

            for step in range(KD + 2):
                if step < KD:
                    cols_to_rows(step)
                if 1 <= step <= KD:
                    cols_finish(step - 1)
                    if step == 1:
                        dve.wait_ge(rstd_ready, 1)
                    h_pre(0, step - 1, A1)
                if step >= 2:
                    h_low(0, step - 2, 0)

            st, past_prod = dc, wk[1]
            dve.wait_ge(hlo_ready, KD)
            def past(dst, ps, taps, k):
                prod = past_prod[:, 0:S * k].rearrange("p (b t) -> p b t", b=S)
                link(nc.vector.tensor_tensor(prod, ps.rearrange("p (b t) -> p b t", b=S),
                                             taps.unsqueeze(1).broadcast_to([P, S, k]), ALU.mult))
                link(nc.vector.tensor_reduce(dst, prod, AX_X, ALU.add))

            for c in range(CONV_C):
                conf_taps = tapT[:].rearrange("p (j c) -> p c j", c=CONV_C)[:, c, 0:CK - 1]
                past(past_conf[:, c, :], st[:, c, 0:S * (CK - 1)], conf_taps, CK - 1)
                taps = sconvT.rearrange("p (j c) -> p c j", c=CONV_C)[:, c, 0:SK - 1]
                past(past_sconv[:, c, :], st[:, c, 240:240 + S * (SK - 1)], taps, SK - 1)
            for g, w in enumerate(WINDOWS):
                half, c = slice(64 * (g % 2), 64 * (g % 2) + 64), g // 2
                rows = st[half, c, 256:256 + S * PBUF].rearrange("p (b t) -> p b t", b=S)
                ins = nc.vector.tensor_reduce(past_pool[half, c, :], rows[:, :, PBUF - (w - 1):PBUF], AX_X, ALU.add)
                link(ins)

            steps = [(c, s) for c in range(CONV_C) for s in range(CK + 1)]
            done = 0

            def convolve(count):
                nonlocal done
                for c, s in steps[done:done + count]:
                    if s == 0:
                        dve.wait_ge(glu_ready, c + 1)
                        ins = nc.vector.tensor_scalar(dc[:, c, :], glu[:, c, :], tapT[:, 3 * (CK - 1) + c:3 * (CK - 1) + c + 1],
                                                      cbT[:, c:c + 1], ALU.mult, ALU.add)
                    else:
                        dve.wait_ge(conv_step, done)
                        if s < CK:
                            tap = 3 * (CK - 1 - s) + c
                            ins = nc.vector.scalar_tensor_tensor(dc[:, c, s:T], glu[:, c, 0:T - s], tapT[:, tap:tap + 1],
                                                                 dc[:, c, s:T], ALU.mult, ALU.add)
                        else:
                            ins = nc.vector.tensor_tensor(dc[:, c, T:N], dc[:, c, T:N], past_conf[:, c, :], ALU.add)
                    ins.then_inc(conv_step, 1)
                    done += 1

            def pooled(c):
                dve.wait_ge(u_ready, c + 1)
                u, s2 = work[c], work[2]
                if c == 0:
                    s4 = work[1]
                else:
                    dve.wait_ge(psum_full, CHUNK_AT[("ya", 0)] + 1)
                    s4 = work[0]

                def twice(dst, src, w, lo):
                    link(nc.vector.tensor_tensor(dst[lo:P, PAD:PAD + T], src[lo:P, PAD:PAD + T],
                                                 src[lo:P, PAD - w:PAD - w + T], ALU.add))

                twice(s2, u, 1, 0)
                if c == 0:
                    twice(s4, s2, 2, 64)
                    low, high_ = s2, s4
                else:
                    twice(s4, s2, 2, 0)
                    twice(s2, s4, 4, 0)
                    twice(s4, s2, 8, 64)
                    low, high_ = s2, s4
                for hf, s in ((0, low), (1, high_)):
                    p, w = slice(64 * hf, 64 * hf + 64), WINDOWS[2 * c + hf]
                    link(nc.vector.tensor_tensor(s[p, PAD + T:], u[p, PAD + T:], past_pool[p, c, :], ALU.add))
                    link(nc.vector.tensor_tensor(s[p, PAD:2 * PAD], s[p, PAD:2 * PAD], head_rc[p, c, :], ALU.mult))
                    link(nc.vector.tensor_tensor(u[p, PAD:2 * PAD], s[p, PAD:2 * PAD], u[p, PAD:2 * PAD], ALU.subtract))
                    ins = nc.vector.scalar_tensor_tensor(u[p, 2 * PAD:], s[p, 2 * PAD:], 1.0 / w, u[p, 2 * PAD:],
                                                         ALU.mult, ALU.subtract)
                    if hf == 0:
                        link(ins)
                    else:
                        ins.then_inc(pool_ready, 1)

            def ya_low(c):
                n = CHUNK_AT[("ya", c)]
                dve.wait_ge(yhi_ready, c + 1)
                nc.vector.scalar_tensor_tensor(tiled(yab_lo[:, c, :]), flat(chunk_of(n)), pscaleT[:, c:c + 1],
                                               tiled(yab_hi[:, c, :].bitcast(F32)), ALU.mult, ALU.subtract
                                               ).then_inc(ylo_ready, 1)

            def residual(n, d, gate):
                ps = acc[:, n % 2, :, :]
                g1 = modT[:, gate + d, 0:1]
                w2 = T - 2 * TW
                nc.vector.scalar_tensor_tensor(pair(xT[:, d, 0:2 * TW]), ps[:, 0:2, 0:TW], g1,
                                               pair(xT[:, d, 0:2 * TW]), ALU.mult, ALU.add)
                nc.vector.scalar_tensor_tensor(xT[:, d, 2 * TW:T], ps[:, 2, 0:w2], g1,
                                               xT[:, d, 2 * TW:T], ALU.mult, ALU.add)
                nc.vector.tensor_copy(gate_s[:, d, :], ps[:, 2, w2:TW]).then_inc(freed_v, 1)

            def add_squares(n, d):
                dve.wait_ge(sq_ready, SQ[n] + d + 1)
                if d >= 2:
                    dve.wait_ge(sq_added, ADDED[n] + d - 1)
                w, tile = (N, wk[1]) if n == 2 else (T, wk[sq_tile(d)])
                nc.vector.tensor_tensor(wk[0][:, 0:w], wk[0][:, 0:w], tile[:, 0:w], ALU.add).then_inc(sq_added, 1)

            def residual_sample(gate, wait_copy, updated):
                dve.wait_ge(freed_v, wait_copy)
                nc.vector.tensor_tensor(small[:], gate_s[:], modT[:, gate:gate + KD, 1:R], ALU.mult
                                        ).then_inc(x_updated, 1)
                dve.wait_ge(x_updated, updated - 1)
                nc.vector.tensor_tensor(xT[:, :, T:N], xT[:, :, T:N], small[:], ALU.add).then_inc(x_updated, 1)

            def square_sample(updated):
                dve.wait_ge(x_updated, updated)
                link(nc.vector.tensor_tensor(small[:], xT[:, :, T:N], xT[:, :, T:N], ALU.mult))
                nc.vector.tensor_reduce(sample_sq[:], small[:].rearrange("p k s -> p s k"), AX_X, ALU.add
                                        ).then_inc(xsq_ready, 1)

            for u in range(U_FF):
                (kind, c), n = UNITS[u]
                ps = flat(chunk_of(n))
                if kind == "ga":
                    dve.wait_ge(psum_full, n + 1)
                    dve.wait_ge(sig_ready, c + 1)
                    nc.vector.tensor_tensor(last_cols[:, 1, LASTC * c:LASTC * c + LASTC],
                                            chunk_of(n)[:, 2, TW - LASTC:TW], wk[2][:, N - LASTC:N], ALU.mult
                                            ).then_inc(last_v, 1)
                    nc.vector.tensor_tensor(tiled(glu[:, c, :]), ps, tiled(wk[2]), ALU.mult).then_inc(glu_ready, 1)
                    if c == 2:
                        mod_to_rows(2)
                    convolve(14 if c < 2 else 7)
                if kind == "gg" and c == 1:
                    mod_to_rows(1)
                if kind == "gg" and c == 2:
                    mod_finish(1)
                if kind == "u":
                    if c == 0:
                        mod_finish(2)
                        nc.vector.scalar_tensor_tensor(A2[:], modT[:, 4 * KD:5 * KD, :], 1.0,
                                                       n2T.unsqueeze(2).broadcast_to([P, KD, R]),
                                                       ALU.add, ALU.mult).then_inc(gains_ready, 1)
                    pooled(c)
                    if c == 1:
                        ya_low(0)
                    convolve(4)
                if kind == "v":
                    if c == 0:
                        ya_low(1)
                    convolve(7)
                if kind == "gc":
                    dve.wait_ge(psum_full, n + 1)
                    dve.wait_ge(v_ready, c + 1)
                    if c == 0:
                        dve.wait_ge(psum_full, CHUNK_AT[("ya", 1)] + 1)
                    nc.vector.tensor_tensor(last_cols[:, 0, 46 + 10 * c:56 + 10 * c],
                                            chunk_of(n)[:, 2, TW - 10:TW], wk[0][:, N - 10:N], ALU.mult
                                            ).then_inc(last_v, 1)
                    nc.vector.tensor_tensor(tiled(wk[1]), ps, tiled(wk[0]), ALU.mult).then_inc(freed_v, 1)
                    dve.wait_ge(freed_v, FREED_V[n])
                    cv, out = wk[1], wk[2]
                    tap = [sconvT[:, 3 * j + c:3 * j + c + 1] for j in range(SK)]
                    link(nc.vector.tensor_scalar(out[:], cv[:], tap[2], None, ALU.mult))
                    for s in (1, 2):
                        link(nc.vector.scalar_tensor_tensor(out[:, s:T], cv[:, 0:T - s], tap[2 - s], out[:, s:T],
                                                            ALU.mult, ALU.add))
                    link(nc.vector.tensor_tensor(out[:, T:N], out[:, T:N], past_sconv[:, c, :], ALU.add))
                    convolve(5)
                if kind == "gb":
                    dve.wait_ge(psum_full, n + 1)
                    nc.vector.tensor_tensor(tiled(wk[0]), ps, tiled(wk[2]), ALU.mult).then_inc(yb_ready, 1)
                    dve.wait_ge(yb_ready, c + 1)
                    dve.wait_ge(yhi_ready, POOL_C + c + 1)
                    nc.vector.tensor_tensor(yab_lo[:, POOL_C + c, :], wk[0][:], yab_hi[:, POOL_C + c, :].bitcast(F32),
                                            ALU.subtract).then_inc(ylo_ready, 1)
                    convolve(6 if c < 2 else 200)
                if kind == "p1":
                    if c == 2:
                        m = CHUNK_AT["lnmean"]
                        dve.wait_ge(psum_full, m + 1)
                        for j in range(CONV_C):
                            nc.vector.scalar_tensor_tensor(tiled(dc[:, j, :]), flat(chunk_of(m)), -1.0 / 384,
                                                           tiled(dc[:, j, :]), ALU.mult, ALU.add).then_inc(centred, 1)
                    if c == LN_ROOT:
                        dve.wait_ge(sq_used, 1)
                        mean_squares(2, tps, CONV_C * P)
                        diagonals(2)
                    if c == 5:
                        m = CHUNK_AT["lnvar"]
                        dve.wait_ge(psum_full, m + 1)
                        dve.wait_ge(centred, CONV_C)
                        for j in range(CONV_C):
                            nc.vector.scalar_tensor_tensor(tiled(dc[:, j, :]), tiled(dc[:, j, :]), lgT[:, j:j + 1],
                                                           flat(chunk_of(m)), ALU.mult, ALU.mult
                                                           ).then_inc(ln_scaled, 1)
                        for j in range(CONV_C):
                            dve.wait_ge(ln_scaled, j + 1)
                            dve.wait_ge(lsig_ready, j + 1)
                            nc.vector.scalar_tensor_tensor(dc[:, j, :], dc[:, j, :], lbT[:, j:j + 1], wk[1 + j % 2][:],
                                                           ALU.add, ALU.mult).then_inc(silu_ready, 1)
                    if c == 6:
                        for j in range(CONV_C):
                            dve.wait_ge(silu_ready, j + 1)
                            dve.wait_ge(yhi_ready, 5 + j + 1)
                            nc.vector.tensor_tensor(yc_lo[:, j, :], dc[:, j, :], yc_hi[:, j, :].bitcast(F32),
                                                    ALU.subtract).then_inc(ylo_ready, 1)
                    dve.wait_ge(psum_full, n + 1)
                    residual(n, c, 2 * KD)
                    if c == 0:
                        dve.wait_ge(tps_full, KD + 4)
                        nc.vector.tensor_copy(states_out[:], tps[:, 0:2 * P].rearrange("p (a n) -> p a n", a=2)
                                              ).then_inc(states_ready, 1)
                    if c == 2:
                        add_squares(2, 1)
                    if c == 7:
                        residual_sample(2 * KD, FREED_V[n], 2)
                if kind == "p2":
                    for d in (2 * c, 2 * c + 1):
                        m = CHUNK_AT[("p2", d)]
                        if d >= 2:
                            add_squares(3, d - 1)
                        dve.wait_ge(psum_full, m + 1)
                        if d == 0:
                            dve.wait_ge(x_updated, 2)
                        residual(m, d, 2 * KD)
                    if c == 3:
                        residual_sample(2 * KD, V_FF, 4)

            square_sample(4)
            dve.wait_ge(sq_used, 2)
            mean_squares(3, tps, D)
            diagonals(3)
            dve.wait_ge(rstd_ready, 2)
            dve.wait_ge(gains_ready, KD + 1)
            for step in range(KD + 1):
                if step < KD:
                    h_pre(1, step, A2)
                if step:
                    h_low(1, step - 1, 3 * KD)

            def hidden(at, f, slot, j):
                dve.wait_ge(psum_full, C_FF + at + 1)
                dve.wait_ge(relu_ready, f + 1)
                q = wk[1 + j % 2]
                nc.vector.scalar_tensor_tensor(tiled(q), flat(acc[:, (C_FF + j) % 2, :, :]), 0.0, tiled(wk[0]),
                                               ALU.max, ALU.mult).then_inc(freed_v, 1)
                dve.wait_ge(freed_v, V_FF + at + 1)
                dve.wait_ge(hid_hi_ready, f + 1)
                nc.vector.tensor_tensor(hid_lo[:, slot + j, :], q[:], hid_hi[:, slot + j, :].bitcast(F32),
                                        ALU.subtract).then_inc(hid_lo_ready, 1)

            def down(at, updated, last=False):
                for d in range(KD):
                    if last and d >= 2:
                        add_squares(4, d - 1)
                    dve.wait_ge(psum_full, C_FF + at + d + 1)
                    if d == 0:
                        dve.wait_ge(x_updated, updated)
                    residual(C_FF + d, d, 5 * KD)
                residual_sample(5 * KD, V_FF + at + KD, updated + 2)

            for j in range(FG):
                hidden(j, j, 0, j)

            def step(g, slot):
                for j in range(FG):
                    hidden(g * 12 + 4 + j, g * FG + FG + j, slot, j)
                down(g * 12 + 8, g * 2 + 4)

            with dve.Fori(0, NG - 2, 2) as g:
                step(g, FG)
                step(g + 1, 0)
            step(NG - 2, FG)
            down(C_FIN - C_FF - KD, 2 * (NG - 1) + 4, True)

            square_sample(2 * NG + 4)
            dve.wait_ge(sq_used, 3)
            mean_squares(4, tps, D)
            dve.wait_ge(root_ready, 4)
            link(nc.vector.reciprocal(rstd[:], rstd[:]))
            dve.wait_ge(gain_loaded, 16)
            gain = wraw[:, (U_END - 2) % 2, :]
            for i in range(KD + 1):
                dve.wait_ge(psum_full, C_FIN + i + 1)
                if i >= 3:
                    dve.wait_ge(y_stored[i % 3], 16 * (i // 3))
                rows = slice(0, P if i < KD else S)
                nc.vector.scalar_tensor_tensor(pair(wk[i % 3][rows, 0:D]), rows_bank(i)[rows], rstd[rows, i:i + 1],
                                               pair(gain[rows]), ALU.mult, ALU.mult).then_inc(out_ready, 1)

        @block.tensor
        def _(pe):
            def freed(n):
                if n < 0:
                    return
                name, by = CHUNKS[n]
                if by == "V":
                    pe.wait_ge(freed_v, FREED_V[n])
                elif name == "norm1":
                    pe.wait_ge(rstd_ready, 1)
                elif name == "lnmean":
                    pe.wait_ge(centred, CONV_C)
                elif name == "lnvar":
                    pe.wait_ge(ln_scaled, CONV_C)
                elif name == "norm2":
                    pe.wait_ge(rstd_ready, 2)
                elif name[0] == "ya":
                    pe.wait_ge(ylo_ready, name[1] + 1)
                elif name[0] == "ga":
                    pe.wait_ge(glu_ready, name[1] + 1)
                elif name[0] == "gb":
                    pe.wait_ge(yb_ready, name[1] + 1)
                elif name[0] == "gg":
                    pe.wait_ge(sig_ready, name[1] + 1)
                elif name[0] == "u":
                    pe.wait_ge(u_ready, name[1] + 1)
                else:
                    pe.wait_ge(v_ready, name[1] + 1)

            def product(out, slot, blocks, hi, lo, ready=None):
                for i, (b, k) in enumerate(blocks):
                    if ready:
                        ready(k)
                    for w, x in ((whi, hi), (whi, lo), (wlo, hi)):
                        for t in range(NT):
                            last = nc.tensor.matmul(out[:, t, 0:TW], w[:, slot, b, :], x[:, k, t * TW:(t + 1) * TW],
                                                    start=(i == 0 and w is whi and x is hi),
                                                    stop=(i == len(blocks) - 1 and w is wlo))
                return last

            def products_of_two(u0, outs, nth, ahead=0, before=None):
                for step in range(KD + LAG + ahead):
                    if before:
                        before(step)
                    for j in range(2):
                        k = step - ahead - LAG * j
                        if not 0 <= k < KD:
                            continue
                        if k == 0:
                            pe.wait_ge(wlo_ready, u0 + j + 1)
                        for w, x in ((whi, hhi), (wlo, hhi), (whi, hlo)):
                            if j == 0 and w is whi:
                                pe.wait_ge(hhi_ready if x is hhi else hlo_ready, nth * KD + k + 1)
                            for t in range(NT):
                                last = nc.tensor.matmul(outs[j][:, t, 0:TW], w[:, (u0 + j) % 2, k, :],
                                                        x[:, k, t * TW:(t + 1) * TW],
                                                        start=(k == 0 and w is whi and x is hhi),
                                                        stop=(k == KD - 1 and x is hlo))
                        if k == KD - 1:
                            last.then_inc(psum_full, 1)

            def token_sums(rows, first, last):
                for i in range(KD):
                    ins = nc.tensor.matmul(tps[:, i:i + 1], rows[:, i * P:(i + 1) * P], ones[:, 0:1],
                                           start=(first and i == 0), stop=last, skip_group_check=True)
                return ins

            def sample_sums(rows, stop):
                return nc.tensor.matmul(tps[0:S, KD:R], rows, ones[:, 0:1], start=False, stop=stop,
                                        skip_group_check=True)

            def norm_sums(n):
                pe.wait_ge(ms_ready, n - 1)
                pe.wait_ge(sq_added, ADDED[n] + KD - 2)
                token_sums(wk[0], True, False)
                pe.wait_ge(sq_ready, SQ[n] + KD)
                token_sums(wk[sq_tile(KD - 1)], False, True)
                pe.wait_ge(xsq_ready, n - 2)
                sample_sums(sample_sq[:], True).then_inc(sq_used, 1)

            def spread(n, m):
                freed(m - 2)
                pe.wait_ge(diag_ready, n)
                for t in range(NT):
                    last = nc.tensor.matmul(chunk_of(m)[:, t, 0:TW], ones[:], wk[1][:, t * TW:(t + 1) * TW],
                                            start=True, stop=True)
                last.then_inc(psum_full, 1)

            pe.wait_ge(const_ready, 3)
            for i in range(KD):
                n = CHUNK_AT[("x", i)]
                pe.wait_ge(x_loaded[i], 16)
                freed(n - 2)
                for k in range(KD):
                    last = nc.tensor.transpose(chunk_of(n)[:, k // 4, (k % 4) * P:(k % 4 + 1) * P],
                                               xrow[:, i, k * P:(k + 1) * P], ident[:])
                last.then_inc(psum_full, 1)
            pe.wait_ge(vec_loaded, 16 * 9)
            nc.tensor.transpose(tps[:, 0:84], vrow[:], ident[0:84, 0:84])
            nc.tensor.transpose(tps[:, 84:84 + CK * CONV_C], taprow[:], ident[0:CK * CONV_C, 0:CK * CONV_C])
            pe.wait_ge(c_ready, 1)
            for k in range(KD):
                last = nc.tensor.transpose(tps[:, 192 + 32 * k:224 + 32 * k], csig[:, k * P:(k + 1) * P],
                                           ident[0:32, 0:32])
            last.then_inc(tps_full, 1)
            m = CHUNK_AT["states"]
            st = chunk_of(m)
            freed(m - 2)
            pe.wait_ge(st_loaded, 16 * 4)
            pe.wait_ge(xs_loaded, 16)
            for c in range(CONV_C):
                cols = slice(c * P, (c + 1) * P)
                for i in range(2):
                    nc.tensor.transpose(st[:, c, i * 120:(i + 1) * 120], st_conf[:, i, cols], ident[0:120, 0:120])
                nc.tensor.transpose(st[:, c, 240:256], st_sconv[:, cols], ident[0:16, 0:16])
                if c < POOL_C:
                    nc.tensor.transpose(st[:, c, 256:376], st_pool[:, cols], ident[0:120, 0:120])
            for k in range(KD):
                last = nc.tensor.transpose(st[:, 2, 376 + 8 * k:384 + 8 * k], xsrow[:, k * P:(k + 1) * P],
                                           ident[0:S, 0:S])
            last.then_inc(psum_full, 1)
            spread(1, CHUNK_AT["norm1"])

            def ada_ready(q):
                loads = sum(2 if p < KD else 1 for p in range(q % ADA_SLOTS, q + 1, ADA_SLOTS))
                pe.wait_ge(ada_loaded[q % ADA_SLOTS], 16 * loads)

            def modulate_cols(k):
                ada_ready(k)
                if k:
                    pe.wait_ge(mod_rows, k)
                src = ada[:, k % ADA_SLOTS, :].rearrange("p (k m n) -> p k m n", k=KD, m=2)
                for kk in range(0, KD, 2):
                    for m in range(2):
                        for odd in range(2):
                            j = 2 * m + odd
                            last = nc.tensor.matmul(modps[32 * j:32 * j + 32, 0:P],
                                                    cT[:, kk + odd, :], src[:, kk + odd, m, :],
                                                    start=(kk == 0), stop=(kk == KD - 2),
                                                    tile_position=(0, 32 * j), skip_group_check=True)
                last.then_inc(ada_used, 1)

            def transpose_cols(k):
                pe.wait_ge(mod_rows, k + 1)
                if k:
                    pe.wait_ge(gains_ready, k)
                nc.tensor.matmul(tps[:, 0:64], states_out[:, k % 2, :],
                                 halves[:].rearrange("p m r -> p (m r)"), start=True, stop=True
                                 ).then_inc(tps_full, 1)

            def modulate(q):
                b, k = q // KD, q % KD
                ada_ready(q)
                if k == 0:
                    pe.wait_ge(mod_rows, KD + b - 1)
                for j in range(4):
                    last = nc.tensor.matmul(modps[32 * j:32 * j + 32, :], cT[:, k, :],
                                            ada[:, q % ADA_SLOTS, j * 512:(j + 1) * 512],
                                            start=(k == 0), stop=(k == KD - 1), tile_position=(0, 32 * j),
                                            skip_group_check=True)
                last.then_inc(ada_used, 1)

            def mod_transpose(b):
                pe.wait_ge(mod_rows, KD + b)
                pe.wait_ge(gains_ready, KD) if b == 1 else pe.wait_ge(mod_ready, b - 1)
                for q in range(4):
                    last = nc.tensor.transpose(tps[:, q * P:(q + 1) * P], wk[1][:, q * P:(q + 1) * P], ident[:])
                last.then_inc(tps_full, 1)

            def next_cols(step):
                if step == 0:
                    pe.wait_ge(halves_ready, 1)
                    pe.wait_ge(tps_read, 3)
                if 1 <= step <= KD:
                    transpose_cols(step - 1)
                if step < KD:
                    modulate_cols(step)

            def cols_and_sample(step):
                if step:
                    next_cols(step)
                if 0 <= step - COLS_AHEAD < KD:
                    pe.wait_ge(h_sample_ready, step - COLS_AHEAD + 1)

            s = KD
            for u in range(U_FF):
                (kind, c), n = UNITS[u]
                ready = None
                if u:
                    pe.wait_ge(wlo_ready, u + 1)
                if kind == "p1":
                    if c == 0:
                        ready = lambda k: pe.wait_ge(ylo_ready, k + 1)
                    blocks, hi, lo = [(b, b) for b in range(5)], yab_hi, yab_lo
                elif kind != "p2":
                    blocks, hi, lo = [(b, b) for b in range(KD)], hhi, hlo
                if u == 0:
                    next_cols(0)
                    freed(n - 2)
                    freed(n - 1)
                    products_of_two(0, [chunk_of(n), chunk_of(n + 1)], 0, COLS_AHEAD, cols_and_sample)
                elif u == 1:
                    pass
                elif kind != "p2":
                    freed(n - 2)
                    product(chunk_of(n), u % 2, blocks, hi, lo, ready).then_inc(psum_full, 1)
                else:
                    if c == 0:
                        pe.wait_ge(ylo_ready, 8)
                    for d in (2 * c, 2 * c + 1):
                        m = CHUNK_AT[("p2", d)]
                        freed(m - 2)
                        product(chunk_of(m), u % 2, [(2 * b + d % 2, b) for b in range(CONV_C)], yc_hi, yc_lo
                                ).then_inc(psum_full, 1)
                for _ in range(ADA_AFTER.get(u, 0)):
                    modulate(s)
                    s += 1
                if kind == "ga" and c == 1:
                    mod_transpose(1)
                if kind == "u" and c == 0:
                    mod_transpose(2)
                pooled = {("u", 1): 0, ("v", 0): 1}.get((kind, c))
                if pooled is not None:
                    m = CHUNK_AT[("ya", pooled)]
                    freed(m - 2)
                    pe.wait_ge(pool_ready, pooled + 1)
                    pe.wait_ge(pw_loaded, 16 * 4)
                    for t in range(NT):
                        last = nc.tensor.matmul(chunk_of(m)[:, t, 0:TW], pw[:, pooled, :],
                                                wk[pooled][:, t * TW:(t + 1) * TW], start=True, stop=True)
                    last.then_inc(psum_full, 1)
                if kind == "gb" and c == 2:
                    pe.wait_ge(mod_ready, 2)
                    pe.wait_ge(last_u, 2)
                    pe.wait_ge(last_v, 2 * CONV_C)
                    for a in range(2):
                        last = nc.tensor.transpose(tps[:, a * P:(a + 1) * P], last_cols[:, a, :], ident[:])
                    last.then_inc(tps_full, 1)
                if kind == "p1" and c == 1:
                    m = CHUNK_AT["lnmean"]
                    freed(m - 2)
                    for j in range(CONV_C):
                        pe.wait_ge(conv_step, (j + 1) * (CK + 1))
                        for t in range(NT):
                            last = nc.tensor.matmul(chunk_of(m)[:, t, 0:TW], ones[:], dc[:, j, t * TW:(t + 1) * TW],
                                                    start=(j == 0), stop=(j == CONV_C - 1))
                    last.then_inc(psum_full, 1)
                if kind == "p1" and c == LN_ROOT - 1:
                    pe.wait_ge(states_ready, 1)
                    for j in (0, 2):
                        pe.wait_ge(sq_added, 1) if j == 0 else pe.wait_ge(sq_ready, CONV_C)
                        token_sums(wk[j], j == 0, j == 2)
                        last = sample_sums(wk[j][:, T:N], j == 2)
                    last.then_inc(sq_used, 1)
                if kind == "p1" and c == 4:
                    spread(2, CHUNK_AT["lnvar"])

            norm_sums(3)
            spread(3, CHUNK_AT["norm2"])

            def up(at, j0, pairs, first=0):
                for j in range(first, FG):
                    pe.wait_ge(wlo_ready, U_FF + j0 + j + 1 + pairs * 2)
                    freed_before(at + j)
                    product(acc[:, (C_FF + j) % 2, :, :], (U_FF + j) % 2, [(b, b) for b in range(KD)], hhi, hlo
                            ).then_inc(psum_full, 1)

            def freed_before(at):
                if isinstance(at, int) and at < 2:
                    freed(C_FF + at - 2)
                else:
                    pe.wait_ge(freed_v, V_FF - 1 + at)

            def down(at, j0, pairs, f, slot):
                pe.wait_ge(hid_lo_ready, f)
                for j in range(FG):
                    pe.wait_ge(wlo_ready, U_FF + j0 + j + 1 + pairs * 2)
                    for dd in range(2):
                        d = 2 * j + dd
                        freed_before(at + d)
                        product(acc[:, (C_FF + d) % 2, :, :], (U_FF + j) % 2,
                                [(2 * b + dd, slot + b) for b in range(FG)], hid_hi, hid_lo).then_inc(psum_full, 1)

            pe.wait_ge(h_sample_ready, KD + 1)
            freed_before(0)
            freed_before(1)
            products_of_two(U_FF, [chunk_of(C_FF), chunk_of(C_FF + 1)], 1)
            up(0, 0, 0, 2)

            def step(g, slot):
                up(g * 12 + 4, 4, g * 4)
                down(g * 12 + 8, 8, g * 4, g * FG + FG, FG - slot)

            with pe.Fori(0, NG - 2, 2) as g:
                step(g, FG)
                step(g + 1, 0)
            step(NG - 2, FG)
            down(C_FIN - C_FF - KD, 2 * FF_C - 4, 0, FF_C, FG)

            def rows_out(i):
                if i >= 3:
                    pe.wait_ge(out_ready, i - 2)
                rows = P if i < KD else S
                for k in range(KD):
                    last = nc.tensor.transpose(rows_bank(i)[0:rows, k // 4, (k % 4) * P:(k % 4 + 1) * P],
                                               xT[:, k, i * P:i * P + rows], ident[:])
                last.then_inc(psum_full, 1)

            pe.wait_ge(freed_v, V_FF + C_FIN - C_FF)
            rows_out(0)
            norm_sums(4)
            for i in range(1, KD + 1):
                rows_out(i)


_INS = ["x_prompt", "x_sample", "c_prompt", "c_sample", "state_pool", "state_sconv", "state_conf", "w_ada", "b_ada",
        "norm1_g", "norm2_g", "w_in", "pool_w", "pool_scale", "sconv_w", "conf_w", "conf_b", "conf_ln_g",
        "conf_ln_b", "w_out", "w_ff1", "w_ff2", "final_g"]
_OUTS = [(1, T, D), (S, 1, D), (1, 1, PBUF, 256), (1, 1, SK - 1, 384), (1, 1, CK - 1, 384),
         (1, S, PBUF, 256), (1, S, SK - 1, 384), (1, S, CK - 1, 384)]


def kernel(**inputs):
    import numpy as _np
    import concourse.bacc as _bacc
    from concourse import mybir as _mybir
    from concourse.bass_utils import run_bass_kernel_spmd as _run

    nc = _bacc.Bacc("TRN2", target_bir_lowering=False, num_devices=1)
    arrays, args = {}, []
    for name in _INS:
        a = _np.ascontiguousarray(inputs[name])
        arrays[f"in_{name}"] = a
        args.append(nc.dram_tensor(f"in_{name}", a.shape, _mybir.dt.from_np(a.dtype), kind="ExternalInput").ap())
    for i, shape in enumerate(_OUTS):
        args.append(nc.dram_tensor(f"out_{i}", shape, F32, kind="ExternalOutput").ap())
    decoder_trunk(nc, *args)
    r = _run(nc, [arrays], core_ids=[0])
    return tuple(r.results[0][f"out_{i}"] for i in range(len(_OUTS)))
```

```python
from contextlib import ExitStack

import concourse.bass as bass
from concourse import mybir

F32 = mybir.dt.float32
F32R = mybir.dt.float32r
ALU = mybir.AluOpType
ACT = mybir.ActivationFunctionType
AX_X = mybir.AxisListType.X

P = 128
D = 1024
T = 1024
S = 8
N = T + S
NT = 3
TW = N // NT
KD = D // P
R = 1 + S
EPS = 1e-6
POOL_C, CONV_C = 2, 3
WINDOWS = (2, 4, 8, 16)
PBUF = 15
SK = 3
CK = 31
FF_C = 32
FG = 4
NG = FF_C // FG
PAD = 16
MROUNDS = 3
MC = 6 * KD // MROUNDS
ADA_SLOTS = 5
LASTC = 38

U0, GB0, GC0, V0, GA0, GG0 = 0, 2, 5, 8, 11, 14


def plan():
    units, chunks = [], []

    def chunk(name, by):
        chunks.append((name, by))

    for i in range(KD):
        chunk(("x", i), "V")
    chunk("states", "V")
    chunk("norm1", "-")
    for c in range(CONV_C):
        units.append((("gg", c), len(chunks)))
        chunk(("gg", c), "-")
        units.append((("ga", c), len(chunks)))
        chunk(("ga", c), "-")
    for c in range(POOL_C):
        units.append((("u", c), len(chunks)))
        chunk(("u", c), "-")
        if c == 1:
            chunk(("ya", 0), "-")
    for c in range(CONV_C):
        units.append((("v", c), len(chunks)))
        chunk(("v", c), "-")
        if c == 0:
            chunk(("ya", 1), "-")
        units.append((("gc", c), len(chunks)))
        chunk(("gc", c), "V")
        units.append((("gb", c), len(chunks)))
        chunk(("gb", c), "-")
    for d in range(KD):
        units.append((("p1", d), len(chunks)))
        chunk(("p1", d), "V")
        if d == 1:
            chunk("lnmean", "-")
        if d == 4:
            chunk("lnvar", "-")
    for d in range(KD):
        if d % 2 == 1:
            units.append((("p2", d // 2), len(chunks)))
        chunk(("p2", d), "V")
    chunk("norm2", "-")
    return units, chunks


UNITS, CHUNKS = plan()
UNIT_AT = {name: i for i, (name, _) in enumerate(UNITS)}
CHUNK_AT = {name: i for i, (name, _) in enumerate(CHUNKS)}
U_FF = len(UNITS)
C_FF = len(CHUNKS)
FREED_V = [sum(by == "V" for _, by in CHUNKS[:i + 1]) for i in range(C_FF)]
V_FF = FREED_V[-1]
AT_LAST = FF_C + (NG - 1) * KD
SUB = (0, P, TW - P)
U_END = U_FF + 2 * FF_C
LN_ROOT = 4
BLOCKS = {"gg": 8, "ga": 8, "u": 8, "v": 8, "gc": 8, "gb": 8, "p1": 5, "p2": 6}
ADA = MROUNDS * KD
ADA_AFTER = {1: 4, 2: 4, 3: 3, 4: 3, 5: 2}
COLS_AHEAD = 3
WARM = (7, 12, 23)
LAG = 2
SQ = {2: 0, 3: CONV_C, 4: CONV_C + KD}
ADDED = {2: 0, 3: 1, 4: KD - 1}


def decoder_trunk(nc, x_prompt, x_sample, c_prompt, c_sample, state_pool, state_sconv, state_conf,
                  w_ada, b_ada, norm1_g, norm2_g, w_in, pool_w, pool_scale, sconv_w, conf_w,
                  conf_b, conf_ln_g, conf_ln_b, w_out, w_ff1, w_ff2, final_g,
                  y_prompt, y_sample, np_pool, np_sconv, np_conf, ns_pool, ns_sconv, ns_conf):
    ctx = ExitStack()

    def sb(name, shape, dt=F32, scope=ctx):
        return scope.enter_context(nc.sbuf_tensor(name, shape, dt))

    def sem(name):
        return ctx.enter_context(nc.semaphore(name))

    with ctx:
        xT = sb("xT", [P, KD, N])
        whi = sb("whi", [P, 2, 8, P], F32R)
        wlo = sb("wlo", [P, 2, 8, P], F32R)
        wraw = sb("wraw", [P, 2, 8 * P])
        work = [sb(f"work{i}", [P, PAD + N]) for i in range(3)]
        wk = [w[:, PAD:] for w in work]
        ident = sb("ident", [P, P])
        ones = sb("ones", [P, P])
        quarters = sb("quarters", [P, 32])
        modT = sb("modT", [P, 6 * KD, R])
        vecT = sb("vecT", [P, 84])
        tapT = sb("tapT", [P, CK * CONV_C])
        cT = sb("cT", [P, KD, 32])
        A1 = sb("A1", [P, KD, R])
        A2 = sb("A2", [P, KD, R])
        pw = sb("pw", [P, POOL_C, P])
        past_pool = sb("past_pool", [P, POOL_C, S])
        past_sconv = sb("past_sconv", [P, CONV_C, S])
        past_conf = sb("past_conf", [P, CONV_C, S])
        head_rc = sb("head_rc", [P, POOL_C, PAD])
        gate_s = sb("gate_s", [P, KD, S])
        hs = sb("hs", [P, KD, S])
        sample_sq = sb("sample_sq", [P, S])
        small = sb("small", [P, KD, S])
        last_cols = sb("last_cols", [P, 2, P])
        states_out = sb("states_out", [P, 2, P])
        sumsq = sb("sumsq", [P, R])
        rstd = sb("rstd", [P, R])

        b_adaT = vecT[:, 0:48]
        n1T, n2T = vecT[:, 48:56], vecT[:, 56:64]
        pscaleT = vecT[:, 64:66]
        sconvT = vecT[:, 66:75]
        cbT, lgT, lbT = vecT[:, 75:78], vecT[:, 78:81], vecT[:, 81:84]

        with ExitStack() as scope:
            xrow = sb("xrow", [P, KD, D], scope=scope)
            xsrow = sb("xsrow", [S, D], scope=scope)
            crow = sb("crow", [32, D], scope=scope)
            csig = sb("csig", [32, D], scope=scope)
            vrow = sb("vrow", [84, P], scope=scope)
            taprow = sb("taprow", [CK * CONV_C, P], scope=scope)
            st_pool = sb("st_pool", [S * PBUF, 256], scope=scope)
            st_conf = sb("st_conf", [S // 2 * (CK - 1), 2, 384], scope=scope)
            st_sconv = sb("st_sconv", [S * (SK - 1), 384], scope=scope)
        hhi = sb("hhi", [P, KD, N], F32R)
        hlo = sb("hlo", [P, KD, N], F32R)
        with ExitStack() as scope:
            with ExitStack() as heads:
                glu = sb("glu", [P, CONV_C, N], scope=heads)
                dc = sb("dc", [P, CONV_C, N], scope=heads)
                ada = sb("ada", [P, ADA_SLOTS, 2048], scope=heads)
            yc_hi = sb("yc_hi", [P, CONV_C, N], F32R, scope=scope)
            yc_lo = sb("yc_lo", [P, CONV_C, N], F32R, scope=scope)
            yab_hi = sb("yab_hi", [P, 5, N], F32R, scope=scope)
            yab_lo = sb("yab_lo", [P, 5, N], F32R, scope=scope)
        hid_hi = sb("hid_hi", [P, 2 * FG, N], F32R)
        hid_lo = sb("hid_lo", [P, 2 * FG, N], F32R)

        acc = ctx.enter_context(nc.psum_tensor("acc", [P, 2, 3, 512], F32))
        modps = ctx.enter_context(nc.psum_tensor("modps", [P, 512], F32))
        tps = ctx.enter_context(nc.psum_tensor("tps", [P, 512], F32))

        const_ready = sem("const_ready")
        crow_cleared = sem("crow_cleared")
        c_loaded = sem("c_loaded")
        vec_loaded = sem("vec_loaded")
        st_loaded = sem("st_loaded")
        xs_loaded = sem("xs_loaded")
        st_copied = sem("st_copied")
        pw_loaded = sem("pw_loaded")
        x_loaded = [sem(f"x_loaded{i}") for i in range(KD)]
        ada_loaded = [sem(f"ada_loaded{k}") for k in range(ADA_SLOTS)]
        w_loaded = [sem(f"w_loaded{s}") for s in range(2)]
        whi_ready = sem("whi_ready")
        wlo_ready = sem("wlo_ready")
        psum_full = sem("psum_full")
        freed_v = sem("freed_v")
        tps_full = sem("tps_full")
        tps_read = sem("tps_read")
        csig_ready = sem("csig_ready")
        quarters_ready = sem("quarters_ready")
        c_ready = sem("c_ready")
        sq_ready = sem("sq_ready")
        sq_added = sem("sq_added")
        xsq_ready = sem("xsq_ready")
        sq_used = sem("sq_used")
        ada_used = sem("ada_used")
        mod_rows = sem("mod_rows")
        mod_ready = sem("mod_ready")
        ms_ready = sem("ms_ready")
        root_ready = sem("root_ready")
        diag_ready = sem("diag_ready")
        spread_full = sem("spread_full")
        rstd_ready = sem("rstd_ready")
        gains_ready = sem("gains_ready")
        hpre_ready = sem("hpre_ready")
        hhi_ready = sem("hhi_ready")
        hlo_ready = sem("hlo_ready")
        h_sample_ready = sem("h_sample_ready")
        sig_ready = sem("sig_ready")
        glu_ready = sem("glu_ready")
        conv_step = sem("conv_step")
        u_ready = sem("u_ready")
        pool_ready = sem("pool_ready")
        v_ready = sem("v_ready")
        yb_ready = sem("yb_ready")
        yhi_ready = sem("yhi_ready")
        ylo_ready = sem("ylo_ready")
        dc_added = sem("dc_added")
        centred = sem("centred")
        ln_scaled = sem("ln_scaled")
        lsig_ready = sem("lsig_ready")
        silu_ready = sem("silu_ready")
        last_u = sem("last_u")
        last_v = sem("last_v")
        x_updated = sem("x_updated")
        relu_ready = sem("relu_ready")
        hid_hi_ready = sem("hid_hi_ready")
        hid_lo_ready = sem("hid_lo_ready")
        part_full = sem("part_full")
        part_read = sem("part_read")
        xs_updated = sem("xs_updated")
        rows_full = sem("rows_full")
        sumsq_ready = sem("sumsq_ready")
        out_ready = sem("out_ready")
        gain_loaded = sem("gain_loaded")
        y_stored = [sem(f"y_stored{i}") for i in range(2)]
        old_stored = sem("old_stored")
        new_stored = sem("new_stored")
        states_ready = sem("states_ready")
        order = sem("order")
        porder = sem("porder")

        def chunk_of(n):
            return acc[:, n % 2, :, :]

        def flat(ap):
            return ap[:, :, 0:TW]

        def tiled(ap):
            return ap.rearrange("p (t w) -> p t w", t=NT)

        def pair(ap):
            return ap.rearrange("p (t w) -> p t w", t=2)

        def last_bank(i):
            return acc[:, (C_FF + (i % 4) // 3) % 2, min(i % 4, 2), :]

        def rows_bank(i):
            return acc[:, (C_FF if i in (3 * NT - 3, 3 * NT - 1) else C_FF + 1) % 2, 0:2, :]

        def mod_part(k):
            return glu[:, k % 2, 0:2 * P]

        def square_of(i):
            return i // 3 * TW + SUB[i % 3]

        def sq_part(d):
            return wk[2][:, sq_tile(d) * TW:(sq_tile(d) + 1) * TW]

        def split_at(w, u):
            if isinstance(u, int) and u >= U_END - FG:
                h = hhi if w is whi else hlo
                return h[:, u - (U_END - FG), 0:D].rearrange("p (k n) -> p k n", n=P)
            return w[:, u % 2, :, :]

        def w_source(u):
            name, _ = UNITS[u]
            kind, c = name
            col0 = {"gg": GG0, "ga": GA0, "u": U0, "v": V0, "gc": GC0, "gb": GB0}
            if kind in col0:
                j = col0[kind] + c
                return w_in[0, :, j * P:(j + 1) * P].rearrange("(k p) n -> p k n", p=P)
            if kind == "p1":
                return w_out[0, 0:5 * P, c * P:(c + 1) * P].rearrange("(k p) n -> p k n", p=P)
            return w_out[0, 5 * P:8 * P, c * 256:(c + 1) * 256].rearrange("(k p) n -> p k n", p=P)

        def blocks_of(u):
            return BLOCKS[UNITS[u][0][0]]

        def sq_tile(d):
            return 0 if d == 0 else 1 + d % 2

        w1v = w_ff1[0].rearrange("(k p) n -> p k n", p=P)
        w2v = w_ff2[0].rearrange("(f p) n -> p f n", p=P)

        block = ctx.enter_context(nc.Block())

        @block.sync
        def _(sp):
            def load_w(u):
                if u >= 2:
                    sp.wait_ge(wlo_ready, u - 1)
                src = w_source(u)
                n = blocks_of(u) * P
                dst = wraw[:, u % 2, 0:n].rearrange("p (k n) -> p k n", k=src.shape[1])
                sp.dma_start(dst, src).then_inc(w_loaded[u % 2], 16)

            def load_ada(q):
                if q >= ADA_SLOTS:
                    sp.wait_ge(ada_used, q - ADA_SLOTS + 1)
                dst = ada[:, q % ADA_SLOTS, :]
                if q < KD:
                    for m in range(2):
                        sp.dma_start(dst.rearrange("p (k m n) -> p k m n", k=KD, m=2)[:, :, m, :],
                                     w_ada[0, :, m * D + q * P:m * D + (q + 1) * P].rearrange("(k p) n -> p k n", p=P)
                                     ).then_inc(ada_loaded[q % ADA_SLOTS], 16)
                else:
                    b, k = q // KD, q % KD
                    sp.dma_start(dst, w_ada[0, k * P:(k + 1) * P, b * 2048:(b + 1) * 2048]
                                 ).then_inc(ada_loaded[q % ADA_SLOTS], 16)

            for i in range(KD):
                sp.dma_start(xrow[:, i, :], x_prompt[0, i * P:(i + 1) * P, :]).then_inc(x_loaded[i], 16)
            rows = [(b_ada, 48), (norm1_g, 8), (norm2_g, 8), (pool_scale, 2), (sconv_w, 9),
                    (conf_b, 3), (conf_ln_g, 3), (conf_ln_b, 3)]
            at = 0
            for v, n in rows:
                v2 = (v.rearrange("l a n -> (l a n)") if len(v.shape) == 3 else v.rearrange("l n -> (l n)"))
                sp.dma_start(vrow[at:at + n, :], v2.rearrange("(c p) -> c p", p=P)).then_inc(vec_loaded, 16)
                at += n
            sp.dma_start(taprow[:], conf_w.rearrange("l a n -> (l a n)").rearrange("(c p) -> c p", p=P)
                          ).then_inc(vec_loaded, 16)
            load_ada(0)
            load_ada(1)
            load_w(0)
            load_ada(2)
            load_ada(3)
            load_w(1)
            for q in range(4, KD + ADA_SLOTS):
                load_ada(q)
            q = KD + ADA_SLOTS
            for u in range(2, U_FF):
                more = sum(n for v, n in ADA_AFTER.items() if v <= u - 2)
                load_w(u)
                while q < ADA and q < KD + ADA_SLOTS + more:
                    load_ada(q)
                    q += 1

            def load_ff(u, slot, src, k):
                sp.wait_ge(wlo_ready, u - 1)
                sp.dma_start(wraw[:, slot, :].rearrange("p (k n) -> p k n", k=k), src
                             ).then_inc(w_loaded[slot], 16)

            def load_up(u0, f0):
                for j in range(FG):
                    load_ff(u0 + j, (U_FF + j) % 2, w1v[:, :, bass.ds((f0 + j) * P, P)], KD)

            def load_down(u0, f0):
                for j in range(FG):
                    load_ff(u0 + j, (U_FF + j) % 2, w2v[:, bass.ds(f0, FG), j * 256:(j + 1) * 256], FG)

            load_up(U_FF, 0)
            with sp.Fori(0, NG - 1) as g:
                load_up(U_FF + 4 + g * 8, g * FG + FG)
                load_down(U_FF + 8 + g * 8, g * FG)
            load_down(U_FF + 60, (NG - 1) * FG)

            sp.wait_ge(wlo_ready, U_END - 1)
            sp.dma_start(wraw[:, (U_END - 2) % 2, :], final_g.rearrange("(a n) -> a n", a=1)
                         .broadcast_to([P, D])).then_inc(gain_loaded, 16)
            for i in range(3 * NT):
                sp.wait_ge(out_ready, i + 1)
                r0 = 0 if i % 3 < 2 else 2 * P - SUB[2]
                c0 = square_of(i) + r0
                rows = min(P - r0, T - c0)
                sp.dma_start(y_prompt[0, c0:c0 + rows, :], wk[i % 2][r0:r0 + rows, 0:D]
                             ).then_inc(y_stored[i % 2], 16)
            sp.dma_start(y_sample.rearrange("s a d -> (s a) d"), wk[0][P - S:P, 0:D]).then_inc(y_stored[0], 16)
            sp.wait_ge(y_stored[0], 16 * 6)
            sp.wait_ge(y_stored[1], 16 * 4)

        @block.gpsimd
        def _(pool):
            nc.gpsimd.memset(crow[:], 0.0).then_inc(crow_cleared, 1)
            made = 0

            def const(ins):
                nonlocal made
                made += 1
                ins.then_inc(const_ready, 1)
                return made

            const(nc.gpsimd.memset(ones[:], 1.0))
            pool.wait_ge(const_ready, const(nc.gpsimd.memset(ident[:], 0.0)))
            const(nc.gpsimd.affine_select(out=ident[:], in_=ident[:], compare_op=ALU.not_equal, fill=1.0,
                                          base=0, pattern=[[-1, P]], channel_multiplier=1))
            const(nc.gpsimd.memset(pw[:], 0.0))
            const(nc.gpsimd.memset(last_cols[:], 0.0))
            const(nc.gpsimd.memset(sumsq[:], 1.0))
            for w in work:
                const(nc.gpsimd.memset(w[:, 0:PAD], 0.0))
            for g, w in enumerate(WINDOWS):
                half = slice(64 * (g % 2), 64 * (g % 2) + 64)
                pool.wait_ge(const_ready, const(nc.gpsimd.memset(head_rc[half, g // 2, :], 1.0 / w)))
                for t in range(w - 1):
                    const(nc.gpsimd.memset(head_rc[half, g // 2, t:t + 1], 1.0 / (t + 1)))

            pool.dma_start(st_pool[:], state_pool.rearrange("l b t n -> (l b t) n")).then_inc(st_loaded, 16)
            pool.dma_start(st_sconv[:], state_sconv.rearrange("l b t n -> (l b t) n")).then_inc(st_loaded, 16)
            conf_rows = state_conf.rearrange("l b t n -> (l b t) n")
            for i in range(2):
                pool.dma_start(st_conf[:, i, :], conf_rows[i * 120:(i + 1) * 120, :]).then_inc(st_loaded, 16)
            pool.wait_ge(const_ready, 4)
            for g in range(4):
                h = 64 * (g % 2)
                pool.dma_start(pw[h:h + 64, g // 2, h:h + 64], pool_w[0, g]).then_inc(pw_loaded, 16)

            def low(u, slot, n):
                pool.wait_ge(whi_ready, u + 1)
                a = wraw[:, slot, 0:n * P]
                b = whi[:, slot, 0:n, :].bitcast(F32).rearrange("p k n -> p (k n)")
                o = wlo[:, slot, 0:n, :].rearrange("p k n -> p (k n)")
                nc.gpsimd.tensor_tensor(o, a, b, ALU.subtract).then_inc(wlo_ready, 1)

            links = 0

            def link(ins):
                nonlocal links
                links += 1
                ins.then_inc(porder, 1)
                pool.wait_ge(porder, links)

            def sample_h(A, shift, k0, k1):
                n = k1 - k0
                xs = xT[:, k0:k1, T:N]
                h = hs[:, k0:k1, :]
                r = wk[0][:, T:N].unsqueeze(1).broadcast_to([P, n, S])
                link(nc.gpsimd.tensor_tensor(h, xs, r, ALU.mult))
                link(nc.gpsimd.tensor_tensor(h, h, A[:, k0:k1, 1:R], ALU.mult))
                link(nc.gpsimd.tensor_tensor(h, h, modT[:, shift + k0:shift + k1, 1:R], ALU.add))
                link(nc.gpsimd.tensor_copy(hhi[:, k0:k1, T:N], h))
                nc.gpsimd.tensor_tensor(hlo[:, k0:k1, T:N], h, hhi[:, k0:k1, T:N].bitcast(F32),
                                        ALU.subtract).then_inc(h_sample_ready, 1)

            pool.wait_ge(const_ready, made)
            low(0, 0, 8)
            pool.wait_ge(rstd_ready, NT)
            for k in range(KD):
                if k == LAG:
                    low(1, 1, 8)
                pool.wait_ge(gains_ready, k + 1)
                sample_h(A1, 0, k, k + 1)
            for u in range(2, U_FF + 2):
                low(u, u % 2, blocks_of(u) if u < U_FF else 8)
            pool.wait_ge(rstd_ready, 2 * NT)
            pool.wait_ge(gains_ready, KD + 1)
            sample_h(A2, 3 * KD, 0, KD)
            with pool.Fori(U_FF + 2, U_END - FG, 2) as u:
                low(u, U_FF % 2, 8)
                low(u + 1, (U_FF + 1) % 2, 8)
            for u in range(U_END - FG, U_END):
                pool.wait_ge(whi_ready, u + 1)
                nc.gpsimd.tensor_tensor(split_at(wlo, u), wraw[:, u % 2, :].rearrange("p (k n) -> p k n", n=P),
                                        split_at(whi, u).bitcast(F32), ALU.subtract).then_inc(wlo_ready, 1)

        @block.scalar
        def _(act):
            act.wait_ge(crow_cleared, 1)
            act.dma_start(crow[0:1, :], c_prompt).then_inc(c_loaded, 16)
            act.dma_start(crow[1:R, :], c_sample).then_inc(c_loaded, 16)
            act.dma_start(xsrow[:], x_sample.rearrange("s a d -> (s a) d")).then_inc(xs_loaded, 16)

            def row_sum(i, rows, src):
                if i:
                    act.wait_ge(sumsq_ready, i)
                nc.scalar.activation(wk[1][rows, 0:D], src, ACT.Square, accum_out=sumsq[rows, i:i + 1]
                                     ).then_inc(sumsq_ready, 1)

            act.wait_ge(const_ready, 6)
            for i in range(KD):
                if i == 3:
                    act.wait_ge(c_loaded, 32)
                    nc.scalar.activation(csig[:], crow[:], ACT.Sigmoid).then_inc(csig_ready, 1)
                act.wait_ge(x_loaded[i], 16)
                row_sum(i, slice(0, P), xrow[:, i, :])
            act.wait_ge(xs_loaded, 16)
            row_sum(KD, slice(0, S), xsrow[:])

            def high(u, slot, n, nth, prev_chunk):
                act.wait_ge(w_loaded[slot], nth * 16)
                if prev_chunk is not None:
                    act.wait_ge(psum_full, prev_chunk + 1)
                nc.scalar.activation(whi[:, slot, 0:n, :].rearrange("p k n -> p (k n)"),
                                     wraw[:, slot, 0:n * P], ACT.Copy).then_inc(whi_ready, 1)

            def high_of(u):
                if u < U_FF:
                    n = blocks_of(u)
                else:
                    n = 8
                high(u, u % 2, n, u // 2 + 1, UNITS[u - 2][1] if u >= 2 else None)

            def root(n):
                act.wait_ge(ms_ready, n)
                nc.scalar.activation(rstd[:], rstd[:], ACT.Sqrt).then_inc(root_ready, 1)

            def spread_copy(n, m):
                for t in range(NT):
                    if t < NT - 1:
                        act.wait_ge(spread_full, (NT - 1) * (n - 1) + t + 1)
                    else:
                        act.wait_ge(psum_full, m + 1)
                    nc.scalar.activation(wk[0][:, t * TW:(t + 1) * TW], chunk_of(m)[:, t, 0:TW], ACT.Copy
                                         ).then_inc(rstd_ready, 1)

            def squares(n, d, updated):
                act.wait_ge(freed_v, updated)
                if d >= 3:
                    act.wait_ge(sq_added, ADDED[n] + d - 2)
                nc.scalar.activation(wk[sq_tile(d)][:, 0:T], xT[:, d, 0:T], ACT.Square).then_inc(sq_ready, 1)

            def h_high(n, shift):
                for k in range(KD):
                    if n == 0 and k == LAG:
                        high_of(1)
                    act.wait_ge(hpre_ready, n * KD + k + 1)
                    nc.scalar.activation(hhi[:, k, 0:T], wk[1 + k % 2][:, 0:T], ACT.Identity,
                                         bias=modT[:, shift + k, 0:1]).then_inc(hhi_ready, 1)

            root(1)
            m = CHUNK_AT["states"]
            act.wait_ge(psum_full, m + 1)
            nc.scalar.activation(dc[:, :, 0:256], chunk_of(m)[:, :, 0:256], ACT.Copy).then_inc(st_copied, 1)
            nc.scalar.activation(dc[:, 0:POOL_C, 256:376], chunk_of(m)[:, 0:POOL_C, 256:376], ACT.Copy
                                 ).then_inc(st_copied, 1)
            spread_copy(1, CHUNK_AT["norm1"])
            high_of(0)
            h_high(0, 0)

            def ya_high(c):
                n = CHUNK_AT[("ya", c)]
                act.wait_ge(psum_full, n + 1)
                nc.scalar.activation(tiled(yab_hi[:, c, :]), flat(chunk_of(n)), ACT.Copy,
                                     scale=pscaleT[:, c:c + 1]).then_inc(yhi_ready, 1)

            for u in range(U_FF):
                (kind, c), n = UNITS[u]
                ps = flat(chunk_of(n))
                if kind == "p2":
                    squares(3, 2 * c, FREED_V[CHUNK_AT[("p2", 2 * c)]])
                if kind == "p1" and c == 2:
                    for j in range(CONV_C):
                        act.wait_ge(centred, j + 1)
                        nc.scalar.activation(wk[j][:], dc[:, j, :], ACT.Square).then_inc(sq_ready, 1)
                if kind == "p1" and c == LN_ROOT:
                    root(2)
                if kind == "p1" and c == 5:
                    for j in range(CONV_C):
                        act.wait_ge(ln_scaled, j + 1)
                        if j == 2:
                            act.wait_ge(silu_ready, 1)
                        nc.scalar.activation(wk[1 + j % 2][:], dc[:, j, :], ACT.Sigmoid,
                                             bias=lbT[:, j:j + 1]).then_inc(lsig_ready, 1)
                high_of(u + 2)
                if kind == "gg":
                    if c:
                        act.wait_ge(glu_ready, c)
                    nc.scalar.activation(tiled(wk[2]), ps, ACT.Sigmoid).then_inc(sig_ready, 1)
                if kind == "gg" and c == 2:
                    act.dma_start(ns_pool[0, :, 0:PBUF - 1, :], state_pool[0, :, 1:PBUF, :]).then_inc(old_stored, 16)
                    act.dma_start(ns_sconv[0, :, 0:SK - 2, :], state_sconv[0, :, 1:SK - 1, :]).then_inc(old_stored, 16)
                    act.dma_start(ns_conf[0, :, 0:CK - 2, :], state_conf[0, :, 1:CK - 1, :]).then_inc(old_stored, 16)
                if kind == "u":
                    nc.scalar.activation(last_cols[:, 0, 23 * c:23 * c + 23],
                                         chunk_of(n)[:, 2, TW - 23:TW], ACT.Copy).then_inc(last_u, 1)
                    if c == 1:
                        act.wait_ge(pool_ready, 1)
                    nc.scalar.activation(tiled(wk[c]), ps, ACT.Copy).then_inc(u_ready, 1)
                    if c == 1:
                        ya_high(0)
                if kind == "v":
                    if c == 0:
                        act.wait_ge(pool_ready, 2)
                    else:
                        act.wait_ge(ylo_ready, POOL_C + c)
                    nc.scalar.activation(tiled(wk[0]), ps, ACT.Copy).then_inc(v_ready, 1)
                    if c == 0:
                        ya_high(1)
                if kind == "gb":
                    act.wait_ge(yb_ready, c + 1)
                    nc.scalar.activation(yab_hi[:, POOL_C + c, :], wk[0][:], ACT.Copy).then_inc(yhi_ready, 1)
                if kind == "p1" and c == 5:
                    act.wait_ge(states_ready, 1)
                    for j in range(POOL_C):
                        r, cols = 23 * j, slice(j * P, (j + 1) * P)
                        act.dma_start(np_pool[0, 0, :, cols], states_out[r:r + PBUF, 0, :]).then_inc(new_stored, 16)
                        act.dma_start(ns_pool[0, :, PBUF - 1, cols], states_out[r + PBUF:r + 23, 0, :]
                                      ).then_inc(new_stored, 16)
                    for j in range(CONV_C):
                        r, cols = 46 + 10 * j, slice(j * P, (j + 1) * P)
                        act.dma_start(np_sconv[0, 0, :, cols], states_out[r:r + 2, 0, :]).then_inc(new_stored, 16)
                        act.dma_start(ns_sconv[0, :, SK - 2, cols], states_out[r + 2:r + 10, 0, :]
                                      ).then_inc(new_stored, 16)
                        r = LASTC * j
                        act.dma_start(np_conf[0, 0, :, cols], states_out[r:r + CK - 1, 1, :]).then_inc(new_stored, 16)
                        act.dma_start(ns_conf[0, :, CK - 2, cols], states_out[r + CK - 1:r + LASTC, 1, :]
                                      ).then_inc(new_stored, 16)
                if kind == "p1" and c == 5:
                    for j in range(CONV_C):
                        act.wait_ge(silu_ready, j + 1)
                        nc.scalar.activation(yc_hi[:, j, :], dc[:, j, :], ACT.Copy).then_inc(yhi_ready, 1)
                if kind == "p2":
                    squares(3, 2 * c + 1, FREED_V[CHUNK_AT[("p2", 2 * c + 1)]])

            root(3)
            spread_copy(3, CHUNK_AT["norm2"])
            h_high(1, 3 * KD)

            def hidden(at, slot, j):
                act.wait_ge(psum_full, C_FF + at + 1)
                act.wait_ge(freed_v, V_FF + at)
                nc.scalar.activation(tiled(wk[0]), flat(acc[:, (C_FF + j) % 2, :, :]), ACT.Relu
                                     ).then_inc(relu_ready, 1)
                act.wait_ge(freed_v, V_FF + at + 1)
                nc.scalar.activation(hid_hi[:, slot + j, :], wk[1 + j % 2][:], ACT.Copy
                                     ).then_inc(hid_hi_ready, 1)

            def high_ff(j0, pairs, last):
                u = U_FF + j0 + 2
                high(u, u % 2, 8, u // 2 + 1 + pairs, C_FF + last)

            for j in range(FG):
                high_ff(j, 0, j)
                hidden(j, 0, j)

            def step(g, slot, highs=FG):
                for j in range(FG):
                    high_ff(4 + j, g * 4, g * 12 + 4 + j)
                    hidden(g * 12 + 4 + j, slot, j)
                for j in range(highs):
                    high_ff(8 + j, g * 4, g * 12 + 9 + 2 * j)

            with act.Fori(0, NG - 2, 2) as g:
                step(g, FG)
                step(g + 1, 0)
            step(NG - 2, FG, 2)
            act.wait_ge(psum_full, C_FF + AT_LAST - KD)
            for u in range(U_END - FG, U_END):
                act.wait_ge(w_loaded[u % 2], 16 * (u // 2 + 1))
                nc.scalar.activation(split_at(whi, u), wraw[:, u % 2, :].rearrange("p (k n) -> p k n", n=P),
                                     ACT.Copy).then_inc(whi_ready, 1)

            def root_of_tile(t):
                act.wait_ge(ms_ready, 4 + t)
                nc.scalar.activation(rstd[:, 3 * t:3 * t + 3], rstd[:, 3 * t:3 * t + 3], ACT.Sqrt
                                     ).then_inc(root_ready, 1)

            act.wait_ge(hid_lo_ready, FF_C)
            for t in range(NT):
                for d in range(KD):
                    if t == NT - 1:
                        act.wait_ge(xs_updated, d + 1)
                    else:
                        act.wait_ge(part_read, t * KD + d + 1)
                    if d >= 3:
                        act.wait_ge(sq_added, ADDED[4] + t * (KD - 2) + d - 2)
                    elif t:
                        act.wait_ge(sq_used, 2 + t)
                    nc.scalar.activation(sq_part(d), xT[:, d, t * TW:(t + 1) * TW], ACT.Square).then_inc(sq_ready, 1)
                    if t and d == 1:
                        root_of_tile(t - 1)
            root_of_tile(NT - 1)
            act.wait_ge(old_stored, 16 * 3)
            act.wait_ge(new_stored, 16 * (2 * POOL_C + 4 * CONV_C))

        @block.vector
        def _(dve):
            links = 0

            def link(ins):
                nonlocal links
                links += 1
                ins.then_inc(order, 1)
                dve.wait_ge(order, links)

            dve.wait_ge(const_ready, 3)
            nc.vector.tensor_reduce(quarters[:], ident[:].rearrange("p (q r) -> p r q", q=4), AX_X, ALU.add
                                    ).then_inc(quarters_ready, 1)
            for i in range(KD):
                n = CHUNK_AT[("x", i)]
                if i == 4:
                    dve.wait_ge(csig_ready, 1)
                    nc.vector.tensor_tensor(csig[:], crow[:], csig[:], ALU.mult).then_inc(c_ready, 1)
                dve.wait_ge(psum_full, n + 1)
                nc.vector.tensor_copy(xT[:, :, i * P:(i + 1) * P],
                                      chunk_of(n)[:, 0:2, :].rearrange("p a (b n) -> p (a b) n", n=P)
                                      ).then_inc(freed_v, 1)

            def mean_squares(n, src, width):
                for rows, cols in ((slice(0, P), slice(0, KD)), (slice(0, S), slice(KD, R))):
                    ins = nc.vector.tensor_scalar(rstd[rows, cols], src[rows, cols], 1.0 / width, EPS,
                                                  ALU.mult, ALU.add)
                    if cols.start == 0:
                        link(ins)
                    else:
                        ins.then_inc(ms_ready, 1)

            def diagonals(n):
                dve.wait_ge(root_ready, n)
                link(nc.vector.reciprocal(rstd[:], rstd[:]))
                link(nc.vector.tensor_scalar(wk[1][:, T:N], ident[:, 0:S], rstd[:, KD:R], None, ALU.mult))
                for i0, i1 in ((0, 3), (3, 6), (6, KD)):
                    nc.vector.tensor_tensor(wk[1][:, i0 * P:i1 * P].rearrange("p (i n) -> p i n", n=P),
                                            ident[:].unsqueeze(1).broadcast_to([P, i1 - i0, P]),
                                            rstd[:, i0:i1].unsqueeze(2).broadcast_to([P, i1 - i0, P]), ALU.mult
                                            ).then_inc(diag_ready, 1)

            dve.wait_ge(sumsq_ready, R)
            nc.vector.tensor_scalar(rstd[:], sumsq[:], 1.0 / D, EPS, ALU.mult, ALU.add).then_inc(ms_ready, 1)
            dve.wait_ge(tps_full, 1)
            nc.vector.tensor_copy(cT[:], tps[:, 192:448].rearrange("p (k r) -> p k r", k=KD)).then_inc(tps_read, 1)
            nc.vector.tensor_copy(vecT[:], tps[:, 0:84]).then_inc(tps_read, 1)
            nc.vector.tensor_copy(tapT[:], tps[:, 84:84 + CK * CONV_C]).then_inc(tps_read, 1)
            dve.wait_ge(tps_read, 3)
            diagonals(1)

            m = CHUNK_AT["states"]
            dve.wait_ge(psum_full, m + 1)
            dve.wait_ge(st_copied, 2)
            nc.vector.tensor_copy(xT[:, :, T:N], chunk_of(m)[:, 2, 376:376 + KD * S]
                                  .rearrange("p (k s) -> p k s", k=KD)).then_inc(freed_v, 1)

            def mod_to_rows(b):
                dve.wait_ge(ada_used, (b + 1) * KD)
                nc.vector.tensor_copy(wk[1][:, 0:512], modps[:]).then_inc(mod_rows, 1)

            def mod_finish(b):
                dve.wait_ge(tps_full, KD + 1 + b)
                src = tps[:].rearrange("p (q j r) -> p j q r", q=4, j=4)[:, :, :, 0:R]
                dst = modT[:, b * MC:(b + 1) * MC, :].rearrange("p (j q) r -> p j q r", q=4)
                bias = b_adaT[:, b * MC:(b + 1) * MC].rearrange("p (j q) -> p j q", q=4)
                for j in range(4):
                    ins = nc.vector.tensor_tensor(dst[:, j], src[:, j],
                                                  bias[:, j].unsqueeze(2).broadcast_to([P, 4, R]), ALU.add)
                    if j < 3:
                        ins.then_inc(order, 1)
                ins.then_inc(mod_ready, 1)
                nonlocal links
                links += 3
                dve.wait_ge(order, links)
                dve.wait_ge(mod_ready, b)

            def h_pre(nth, k, A):
                if k >= 2:
                    dve.wait_ge(hlo_ready, nth * KD + k - 1)
                nc.vector.scalar_tensor_tensor(wk[1 + k % 2][:, 0:T], xT[:, k, 0:T], A[:, k, 0:1],
                                               wk[0][:, 0:T], ALU.mult, ALU.mult).then_inc(hpre_ready, 1)

            def h_low(nth, k, shift):
                dve.wait_ge(hpre_ready, nth * KD + k + 1)
                dve.wait_ge(hhi_ready, nth * KD + k + 1)
                nc.vector.scalar_tensor_tensor(hlo[:, k, 0:T], wk[1 + k % 2][:, 0:T],
                                               modT[:, shift + k, 0:1], hhi[:, k, 0:T].bitcast(F32),
                                               ALU.add, ALU.subtract).then_inc(hlo_ready, 1)

            def cols_to_rows(k):
                dve.wait_ge(ada_used, k + 1)
                if k >= 2:
                    dve.wait_ge(tps_full, k)
                nc.vector.tensor_copy(mod_part(k), modps[:, 0:2 * P]).then_inc(mod_rows, 1)

            def cols_finish(k):
                dve.wait_ge(tps_full, 2 + k)
                for m in range(2):
                    at = 32 * m
                    j = m * KD + k
                    link(nc.vector.tensor_scalar(modT[:, j, :], tps[:, at:at + R], b_adaT[:, j:j + 1], None, ALU.add))
                nc.vector.tensor_scalar(A1[:, k, :], modT[:, KD + k, :], 1.0, n1T[:, k:k + 1], ALU.add, ALU.mult
                                        ).then_inc(gains_ready, 1)
                dve.wait_ge(gains_ready, k + 1)

            for step in range(KD + 2):
                if step < KD:
                    cols_to_rows(step)
                if 1 <= step <= KD:
                    cols_finish(step - 1)
                    if step == 1:
                        dve.wait_ge(rstd_ready, NT)
                    h_pre(0, step - 1, A1)
                if step >= 2:
                    h_low(0, step - 2, 0)

            st, past_prod = dc, wk[1]
            dve.wait_ge(hlo_ready, KD)
            def past(dst, ps, taps, k):
                prod = past_prod[:, 0:S * k].rearrange("p (b t) -> p b t", b=S)
                link(nc.vector.tensor_tensor(prod, ps.rearrange("p (b t) -> p b t", b=S),
                                             taps.unsqueeze(1).broadcast_to([P, S, k]), ALU.mult))
                link(nc.vector.tensor_reduce(dst, prod, AX_X, ALU.add))

            for c in range(CONV_C):
                conf_taps = tapT[:].rearrange("p (j c) -> p c j", c=CONV_C)[:, c, 0:CK - 1]
                past(past_conf[:, c, :], st[:, c, 0:S * (CK - 1)], conf_taps, CK - 1)
                taps = sconvT.rearrange("p (j c) -> p c j", c=CONV_C)[:, c, 0:SK - 1]
                past(past_sconv[:, c, :], st[:, c, 240:240 + S * (SK - 1)], taps, SK - 1)
            for g, w in enumerate(WINDOWS):
                half, c = slice(64 * (g % 2), 64 * (g % 2) + 64), g // 2
                rows = st[half, c, 256:256 + S * PBUF].rearrange("p (b t) -> p b t", b=S)
                ins = nc.vector.tensor_reduce(past_pool[half, c, :], rows[:, :, PBUF - (w - 1):PBUF], AX_X, ALU.add)
                link(ins)

            steps = [(c, s) for c in range(CONV_C) for s in range(CK + 1)]
            done = 0

            def convolve(count):
                nonlocal done
                for c, s in steps[done:done + count]:
                    if s == 0:
                        dve.wait_ge(glu_ready, c + 1)
                        tap = 3 * (CK - 1) + c
                        ins = nc.vector.tensor_scalar(dc[:, c, :], glu[:, c, :], tapT[:, tap:tap + 1],
                                                      cbT[:, c:c + 1], ALU.mult, ALU.add)
                    else:
                        dve.wait_ge(conv_step, done)
                        if s < CK:
                            tap = 3 * (CK - 1 - s) + c
                            ins = nc.vector.scalar_tensor_tensor(dc[:, c, s:T], glu[:, c, 0:T - s],
                                                                 tapT[:, tap:tap + 1], dc[:, c, s:T],
                                                                 ALU.mult, ALU.add)
                        else:
                            ins = nc.vector.tensor_tensor(dc[:, c, T:N], dc[:, c, T:N], past_conf[:, c, :], ALU.add)
                    ins.then_inc(conv_step, 1)
                    done += 1

            def pooled(c):
                dve.wait_ge(u_ready, c + 1)
                u, s2 = work[c], work[2]
                if c == 0:
                    s4 = work[1]
                else:
                    dve.wait_ge(psum_full, CHUNK_AT[("ya", 0)] + 1)
                    s4 = work[0]

                def twice(dst, src, w, lo):
                    link(nc.vector.tensor_tensor(dst[lo:P, PAD:PAD + T], src[lo:P, PAD:PAD + T],
                                                 src[lo:P, PAD - w:PAD - w + T], ALU.add))

                twice(s2, u, 1, 0)
                if c == 0:
                    twice(s4, s2, 2, 64)
                    low, high_ = s2, s4
                else:
                    twice(s4, s2, 2, 0)
                    twice(s2, s4, 4, 0)
                    twice(s4, s2, 8, 64)
                    low, high_ = s2, s4
                for hf, s in ((0, low), (1, high_)):
                    p, w = slice(64 * hf, 64 * hf + 64), WINDOWS[2 * c + hf]
                    link(nc.vector.tensor_tensor(s[p, PAD + T:], u[p, PAD + T:], past_pool[p, c, :], ALU.add))
                    link(nc.vector.tensor_tensor(s[p, PAD:2 * PAD], s[p, PAD:2 * PAD], head_rc[p, c, :], ALU.mult))
                    link(nc.vector.tensor_tensor(u[p, PAD:2 * PAD], s[p, PAD:2 * PAD], u[p, PAD:2 * PAD], ALU.subtract))
                    ins = nc.vector.scalar_tensor_tensor(u[p, 2 * PAD:], s[p, 2 * PAD:], 1.0 / w, u[p, 2 * PAD:],
                                                         ALU.mult, ALU.subtract)
                    if hf == 0:
                        link(ins)
                    else:
                        ins.then_inc(pool_ready, 1)

            def ya_low(c):
                n = CHUNK_AT[("ya", c)]
                dve.wait_ge(yhi_ready, c + 1)
                nc.vector.scalar_tensor_tensor(tiled(yab_lo[:, c, :]), flat(chunk_of(n)), pscaleT[:, c:c + 1],
                                               tiled(yab_hi[:, c, :].bitcast(F32)), ALU.mult, ALU.subtract
                                               ).then_inc(ylo_ready, 1)

            def residual(n, d, gate):
                ps = acc[:, n % 2, :, :]
                g1 = modT[:, gate + d, 0:1]
                w2 = T - 2 * TW
                nc.vector.scalar_tensor_tensor(pair(xT[:, d, 0:2 * TW]), ps[:, 0:2, 0:TW], g1,
                                               pair(xT[:, d, 0:2 * TW]), ALU.mult, ALU.add)
                nc.vector.scalar_tensor_tensor(xT[:, d, 2 * TW:T], ps[:, 2, 0:w2], g1,
                                               xT[:, d, 2 * TW:T], ALU.mult, ALU.add)
                nc.vector.tensor_copy(gate_s[:, d, :], ps[:, 2, w2:TW]).then_inc(freed_v, 1)

            def add_squares(n, d):
                dve.wait_ge(sq_ready, SQ[n] + d + 1)
                if d >= 2:
                    dve.wait_ge(sq_added, ADDED[n] + d - 1)
                w, tile = (N, wk[1]) if n == 2 else (T, wk[sq_tile(d)])
                nc.vector.tensor_tensor(wk[0][:, 0:w], wk[0][:, 0:w], tile[:, 0:w], ALU.add).then_inc(sq_added, 1)

            def residual_sample(gate, wait_copy, updated):
                dve.wait_ge(freed_v, wait_copy)
                nc.vector.tensor_tensor(small[:], gate_s[:], modT[:, gate:gate + KD, 1:R], ALU.mult
                                        ).then_inc(x_updated, 1)
                dve.wait_ge(x_updated, updated - 1)
                nc.vector.tensor_tensor(xT[:, :, T:N], xT[:, :, T:N], small[:], ALU.add).then_inc(x_updated, 1)

            def square_sample(updated):
                dve.wait_ge(x_updated, updated)
                link(nc.vector.tensor_tensor(small[:], xT[:, :, T:N], xT[:, :, T:N], ALU.mult))
                nc.vector.tensor_reduce(sample_sq[:], small[:].rearrange("p k s -> p s k"), AX_X, ALU.add
                                        ).then_inc(xsq_ready, 1)

            for u in range(U_FF):
                (kind, c), n = UNITS[u]
                ps = flat(chunk_of(n))
                if kind == "ga":
                    dve.wait_ge(psum_full, n + 1)
                    dve.wait_ge(sig_ready, c + 1)
                    nc.vector.tensor_tensor(last_cols[:, 1, LASTC * c:LASTC * c + LASTC],
                                            chunk_of(n)[:, 2, TW - LASTC:TW], wk[2][:, N - LASTC:N], ALU.mult
                                            ).then_inc(last_v, 1)
                    nc.vector.tensor_tensor(tiled(glu[:, c, :]), ps, tiled(wk[2]), ALU.mult).then_inc(glu_ready, 1)
                    if c == 2:
                        mod_to_rows(2)
                    convolve(14 if c < 2 else 7)
                if kind == "gg" and c == 1:
                    mod_to_rows(1)
                if kind == "gg" and c == 2:
                    mod_finish(1)
                if kind == "u":
                    if c == 0:
                        mod_finish(2)
                        nc.vector.scalar_tensor_tensor(A2[:], modT[:, 4 * KD:5 * KD, :], 1.0,
                                                       n2T.unsqueeze(2).broadcast_to([P, KD, R]),
                                                       ALU.add, ALU.mult).then_inc(gains_ready, 1)
                    pooled(c)
                    if c == 1:
                        ya_low(0)
                    convolve(4)
                if kind == "v":
                    if c == 0:
                        ya_low(1)
                    convolve(7)
                if kind == "gc":
                    dve.wait_ge(psum_full, n + 1)
                    dve.wait_ge(v_ready, c + 1)
                    if c == 0:
                        dve.wait_ge(psum_full, CHUNK_AT[("ya", 1)] + 1)
                    nc.vector.tensor_tensor(last_cols[:, 0, 46 + 10 * c:56 + 10 * c],
                                            chunk_of(n)[:, 2, TW - 10:TW], wk[0][:, N - 10:N], ALU.mult
                                            ).then_inc(last_v, 1)
                    nc.vector.tensor_tensor(tiled(wk[1]), ps, tiled(wk[0]), ALU.mult).then_inc(freed_v, 1)
                    dve.wait_ge(freed_v, FREED_V[n])
                    cv, out = wk[1], wk[2]
                    tap = [sconvT[:, 3 * j + c:3 * j + c + 1] for j in range(SK)]
                    link(nc.vector.tensor_scalar(out[:], cv[:], tap[2], None, ALU.mult))
                    for s in (1, 2):
                        link(nc.vector.scalar_tensor_tensor(out[:, s:T], cv[:, 0:T - s], tap[2 - s], out[:, s:T],
                                                            ALU.mult, ALU.add))
                    link(nc.vector.tensor_tensor(out[:, T:N], out[:, T:N], past_sconv[:, c, :], ALU.add))
                    convolve(5)
                if kind == "gb":
                    dve.wait_ge(psum_full, n + 1)
                    nc.vector.tensor_tensor(tiled(wk[0]), ps, tiled(wk[2]), ALU.mult).then_inc(yb_ready, 1)
                    dve.wait_ge(yb_ready, c + 1)
                    dve.wait_ge(yhi_ready, POOL_C + c + 1)
                    nc.vector.tensor_tensor(yab_lo[:, POOL_C + c, :], wk[0][:], yab_hi[:, POOL_C + c, :].bitcast(F32),
                                            ALU.subtract).then_inc(ylo_ready, 1)
                    convolve(6 if c < 2 else 200)
                    if c == 2:
                        dve.wait_ge(conv_step, done)
                        link(nc.vector.tensor_tensor(wk[1][:], dc[:, 0, :], dc[:, 1, :], ALU.add))
                        nc.vector.tensor_tensor(wk[1][:], wk[1][:], dc[:, 2, :], ALU.add).then_inc(dc_added, 1)
                if kind == "p1":
                    if c == 2:
                        m = CHUNK_AT["lnmean"]
                        dve.wait_ge(psum_full, m + 1)
                        for j in range(CONV_C):
                            nc.vector.scalar_tensor_tensor(tiled(dc[:, j, :]), flat(chunk_of(m)), -1.0 / 384,
                                                           tiled(dc[:, j, :]), ALU.mult, ALU.add).then_inc(centred, 1)
                    if c == LN_ROOT:
                        dve.wait_ge(sq_used, 1)
                        mean_squares(2, tps, CONV_C * P)
                        diagonals(2)
                    if c == 5:
                        m = CHUNK_AT["lnvar"]
                        dve.wait_ge(psum_full, m + 1)
                        dve.wait_ge(centred, CONV_C)
                        for j in range(CONV_C):
                            nc.vector.scalar_tensor_tensor(tiled(dc[:, j, :]), tiled(dc[:, j, :]), lgT[:, j:j + 1],
                                                           flat(chunk_of(m)), ALU.mult, ALU.mult
                                                           ).then_inc(ln_scaled, 1)
                        for j in range(CONV_C):
                            dve.wait_ge(ln_scaled, j + 1)
                            dve.wait_ge(lsig_ready, j + 1)
                            nc.vector.scalar_tensor_tensor(dc[:, j, :], dc[:, j, :], lbT[:, j:j + 1], wk[1 + j % 2][:],
                                                           ALU.add, ALU.mult).then_inc(silu_ready, 1)
                    if c == 6:
                        for j in range(CONV_C):
                            dve.wait_ge(silu_ready, j + 1)
                            dve.wait_ge(yhi_ready, 5 + j + 1)
                            nc.vector.tensor_tensor(yc_lo[:, j, :], dc[:, j, :], yc_hi[:, j, :].bitcast(F32),
                                                    ALU.subtract).then_inc(ylo_ready, 1)
                    dve.wait_ge(psum_full, n + 1)
                    residual(n, c, 2 * KD)
                    if c == 0:
                        dve.wait_ge(tps_full, KD + 4)
                        nc.vector.tensor_copy(states_out[:], tps[:, 0:2 * P].rearrange("p (a n) -> p a n", a=2)
                                              ).then_inc(states_ready, 1)
                    if c == 2:
                        add_squares(2, 1)
                    if c == 7:
                        residual_sample(2 * KD, FREED_V[n], 2)
                if kind == "p2":
                    for d in (2 * c, 2 * c + 1):
                        m = CHUNK_AT[("p2", d)]
                        if d >= 2:
                            add_squares(3, d - 1)
                        dve.wait_ge(psum_full, m + 1)
                        if d == 0:
                            dve.wait_ge(x_updated, 2)
                        residual(m, d, 2 * KD)
                    if c == 3:
                        residual_sample(2 * KD, V_FF, 4)

            square_sample(4)
            dve.wait_ge(sq_used, 2)
            mean_squares(3, tps, D)
            diagonals(3)
            dve.wait_ge(rstd_ready, 2 * NT)
            dve.wait_ge(gains_ready, KD + 1)
            for step in range(KD + 1):
                if step < KD:
                    h_pre(1, step, A2)
                if step:
                    h_low(1, step - 1, 3 * KD)

            def hidden(at, f, slot, j):
                dve.wait_ge(psum_full, C_FF + at + 1)
                dve.wait_ge(relu_ready, f + 1)
                q = wk[1 + j % 2]
                nc.vector.scalar_tensor_tensor(tiled(q), flat(acc[:, (C_FF + j) % 2, :, :]), 0.0, tiled(wk[0]),
                                               ALU.max, ALU.mult).then_inc(freed_v, 1)
                dve.wait_ge(freed_v, V_FF + at + 1)
                dve.wait_ge(hid_hi_ready, f + 1)
                nc.vector.tensor_tensor(hid_lo[:, slot + j, :], q[:], hid_hi[:, slot + j, :].bitcast(F32),
                                        ALU.subtract).then_inc(hid_lo_ready, 1)

            def down(at, updated):
                for d in range(KD):
                    dve.wait_ge(psum_full, C_FF + at + d + 1)
                    if d == 0:
                        dve.wait_ge(x_updated, updated)
                    residual(C_FF + d, d, 5 * KD)
                residual_sample(5 * KD, V_FF + at + KD, updated + 2)

            for j in range(FG):
                hidden(j, j, 0, j)

            def step(g, slot):
                for j in range(FG):
                    hidden(g * 12 + 4 + j, g * FG + FG + j, slot, j)
                down(g * 12 + 8, g * 2 + 4)

            with dve.Fori(0, NG - 2, 2) as g:
                step(g, FG)
                step(g + 1, 0)
            step(NG - 2, FG)

            def part(i, bank, gate):
                t, d = divmod(i % (NT * KD), KD)
                dve.wait_ge(part_full, i + 1)
                w = min(TW, T - t * TW)
                x = xT[:, d, t * TW:t * TW + w]
                ins = nc.vector.scalar_tensor_tensor(x, bank[:, 0:w], modT[:, gate + d, 0:1], x, ALU.mult, ALU.add)
                if w == TW:
                    ins.then_inc(part_read, 1)
                else:
                    nc.vector.tensor_tensor(small[:, d, :], bank[:, w:TW], modT[:, gate + d, 1:R], ALU.mult
                                            ).then_inc(part_read, 1)
                    dve.wait_ge(part_read, i + 1)
                    nc.vector.tensor_tensor(xT[:, d, T:N], xT[:, d, T:N], small[:, d, :], ALU.add
                                            ).then_inc(xs_updated, 1)

            def add_part(t, d):
                dve.wait_ge(sq_ready, SQ[4] + t * KD + d + 1)
                done = ADDED[4] + t * (KD - 2) + d - 1
                dve.wait_ge(sq_added, done)
                nc.vector.tensor_tensor(sq_part(0), sq_part(0), sq_part(d), ALU.add).then_inc(sq_added, 1)

            def mean_of_tile(t):
                dve.wait_ge(sq_used, 3 + t)
                nc.vector.tensor_scalar(rstd[:, 3 * t:3 * t + 3], tps[:, 3 * t:3 * t + 3], 1.0 / D, EPS,
                                        ALU.mult, ALU.add).then_inc(ms_ready, 1)

            def invert_tile(t):
                dve.wait_ge(root_ready, 4 + t)
                link(nc.vector.reciprocal(rstd[:, 3 * t:3 * t + 3], rstd[:, 3 * t:3 * t + 3]))

            gain = wraw[:, U_END % 2, :]

            def rows_out(i):
                dve.wait_ge(rows_full, i + 1)
                if i >= 2:
                    dve.wait_ge(y_stored[i % 2], 16 * (i // 2))
                nc.vector.scalar_tensor_tensor(pair(wk[i % 2][:, 0:D]), rows_bank(i), rstd[:, i:i + 1],
                                               pair(gain), ALU.mult, ALU.mult).then_inc(out_ready, 1)

            for t in range(NT):
                for d in range(KD):
                    if d >= 2:
                        add_part(t, d - 1)
                    part(t * KD + d, last_bank(t * KD + d), 5 * KD)
                    if t and d == 1:
                        mean_of_tile(t - 1)
                    if t and d == 2:
                        invert_tile(t - 1)
                        dve.wait_ge(gain_loaded, 16)
                    if t and d in (2, 4, 6):
                        rows_out(3 * (t - 1) + d // 2 - 1)
            mean_of_tile(NT - 1)
            invert_tile(NT - 1)
            for i in range(3 * NT - 3, 3 * NT):
                rows_out(i)

        @block.tensor
        def _(pe):
            def freed(n):
                if n < 0:
                    return
                name, by = CHUNKS[n]
                if by == "V":
                    pe.wait_ge(freed_v, FREED_V[n])
                elif name == "norm1":
                    pe.wait_ge(rstd_ready, NT)
                elif name == "lnmean":
                    pe.wait_ge(centred, CONV_C)
                elif name == "lnvar":
                    pe.wait_ge(ln_scaled, CONV_C)
                elif name == "norm2":
                    pe.wait_ge(rstd_ready, 2 * NT)
                elif name[0] == "ya":
                    pe.wait_ge(ylo_ready, name[1] + 1)
                elif name[0] == "ga":
                    pe.wait_ge(glu_ready, name[1] + 1)
                elif name[0] == "gb":
                    pe.wait_ge(yb_ready, name[1] + 1)
                elif name[0] == "gg":
                    pe.wait_ge(sig_ready, name[1] + 1)
                elif name[0] == "u":
                    pe.wait_ge(u_ready, name[1] + 1)
                else:
                    pe.wait_ge(v_ready, name[1] + 1)

            def product(out, slot, blocks, hi, lo, ready=None):
                for i, (b, k) in enumerate(blocks):
                    if ready:
                        ready(k)
                    for w, x in ((whi, hi), (whi, lo), (wlo, hi)):
                        for t in range(NT):
                            last = nc.tensor.matmul(out[:, t, 0:TW], w[:, slot, b, :], x[:, k, t * TW:(t + 1) * TW],
                                                    start=(i == 0 and w is whi and x is hi),
                                                    stop=(i == len(blocks) - 1 and w is wlo))
                return last

            def products_of_two(u0, outs, nth, ahead=0, before=None):
                for step in range(KD + LAG + ahead):
                    if before:
                        before(step)
                    for j in range(2):
                        k = step - ahead - LAG * j
                        if not 0 <= k < KD:
                            continue
                        if k == 0:
                            pe.wait_ge(wlo_ready, u0 + j + 1)
                        for w, x in ((whi, hhi), (wlo, hhi), (whi, hlo)):
                            if j == 0 and w is whi:
                                pe.wait_ge(hhi_ready if x is hhi else hlo_ready, nth * KD + k + 1)
                            for t in range(NT):
                                last = nc.tensor.matmul(outs[j][:, t, 0:TW], w[:, (u0 + j) % 2, k, :],
                                                        x[:, k, t * TW:(t + 1) * TW],
                                                        start=(k == 0 and w is whi and x is hhi),
                                                        stop=(k == KD - 1 and x is hlo))
                        if k == KD - 1:
                            last.then_inc(psum_full, 1)

            def token_sums(rows, first, last):
                for i in range(KD):
                    ins = nc.tensor.matmul(tps[:, i:i + 1], rows[:, i * P:(i + 1) * P], ones[:, 0:1],
                                           start=(first and i == 0), stop=last, skip_group_check=True)
                return ins

            def sample_sums(rows, stop):
                return nc.tensor.matmul(tps[0:S, KD:R], rows, ones[:, 0:1], start=False, stop=stop,
                                        skip_group_check=True)

            def keep_clock(count):
                for _ in range(count):
                    nc.tensor.matmul(modps[:, 0:TW], yc_hi[:, 0, 0:P], yc_hi[:, 0, 0:TW], start=True, stop=True)

            def norm_sums(n, warm):
                pe.wait_ge(ms_ready, n - 1)
                pe.wait_ge(sq_added, ADDED[n] + KD - 2)
                token_sums(wk[0], True, False)
                keep_clock(warm)
                pe.wait_ge(sq_ready, SQ[n] + KD)
                token_sums(wk[sq_tile(KD - 1)], False, True)
                pe.wait_ge(xsq_ready, n - 2)
                sample_sums(sample_sq[:], True).then_inc(sq_used, 1)

            def spread(n, m):
                freed(m - 2)
                for t in range(NT):
                    pe.wait_ge(diag_ready, NT * (n - 1) + t + 1)
                    nc.tensor.matmul(chunk_of(m)[:, t, 0:TW], ones[:], wk[1][:, t * TW:(t + 1) * TW],
                                     start=True, stop=True).then_inc(psum_full if t == NT - 1 else spread_full, 1)

            pe.wait_ge(const_ready, 3)
            for i in range(KD):
                n = CHUNK_AT[("x", i)]
                pe.wait_ge(x_loaded[i], 16)
                freed(n - 2)
                for k in range(KD):
                    last = nc.tensor.transpose(chunk_of(n)[:, k // 4, (k % 4) * P:(k % 4 + 1) * P],
                                               xrow[:, i, k * P:(k + 1) * P], ident[:])
                last.then_inc(psum_full, 1)
            pe.wait_ge(vec_loaded, 16 * 9)
            nc.tensor.transpose(tps[:, 0:84], vrow[:], ident[0:84, 0:84])
            nc.tensor.transpose(tps[:, 84:84 + CK * CONV_C], taprow[:], ident[0:CK * CONV_C, 0:CK * CONV_C])
            pe.wait_ge(c_ready, 1)
            for k in range(KD):
                last = nc.tensor.transpose(tps[:, 192 + 32 * k:224 + 32 * k], csig[:, k * P:(k + 1) * P],
                                           ident[0:32, 0:32])
            last.then_inc(tps_full, 1)
            m = CHUNK_AT["states"]
            st = chunk_of(m)
            freed(m - 2)
            pe.wait_ge(st_loaded, 16 * 4)
            pe.wait_ge(xs_loaded, 16)
            for c in range(CONV_C):
                cols = slice(c * P, (c + 1) * P)
                for i in range(2):
                    nc.tensor.transpose(st[:, c, i * 120:(i + 1) * 120], st_conf[:, i, cols], ident[0:120, 0:120])
                nc.tensor.transpose(st[:, c, 240:256], st_sconv[:, cols], ident[0:16, 0:16])
                if c < POOL_C:
                    nc.tensor.transpose(st[:, c, 256:376], st_pool[:, cols], ident[0:120, 0:120])
            for k in range(KD):
                last = nc.tensor.transpose(st[:, 2, 376 + 8 * k:384 + 8 * k], xsrow[:, k * P:(k + 1) * P],
                                           ident[0:S, 0:S])
            last.then_inc(psum_full, 1)
            def ada_ready(q):
                loads = sum(2 if p < KD else 1 for p in range(q % ADA_SLOTS, q + 1, ADA_SLOTS))
                pe.wait_ge(ada_loaded[q % ADA_SLOTS], 16 * loads)

            def modulate_cols(k):
                ada_ready(k)
                if k:
                    pe.wait_ge(mod_rows, k)
                src = ada[:, k % ADA_SLOTS, :]
                for kk in range(KD):
                    j = kk % 4
                    last = nc.tensor.matmul(modps[32 * j:32 * j + 32, 0:2 * P], cT[:, kk, :],
                                            src[:, kk * 2 * P:(kk + 1) * 2 * P], start=(kk < 4), stop=(kk >= 4),
                                            tile_position=(0, 32 * j), skip_group_check=True)
                last.then_inc(ada_used, 1)

            def transpose_cols(k):
                pe.wait_ge(mod_rows, k + 1)
                if k:
                    pe.wait_ge(gains_ready, k)
                for m in range(2):
                    last = nc.tensor.matmul(tps[:, 32 * m:32 * m + 32], mod_part(k)[:, m * P:(m + 1) * P],
                                            quarters[:], start=True, stop=True)
                last.then_inc(tps_full, 1)

            def modulate(q):
                b, k = q // KD, q % KD
                ada_ready(q)
                if k == 0:
                    pe.wait_ge(mod_rows, KD + b - 1)
                for j in range(4):
                    last = nc.tensor.matmul(modps[32 * j:32 * j + 32, :], cT[:, k, :],
                                            ada[:, q % ADA_SLOTS, j * 512:(j + 1) * 512],
                                            start=(k == 0), stop=(k == KD - 1), tile_position=(0, 32 * j),
                                            skip_group_check=True)
                last.then_inc(ada_used, 1)

            def mod_transpose(b):
                pe.wait_ge(mod_rows, KD + b)
                pe.wait_ge(gains_ready, KD) if b == 1 else pe.wait_ge(mod_ready, b - 1)
                for q in range(4):
                    last = nc.tensor.transpose(tps[:, q * P:(q + 1) * P], wk[1][:, q * P:(q + 1) * P], ident[:])
                last.then_inc(tps_full, 1)

            def next_cols(step):
                if step == 0:
                    pe.wait_ge(quarters_ready, 1)
                    pe.wait_ge(tps_read, 3)
                if 1 <= step <= KD:
                    transpose_cols(step - 1)
                if step < KD:
                    modulate_cols(step)

            def cols_and_sample(step):
                if step:
                    next_cols(step)
                if 0 <= step - COLS_AHEAD < KD:
                    pe.wait_ge(h_sample_ready, step - COLS_AHEAD + 1)

            s = KD
            for u in range(U_FF):
                (kind, c), n = UNITS[u]
                ready = None
                if u:
                    pe.wait_ge(wlo_ready, u + 1)
                if kind == "p1":
                    if c == 0:
                        ready = lambda k: pe.wait_ge(ylo_ready, k + 1)
                    blocks, hi, lo = [(b, b) for b in range(5)], yab_hi, yab_lo
                elif kind != "p2":
                    blocks, hi, lo = [(b, b) for b in range(KD)], hhi, hlo
                if u == 0:
                    next_cols(0)
                    spread(1, CHUNK_AT["norm1"])
                    freed(n - 2)
                    freed(n - 1)
                    products_of_two(0, [chunk_of(n), chunk_of(n + 1)], 0, COLS_AHEAD, cols_and_sample)
                elif u == 1:
                    pass
                elif kind != "p2":
                    freed(n - 2)
                    product(chunk_of(n), u % 2, blocks, hi, lo, ready).then_inc(psum_full, 1)
                else:
                    if c == 0:
                        pe.wait_ge(ylo_ready, 8)
                    for d in (2 * c, 2 * c + 1):
                        m = CHUNK_AT[("p2", d)]
                        freed(m - 2)
                        product(chunk_of(m), u % 2, [(2 * b + d % 2, b) for b in range(CONV_C)], yc_hi, yc_lo
                                ).then_inc(psum_full, 1)
                for _ in range(ADA_AFTER.get(u, 0)):
                    modulate(s)
                    s += 1
                if kind == "ga" and c == 1:
                    mod_transpose(1)
                if kind == "u" and c == 0:
                    mod_transpose(2)
                pooled = {("u", 1): 0, ("v", 0): 1}.get((kind, c))
                if pooled is not None:
                    m = CHUNK_AT[("ya", pooled)]
                    freed(m - 2)
                    pe.wait_ge(pool_ready, pooled + 1)
                    pe.wait_ge(pw_loaded, 16 * 4)
                    for t in range(NT):
                        last = nc.tensor.matmul(chunk_of(m)[:, t, 0:TW], pw[:, pooled, :],
                                                wk[pooled][:, t * TW:(t + 1) * TW], start=True, stop=True)
                    last.then_inc(psum_full, 1)
                if kind == "gb" and c == 2:
                    pe.wait_ge(mod_ready, 2)
                    pe.wait_ge(last_u, 2)
                    pe.wait_ge(last_v, 2 * CONV_C)
                    for a in range(2):
                        last = nc.tensor.transpose(tps[:, a * P:(a + 1) * P], last_cols[:, a, :], ident[:])
                    last.then_inc(tps_full, 1)
                if kind == "p1" and c == 1:
                    m = CHUNK_AT["lnmean"]
                    freed(m - 2)
                    pe.wait_ge(dc_added, 1)
                    for t in range(NT):
                        last = nc.tensor.matmul(chunk_of(m)[:, t, 0:TW], ones[:], wk[1][:, t * TW:(t + 1) * TW],
                                                start=True, stop=True)
                    last.then_inc(psum_full, 1)
                if kind == "p1" and c == LN_ROOT - 1:
                    pe.wait_ge(states_ready, 1)
                    for j in (0, 2):
                        pe.wait_ge(sq_added, 1) if j == 0 else pe.wait_ge(sq_ready, CONV_C)
                        token_sums(wk[j], j == 0, j == 2)
                        last = sample_sums(wk[j][:, T:N], j == 2)
                    last.then_inc(sq_used, 1)
                if kind == "p1" and c == 4:
                    spread(2, CHUNK_AT["lnvar"])

            pe.wait_ge(mod_ready, 2)
            norm_sums(3, WARM[0])
            keep_clock(WARM[1])
            spread(3, CHUNK_AT["norm2"])
            keep_clock(WARM[2])

            def up(at, j0, pairs, first=0):
                for j in range(first, FG):
                    pe.wait_ge(wlo_ready, U_FF + j0 + j + 1 + pairs * 2)
                    freed_before(at + j)
                    product(acc[:, (C_FF + j) % 2, :, :], (U_FF + j) % 2, [(b, b) for b in range(KD)], hhi, hlo
                            ).then_inc(psum_full, 1)

            def freed_before(at):
                if isinstance(at, int) and at < 2:
                    freed(C_FF + at - 2)
                else:
                    pe.wait_ge(freed_v, V_FF - 1 + at)

            def down(at, j0, pairs, f, slot):
                pe.wait_ge(hid_lo_ready, f)
                for j in range(FG):
                    pe.wait_ge(wlo_ready, U_FF + j0 + j + 1 + pairs * 2)
                    for dd in range(2):
                        d = 2 * j + dd
                        freed_before(at + d)
                        product(acc[:, (C_FF + d) % 2, :, :], (U_FF + j) % 2,
                                [(2 * b + dd, slot + b) for b in range(FG)], hid_hi, hid_lo).then_inc(psum_full, 1)

            pe.wait_ge(h_sample_ready, KD + 1)
            freed_before(0)
            freed_before(1)
            products_of_two(U_FF, [chunk_of(C_FF), chunk_of(C_FF + 1)], 1)
            up(0, 0, 0, 2)

            def step(g, slot):
                up(g * 12 + 4, 4, g * 4)
                down(g * 12 + 8, 8, g * 4, g * FG + FG, FG - slot)

            with pe.Fori(0, NG - 2, 2) as g:
                step(g, FG)
                step(g + 1, 0)
            step(NG - 2, FG)

            def part(i, bank, blocks, hi, lo):
                cols = slice(i // KD % NT * TW, (i // KD % NT + 1) * TW)
                for b, (w_hi, w_lo, k) in enumerate(blocks):
                    nc.tensor.matmul(bank[:, 0:TW], w_hi, hi[:, k, cols], start=(b == 0), stop=False)
                    nc.tensor.matmul(bank[:, 0:TW], w_hi, lo[:, k, cols], start=False, stop=False)
                    last = nc.tensor.matmul(bank[:, 0:TW], w_lo, hi[:, k, cols], start=False,
                                            stop=(b == len(blocks) - 1))
                last.then_inc(part_full, 1)

            def tile_sums(t):
                pe.wait_ge(ms_ready, 3 + t)
                for d in (0, KD - 1):
                    if d:
                        pe.wait_ge(sq_ready, SQ[4] + t * KD + KD)
                    else:
                        pe.wait_ge(sq_added, ADDED[4] + (t + 1) * (KD - 2))
                    for q in range(3):
                        last = nc.tensor.matmul(tps[:, 3 * t + q:3 * t + q + 1], sq_part(d)[:, SUB[q]:SUB[q] + P],
                                                ones[:, 0:1], start=(d == 0 and q == 0), stop=(d > 0),
                                                skip_group_check=True)
                last.then_inc(sq_used, 1)

            def rows_out(i):
                if i % 3 == 0:
                    pe.wait_ge(part_read, (i // 3 + 1) * KD)
                if i == 3 * NT - 3:
                    pe.wait_ge(xs_updated, KD)
                elif i:
                    pe.wait_ge(out_ready, i if i < 3 * NT - 3 else i - 1)
                for k in range(KD):
                    last = nc.tensor.transpose(rows_bank(i)[:, k // 4, (k % 4) * P:(k % 4 + 1) * P],
                                               xT[:, k, square_of(i):square_of(i) + P], ident[:])
                last.then_inc(rows_full, 1)

            pe.wait_ge(hid_lo_ready, FF_C)
            for t in range(NT):
                for d in range(KD):
                    i, u = t * KD + d, U_END - FG + d // 2
                    if t == 0:
                        pe.wait_ge(wlo_ready, u + 1)
                    if i == 0:
                        pe.wait_ge(freed_v, V_FF + AT_LAST - 1)
                    elif i == 3:
                        pe.wait_ge(freed_v, V_FF + AT_LAST)
                    elif i > 3:
                        pe.wait_ge(part_read, i - 3)
                    w_hi, w_lo = split_at(whi, u), split_at(wlo, u)
                    part(i, last_bank(i), [(w_hi[:, 2 * b + d % 2, :], w_lo[:, 2 * b + d % 2, :], FG + b)
                                           for b in range(FG)], hid_hi, hid_lo)
                    if t and d == 1:
                        tile_sums(t - 1)
                    if t and d in (1, 3, 5):
                        rows_out(3 * (t - 1) + d // 2)
            rows_out(3 * NT - 3)
            tile_sums(NT - 1)
            rows_out(3 * NT - 2)
            rows_out(3 * NT - 1)


_INS = ["x_prompt", "x_sample", "c_prompt", "c_sample", "state_pool", "state_sconv", "state_conf", "w_ada", "b_ada",
        "norm1_g", "norm2_g", "w_in", "pool_w", "pool_scale", "sconv_w", "conf_w", "conf_b", "conf_ln_g",
        "conf_ln_b", "w_out", "w_ff1", "w_ff2", "final_g"]
_OUTS = [(1, T, D), (S, 1, D), (1, 1, PBUF, 256), (1, 1, SK - 1, 384), (1, 1, CK - 1, 384),
         (1, S, PBUF, 256), (1, S, SK - 1, 384), (1, S, CK - 1, 384)]


def kernel(**inputs):
    import numpy as _np
    import concourse.bacc as _bacc
    from concourse import mybir as _mybir
    from concourse.bass_utils import run_bass_kernel_spmd as _run

    nc = _bacc.Bacc("TRN2", target_bir_lowering=False, num_devices=1)
    arrays, args = {}, []
    for name in _INS:
        a = _np.ascontiguousarray(inputs[name])
        arrays[f"in_{name}"] = a
        args.append(nc.dram_tensor(f"in_{name}", a.shape, _mybir.dt.from_np(a.dtype), kind="ExternalInput").ap())
    for i, shape in enumerate(_OUTS):
        args.append(nc.dram_tensor(f"out_{i}", shape, F32, kind="ExternalOutput").ap())
    decoder_trunk(nc, *args)
    r = _run(nc, [arrays], core_ids=[0])
    return tuple(r.results[0][f"out_{i}"] for i in range(len(_OUTS)))
```
